# Optimizing a Trainium2 kernel written in Bass

```python
import numpy as np
import jax, jax.numpy as jnp
from jax import lax

D_MODEL = 1024
BATCH = 1
SEQ = 256
DEPTH = 2

GRID_W = 64
CTX_LEN = 256
N_MIXERS = 2
N_HEADS = 16
HEAD_DIM = D_MODEL // N_HEADS
NA_KH = 8
NA_KW = 16
NA_QCB = NA_KW
NA_KCB = 2 * NA_KW
WA_KV_HEADS = 4
WA_GROUPS = N_HEADS // WA_KV_HEADS
WA_WINDOW = 128
WA_BLOCK = 128
D_FF = 2816
FFN_RES = 0.5
ROPE_BASE = 10000.0
N_MOD = 9
ALPHA = (2 * DEPTH) ** 0.25
BETA = (8 * DEPTH) ** -0.25
LN_EPS = 1e-5
NEG_INF = -1e30
N_NA_LAYERS = (DEPTH + 1) // 2
N_WA_LAYERS = DEPTH // 2


def layer_norm(x, g, b):
    xf = x.astype(jnp.float32)
    mu = jnp.mean(xf, axis=-1, keepdims=True)
    var = jnp.mean(jnp.square(xf - mu), axis=-1, keepdims=True)
    return ((xf - mu) * lax.rsqrt(var + LN_EPS)).astype(x.dtype) * g + b

def modulate(h, shift, scale):
    return h * (1.0 + scale) + shift

def swiglu(u, w_in, w_out):
    a, v = jnp.split(u @ w_in, 2, axis=-1)
    return (jax.nn.silu(a) * v) @ w_out

def ffn_sublayer(h, shift, scale, gate, w_in, w_out, g, b):
    y = swiglu(modulate(h, shift, scale), w_in, w_out)
    return layer_norm(ALPHA * h + FFN_RES * gate * y, g, b)

def axial_rope(x):
    S = x.shape[1]
    t = jnp.arange(S, dtype=jnp.int32)
    rows = (t // GRID_W).astype(jnp.float32)
    cols = (t % GRID_W).astype(jnp.float32)
    n = HEAD_DIM // 4
    inv_freq = ROPE_BASE ** (-jnp.arange(n, dtype=jnp.float32) / n)
    half = HEAD_DIM // 2

    def rot(xa, pos):
        ang = pos[:, None] * inv_freq[None, :]
        cos = jnp.cos(ang)[None, :, None, :].astype(x.dtype)
        sin = jnp.sin(ang)[None, :, None, :].astype(x.dtype)
        x1, x2 = xa[..., :n], xa[..., n:]
        return jnp.concatenate([x1 * cos - x2 * sin, x2 * cos + x1 * sin], axis=-1)

    return jnp.concatenate([rot(x[..., :half], rows), rot(x[..., half:], cols)], axis=-1)

def ctx_attention(qc, kc, vc, sink):
    B, C, H, d = qc.shape
    hk = kc.shape[2]
    g = H // hk
    qg = qc.reshape(B, C, hk, g, d)
    s = jnp.einsum('bqhgd,bkhd->bhgqk', qg, kc).astype(jnp.float32)
    if sink is not None:
        sk = jnp.broadcast_to(sink.astype(jnp.float32).reshape(1, hk, g, 1, 1), s.shape[:-1] + (1,))
        s = jnp.concatenate([s, sk], axis=-1)
    p = jax.nn.softmax(s, axis=-1)[..., :C].astype(vc.dtype)
    o = jnp.einsum('bhgqk,bkhd->bqhgd', p, vc)
    return o.reshape(B, C, H * d)

def neighborhood_attention(u_lat, u_ctx, w_qkv, w_o, rpb, with_ctx_out):
    B, S, _ = u_lat.shape
    C = u_ctx.shape[1]
    rows = S // GRID_W
    kh = min(NA_KH, rows)
    scale = HEAD_DIM ** -0.5
    qkv = (u_lat @ w_qkv).reshape(B, rows, GRID_W, 3, N_HEADS, HEAD_DIM)
    q = qkv[:, :, :, 0] * scale
    k = qkv[:, :, :, 1]
    v = qkv[:, :, :, 2]
    kvc = (u_ctx @ w_qkv[:, D_MODEL:]).reshape(B, C, 2, N_HEADS, HEAD_DIM)
    kc, vc = kvc[:, :, 0], kvc[:, :, 1]

    ncb = GRID_W // NA_QCB
    qcol = np.arange(GRID_W).reshape(ncb, NA_QCB)
    blk_start = np.clip(np.arange(ncb) * NA_QCB - NA_KW // 2, 0, GRID_W - NA_KCB)
    kcol = blk_start[:, None] + np.arange(NA_KCB)[None, :]
    win_start = np.clip(qcol - NA_KW // 2, 0, GRID_W - NA_KW)
    col_valid = (kcol[:, None, :] >= win_start[..., None]) & (kcol[:, None, :] < win_start[..., None] + NA_KW)
    col_off = np.clip(kcol[:, None, :] - qcol[..., None], -(NA_KW - 1), NA_KW - 1) + NA_KW - 1
    bias_cols = jnp.where(col_valid, rpb[:, :, col_off].astype(jnp.float32), NEG_INF)
    n_win = kh * NA_KCB

    def row_block(r):
        rs = jnp.clip(r - kh // 2, 0, rows - kh)
        q_r = lax.dynamic_index_in_dim(q, r, axis=1, keepdims=False).reshape(B, ncb, NA_QCB, N_HEADS, HEAD_DIM)
        k_r = lax.dynamic_slice_in_dim(k, rs, kh, axis=1)[:, :, kcol]
        v_r = lax.dynamic_slice_in_dim(v, rs, kh, axis=1)[:, :, kcol]
        row_idx = rs + jnp.arange(kh) - r + NA_KH - 1
        bias = jnp.take(bias_cols, row_idx, axis=1).transpose(0, 2, 3, 1, 4)[None]
        s_win = jnp.einsum('bcqhd,bicjhd->bhcqij', q_r, k_r).astype(jnp.float32) + bias
        s_win = s_win.reshape(B, N_HEADS, ncb, NA_QCB, n_win)
        s_ctx = jnp.einsum('bcqhd,bkhd->bhcqk', q_r, kc).astype(jnp.float32)
        p = jax.nn.softmax(jnp.concatenate([s_win, s_ctx], axis=-1), axis=-1).astype(v.dtype)
        p_win = p[..., :n_win].reshape(B, N_HEADS, ncb, NA_QCB, kh, NA_KCB)
        p_ctx = p[..., n_win:]
        o = (jnp.einsum('bhcqij,bicjhd->bcqhd', p_win, v_r)
             + jnp.einsum('bhcqk,bkhd->bcqhd', p_ctx, vc))
        return o.reshape(B, GRID_W, D_MODEL)

    out = lax.map(row_block, jnp.arange(rows, dtype=jnp.int32))
    y_lat = out.transpose(1, 0, 2, 3).reshape(B, S, D_MODEL) @ w_o
    y_ctx = None
    if with_ctx_out:
        qc = (u_ctx @ w_qkv[:, :D_MODEL]).reshape(B, C, N_HEADS, HEAD_DIM) * scale
        y_ctx = ctx_attention(qc, kc, vc, None) @ w_o
    return y_lat, y_ctx

def window_gqa(u_lat, u_ctx, w_qkv, w_o, sinks, with_ctx_out):
    B, S, _ = u_lat.shape
    C = u_ctx.shape[1]
    dq = N_HEADS * HEAD_DIM
    dkv = WA_KV_HEADS * HEAD_DIM
    scale = HEAD_DIM ** -0.5
    qkv = u_lat @ w_qkv
    q = axial_rope(qkv[..., :dq].reshape(B, S, N_HEADS, HEAD_DIM)) * scale
    k = axial_rope(qkv[..., dq:dq + dkv].reshape(B, S, WA_KV_HEADS, HEAD_DIM))
    v = qkv[..., dq + dkv:].reshape(B, S, WA_KV_HEADS, HEAD_DIM)
    kvc = u_ctx @ w_qkv[:, dq:]
    kc = kvc[..., :dkv].reshape(B, C, WA_KV_HEADS, HEAD_DIM)
    vc = kvc[..., dkv:].reshape(B, C, WA_KV_HEADS, HEAD_DIM)

    nb = S // WA_BLOCK
    pad = ((0, 0), (WA_BLOCK, WA_BLOCK), (0, 0), (0, 0))
    k_pad = jnp.pad(k, pad)
    v_pad = jnp.pad(v, pad)
    q_blk = q.reshape(B, nb, WA_BLOCK, WA_KV_HEADS, WA_GROUPS, HEAD_DIM)
    sink = sinks.astype(jnp.float32).reshape(1, WA_KV_HEADS, WA_GROUPS, 1, 1)
    qi = jnp.arange(WA_BLOCK, dtype=jnp.int32)
    kj = jnp.arange(3 * WA_BLOCK, dtype=jnp.int32)
    n_win = 3 * WA_BLOCK

    def band_block(b):
        qb = lax.dynamic_index_in_dim(q_blk, b, axis=1, keepdims=False)
        kb = lax.dynamic_slice_in_dim(k_pad, b * WA_BLOCK, n_win, axis=1)
        vb = lax.dynamic_slice_in_dim(v_pad, b * WA_BLOCK, n_win, axis=1)
        pos_q = b * WA_BLOCK + qi
        pos_k = (b - 1) * WA_BLOCK + kj
        valid = ((jnp.abs(pos_q[:, None] - pos_k[None, :]) <= WA_WINDOW)
                 & (pos_k >= 0)[None, :] & (pos_k < S)[None, :])
        s_win = jnp.where(valid, jnp.einsum('bqhgd,bkhd->bhgqk', qb, kb).astype(jnp.float32), NEG_INF)
        s_ctx = jnp.einsum('bqhgd,bkhd->bhgqk', qb, kc).astype(jnp.float32)
        s_sink = jnp.broadcast_to(sink, s_win.shape[:-1] + (1,))
        p = jax.nn.softmax(jnp.concatenate([s_win, s_ctx, s_sink], axis=-1), axis=-1).astype(v.dtype)
        o = (jnp.einsum('bhgqk,bkhd->bqhgd', p[..., :n_win], vb)
             + jnp.einsum('bhgqk,bkhd->bqhgd', p[..., n_win:n_win + C], vc))
        return o.reshape(B, WA_BLOCK, D_MODEL)

    out = lax.map(band_block, jnp.arange(nb, dtype=jnp.int32))
    y_lat = out.transpose(1, 0, 2, 3).reshape(B, S, D_MODEL) @ w_o
    y_ctx = None
    if with_ctx_out:
        qc = (u_ctx @ w_qkv[:, :dq]).reshape(B, C, N_HEADS, HEAD_DIM) * scale
        y_ctx = ctx_attention(qc, kc, vc, sinks) @ w_o
    return y_lat, y_ctx

def first_inputs(seed: int = 0) -> dict:
    key = jax.random.key(seed)
    ks = jax.random.split(key, 16)
    f32 = jnp.float32
    dq = N_HEADS * HEAD_DIM
    dkv = WA_KV_HEADS * HEAD_DIM

    def nrm(k, shape, s):
        return jax.random.normal(k, shape, f32) * s

    return {
        "x": nrm(ks[0], (BATCH, SEQ, D_MODEL), 1.0),
        "c": nrm(ks[1], (BATCH, D_MODEL), 1.0),
        "ctx": nrm(ks[2], (BATCH, CTX_LEN, D_MODEL), 1.0),
        "c_ctx": nrm(ks[3], (D_MODEL,), 1.0),
        "w_mod": nrm(ks[4], (DEPTH, D_MODEL, N_MOD * D_MODEL), 0.5 * D_MODEL ** -0.5),
        "b_mod": nrm(ks[5], (DEPTH, N_MOD * D_MODEL), 0.02),
        "ln_g": 1.0 + nrm(ks[6], (DEPTH, 3, D_MODEL), 0.02),
        "ln_b": nrm(ks[7], (DEPTH, 3, D_MODEL), 0.02),
        "ffn_w_in": nrm(ks[8], (DEPTH, 2, D_MODEL, 2 * D_FF), D_MODEL ** -0.5),
        "ffn_w_out": nrm(ks[9], (DEPTH, 2, D_FF, D_MODEL), BETA * D_FF ** -0.5),
        "na_w_qkv": nrm(ks[10], (N_NA_LAYERS, D_MODEL, 3 * dq), D_MODEL ** -0.5),
        "na_w_o": nrm(ks[11], (N_NA_LAYERS, dq, D_MODEL), BETA * dq ** -0.5),
        "na_rpb": nrm(ks[12], (N_NA_LAYERS, N_HEADS, 2 * NA_KH - 1, 2 * NA_KW - 1), 0.1),
        "wa_w_qkv": nrm(ks[13], (N_WA_LAYERS, D_MODEL, dq + 2 * dkv), D_MODEL ** -0.5),
        "wa_w_o": nrm(ks[14], (N_WA_LAYERS, dq, D_MODEL), BETA * dq ** -0.5),
        "wa_sinks": nrm(ks[15], (N_WA_LAYERS, N_HEADS), 0.5),
    }

def first_block(x, c, ctx, c_ctx, w_mod, b_mod, ln_g, ln_b, ffn_w_in, ffn_w_out,
              na_w_qkv, na_w_o, na_rpb, wa_w_qkv, wa_w_o, wa_sinks):
    h_lat, h_ctx = x, ctx
    silu_c = jax.nn.silu(c)
    silu_cc = jax.nn.silu(c_ctx)
    for i in range(DEPTH):
        ctx_needed = i < DEPTH - 1
        m_lat = jnp.split((silu_c @ w_mod[i] + b_mod[i])[:, None, :], N_MOD, axis=-1)
        m_ctx = jnp.split((silu_cc @ w_mod[i] + b_mod[i])[None, None, :], N_MOD, axis=-1)

        h_lat = ffn_sublayer(h_lat, m_lat[0], m_lat[1], m_lat[2], ffn_w_in[i, 0], ffn_w_out[i, 0], ln_g[i, 0], ln_b[i, 0])
        h_ctx = ffn_sublayer(h_ctx, m_ctx[0], m_ctx[1], m_ctx[2], ffn_w_in[i, 0], ffn_w_out[i, 0], ln_g[i, 0], ln_b[i, 0])

        u_lat = modulate(h_lat, m_lat[3], m_lat[4])
        u_ctx = modulate(h_ctx, m_ctx[3], m_ctx[4])
        j = i // N_MIXERS
        if i % N_MIXERS == 0:
            y_lat, y_ctx = neighborhood_attention(u_lat, u_ctx, na_w_qkv[j], na_w_o[j], na_rpb[j], ctx_needed)
        else:
            y_lat, y_ctx = window_gqa(u_lat, u_ctx, wa_w_qkv[j], wa_w_o[j], wa_sinks[j], ctx_needed)
        h_lat = layer_norm(ALPHA * h_lat + m_lat[5] * y_lat, ln_g[i, 1], ln_b[i, 1])

        h_lat = ffn_sublayer(h_lat, m_lat[6], m_lat[7], m_lat[8], ffn_w_in[i, 1], ffn_w_out[i, 1], ln_g[i, 2], ln_b[i, 2])
        if ctx_needed:
            h_ctx = layer_norm(ALPHA * h_ctx + m_ctx[5] * y_ctx, ln_g[i, 1], ln_b[i, 1])
            h_ctx = ffn_sublayer(h_ctx, m_ctx[6], m_ctx[7], m_ctx[8], ffn_w_in[i, 1], ffn_w_out[i, 1], ln_g[i, 2], ln_b[i, 2])
    return h_lat


EPS = 1e-6
FFN_DIM = 1408
Q_BLOCK = 128

SB_HEADS = 4
SB_HEAD_DIM = 64
SB_WIDTH = SB_HEADS * SB_HEAD_DIM

ML_HEADS = 4
ML_HEAD_DIM = 128
ML_WIDTH = ML_HEADS * ML_HEAD_DIM
ML_CHUNK = 128
ML_CONV = 4
ML_FORGET_BIAS_LO = 3.0
ML_FORGET_BIAS_HI = 6.0

MLA_HEADS = 4
MLA_NOPE = 64
MLA_ROPE = 32
MLA_QK = MLA_NOPE + MLA_ROPE
MLA_V = 64
MLA_WIDTH = MLA_HEADS * MLA_V
MLA_Q_RANK = 256
MLA_KV_RANK = 128
ROPE_THETA = 10000.0

N_BRANCH = 3
SEGMENTS = (
    ('sb_q', SB_WIDTH), ('sb_k', SB_WIDTH), ('sb_v', SB_WIDTH),
    ('ml_q', ML_WIDTH), ('ml_k', ML_WIDTH), ('ml_v', ML_WIDTH), ('ml_o', ML_WIDTH),
    ('ml_i', ML_HEADS), ('ml_f', ML_HEADS),
    ('mla_cq', MLA_Q_RANK), ('mla_ckv', MLA_KV_RANK), ('mla_kr', MLA_ROPE),
    ('gates', N_BRANCH * D_MODEL),
)
N_IN = sum(w for _, w in SEGMENTS)


def _seg_range(name):
    off = 0
    for n, w in SEGMENTS:
        if n == name:
            return off, off + w
        off += w
    raise KeyError(name)

def _split_cols(z):
    out = {}
    off = 0
    for n, w in SEGMENTS:
        out[n] = z[..., off:off + w]
        off += w
    return out

def _rms_norm(x, gain):
    xf = x.astype(jnp.float32)
    y = xf * lax.rsqrt(jnp.mean(xf * xf, axis=-1, keepdims=True) + EPS)
    return (y * gain.astype(jnp.float32)).astype(x.dtype)

def _swiglu(u, wi, wo):
    a, g = jnp.split(u @ wi, 2, axis=-1)
    return (jax.nn.silu(a) * g) @ wo

def _to_heads(z, n_heads):
    b, s, w = z.shape
    return z.reshape(b, s, n_heads, w // n_heads).transpose(0, 2, 1, 3)

def _from_heads(z):
    b, h, s, d = z.shape
    return z.transpose(0, 2, 1, 3).reshape(b, s, h * d)

def _strict_lower(n):
    return jnp.asarray(np.tril(np.ones((n, n), np.float32), -1))

def _causal_mask(i, n, strict):
    qpos = i * Q_BLOCK + np.arange(Q_BLOCK)
    kpos = np.arange(n)
    m = kpos[None, :] < qpos[:, None] if strict else kpos[None, :] <= qpos[:, None]
    return jnp.asarray(m)

def _stick_breaking_attention(q, k, v):
    b, h, s, _ = q.shape
    scale = SB_HEAD_DIM ** -0.5
    tri_in = _strict_lower(Q_BLOCK)
    outs = []
    for i in range(s // Q_BLOCK):
        nk = i + 1
        n = nk * Q_BLOCK
        qb = q[:, :, i * Q_BLOCK:n]
        z = jnp.einsum('bhqd,bhkd->bhqk', qb, k[:, :, :n], preferred_element_type=jnp.float32) * scale
        mask = _causal_mask(i, n, strict=True)
        log_keep = jnp.where(mask, jax.nn.log_sigmoid(-z), 0.0)
        lk = log_keep.reshape(b, h, Q_BLOCK, nk, Q_BLOCK)
        within = jnp.einsum('bhqnj,js->bhqns', lk, tri_in)
        after = jnp.einsum('bhqm,mn->bhqn', jnp.sum(lk, axis=-1), _strict_lower(nk))
        later = (within + after[..., None]).reshape(b, h, Q_BLOCK, n)
        w = jnp.where(mask, jnp.exp(jax.nn.log_sigmoid(z) + later), 0.0)
        outs.append(jnp.einsum('bhqk,bhkd->bhqd', w.astype(v.dtype), v[:, :, :n]))
    return jnp.concatenate(outs, axis=2)

def _causal_softmax_attention(q, k, v, scale):
    s = q.shape[2]
    outs = []
    for i in range(s // Q_BLOCK):
        n = (i + 1) * Q_BLOCK
        qb = q[:, :, i * Q_BLOCK:n]
        z = jnp.einsum('bhqd,bhkd->bhqk', qb, k[:, :, :n], preferred_element_type=jnp.float32) * scale
        z = jnp.where(_causal_mask(i, n, strict=False), z, -jnp.inf)
        p = jnp.exp(z - jnp.max(z, axis=-1, keepdims=True))
        denom = jnp.sum(p, axis=-1, keepdims=True)
        o = jnp.einsum('bhqk,bhkd->bhqd', p.astype(v.dtype), v[:, :, :n], preferred_element_type=jnp.float32)
        outs.append((o / denom).astype(v.dtype))
    return jnp.concatenate(outs, axis=2)

def _rope(x, positions):
    half = MLA_ROPE // 2
    inv_freq = jnp.power(ROPE_THETA, -jnp.arange(half, dtype=jnp.float32) / half)
    ang = positions.astype(jnp.float32)[:, None, :, None] * inv_freq
    cos, sin = jnp.cos(ang), jnp.sin(ang)
    xf = x.astype(jnp.float32)
    x1, x2 = xf[..., :half], xf[..., half:]
    return jnp.concatenate([x1 * cos - x2 * sin, x2 * cos + x1 * sin], axis=-1).astype(x.dtype)

def _mla(c_q, c_kv, k_rope, positions, q_norm, kv_norm, wq_up, wkv_up, q_gain, k_gain):
    b, s, _ = c_q.shape
    q = (_rms_norm(c_q, q_norm) @ wq_up).reshape(b, s, MLA_HEADS, MLA_QK)
    kv = (_rms_norm(c_kv, kv_norm) @ wkv_up).reshape(b, s, MLA_HEADS, MLA_NOPE + MLA_V)
    k_nope, v = kv[..., :MLA_NOPE], kv[..., MLA_NOPE:]
    k_pe = jnp.broadcast_to(k_rope[:, :, None, :], (b, s, MLA_HEADS, MLA_ROPE))
    k = jnp.concatenate([k_nope, k_pe], axis=-1)
    q = _rms_norm(q, q_gain).transpose(0, 2, 1, 3)
    k = _rms_norm(k, k_gain).transpose(0, 2, 1, 3)
    v = v.transpose(0, 2, 1, 3)
    q = jnp.concatenate([q[..., :MLA_NOPE], _rope(q[..., MLA_NOPE:], positions)], axis=-1)
    k = jnp.concatenate([k[..., :MLA_NOPE], _rope(k[..., MLA_NOPE:], positions)], axis=-1)
    return _from_heads(_causal_softmax_attention(q, k, v, MLA_QK ** -0.5))

def _causal_dwconv(x, w, bias):
    y = lax.conv_general_dilated(
        x, w[:, None, :], window_strides=(1,), padding=[(ML_CONV - 1, 0)],
        dimension_numbers=('NWC', 'WIO', 'NWC'), feature_group_count=x.shape[-1])
    return y + bias

def _mlstm_chunkwise(q, k, v, ig, lf):
    b, h, s, dk = q.shape
    dv = v.shape[-1]
    nc = s // ML_CHUNK

    def chunks(z):
        return jnp.moveaxis(z.reshape((b, h, nc, ML_CHUNK) + z.shape[3:]), 2, 0)

    causal = jnp.asarray(np.tril(np.ones((ML_CHUNK, ML_CHUNK), dtype=bool)))
    lower_incl = jnp.asarray(np.tril(np.ones((ML_CHUNK, ML_CHUNK), np.float32)))

    def step(carry, xs):
        c_prev, n_prev, m_prev = carry
        qc, kc, vc, igc, lfc = xs
        cum_f = jnp.einsum('bhs,ts->bht', lfc, lower_incl)
        log_intra = jnp.where(causal, cum_f[..., :, None] - cum_f[..., None, :] + igc[..., None, :], -jnp.inf)
        log_inter = cum_f + m_prev[..., None]
        m = jnp.maximum(log_inter, jnp.max(log_intra, axis=-1))
        w_intra = jnp.exp(log_intra - m[..., None])
        w_inter = jnp.exp(log_inter - m)
        scores = jnp.einsum('bhtd,bhsd->bhts', qc, kc) * w_intra
        num = scores @ vc + w_inter[..., None] * (qc @ c_prev)
        den = jnp.sum(scores, axis=-1) + w_inter * jnp.einsum('bhtd,bhd->bht', qc, n_prev)
        h_out = num / jnp.maximum(jnp.abs(den), jnp.exp(-m))[..., None]
        f_total = cum_f[..., -1]
        log_to_end = f_total[..., None] - cum_f + igc
        m_new = jnp.maximum(f_total + m_prev, jnp.max(log_to_end, axis=-1))
        decay = jnp.exp(f_total + m_prev - m_new)
        w_end = jnp.exp(log_to_end - m_new[..., None])
        c_new = decay[..., None, None] * c_prev + jnp.einsum('bhsd,bhsv->bhdv', kc * w_end[..., None], vc)
        n_new = decay[..., None] * n_prev + jnp.einsum('bhs,bhsd->bhd', w_end, kc)
        return (c_new, n_new, m_new), h_out

    f32 = jnp.float32
    init = (jnp.zeros((b, h, dk, dv), f32), jnp.zeros((b, h, dk), f32), jnp.zeros((b, h), f32))
    _, hs = lax.scan(step, init, (chunks(q), chunks(k), chunks(v), chunks(ig), chunks(lf)))
    return jnp.moveaxis(hs, 0, 2).reshape(b, h, s, dv)

def _mlstm(q, k, v, o_pre, i_pre, f_pre, conv_w, conv_b, out_gain):
    b, s, _ = q.shape
    f32 = jnp.float32
    qk = jax.nn.silu(_causal_dwconv(jnp.concatenate([q, k], axis=-1), conv_w, conv_b))
    q, k = jnp.split(qk, 2, axis=-1)
    qh = _to_heads(q, ML_HEADS).astype(f32)
    kh = _to_heads(k, ML_HEADS).astype(f32) * ML_HEAD_DIM ** -0.5
    vh = _to_heads(v, ML_HEADS).astype(f32)
    ig = i_pre.astype(f32).transpose(0, 2, 1)
    lf = jax.nn.log_sigmoid(f_pre.astype(f32)).transpose(0, 2, 1)
    hh = _mlstm_chunkwise(qh, kh, vh, ig, lf).transpose(0, 2, 1, 3)
    hh = _rms_norm(hh, out_gain.reshape(ML_HEADS, ML_HEAD_DIM)).reshape(b, s, ML_WIDTH)
    return (jax.nn.sigmoid(o_pre.astype(f32)) * hh).astype(v.dtype)

def second_inputs(seed: int = 0) -> dict:
    key = jax.random.key(seed)
    ks = jax.random.split(key, 32)
    f32 = jnp.float32

    def normal(k, shape, fan_in):
        return jax.random.normal(k, shape, f32) * fan_in ** -0.5

    def gain(k, shape):
        return 1.0 + 0.02 * jax.random.normal(k, shape, f32)

    L, D = DEPTH, D_MODEL
    x = jax.random.normal(ks[0], (BATCH, SEQ, D), f32)
    offsets = jax.random.randint(ks[1], (BATCH, 1), 0, 4096, dtype=jnp.int32)
    positions = offsets + jnp.arange(SEQ, dtype=jnp.int32)[None, :]

    b_in = 0.01 * jax.random.normal(ks[2], (L, N_IN), f32)
    f0, f1 = _seg_range('ml_f')
    b_in = b_in.at[:, f0:f1].add(jnp.linspace(ML_FORGET_BIAS_LO, ML_FORGET_BIAS_HI, ML_HEADS, dtype=f32))

    return {
        'x': x,
        'positions': positions,
        'ffn1_norm': gain(ks[3], (L, D)),
        'ffn1_wi': normal(ks[4], (L, D, 2 * FFN_DIM), D),
        'ffn1_wo': normal(ks[5], (L, FFN_DIM, D), FFN_DIM),
        'mix_norm': gain(ks[6], (L, D)),
        'w_in': normal(ks[7], (L, D, N_IN), D),
        'b_in': b_in,
        'ml_conv_w': normal(ks[8], (L, ML_CONV, 2 * ML_WIDTH), ML_CONV),
        'ml_conv_b': 0.01 * jax.random.normal(ks[9], (L, 2 * ML_WIDTH), f32),
        'ml_out_norm': gain(ks[10], (L, ML_WIDTH)),
        'mla_q_norm': gain(ks[11], (L, MLA_Q_RANK)),
        'mla_kv_norm': gain(ks[12], (L, MLA_KV_RANK)),
        'mla_wq_up': normal(ks[13], (L, MLA_Q_RANK, MLA_HEADS * MLA_QK), MLA_Q_RANK),
        'mla_wkv_up': normal(ks[14], (L, MLA_KV_RANK, MLA_HEADS * (MLA_NOPE + MLA_V)), MLA_KV_RANK),
        'mla_q_gain': gain(ks[15], (L, MLA_QK)),
        'mla_k_gain': gain(ks[16], (L, MLA_QK)),
        'w_up_sb': normal(ks[17], (L, SB_WIDTH, D), SB_WIDTH),
        'w_up_ml': normal(ks[18], (L, ML_WIDTH, D), ML_WIDTH),
        'w_up_mla': normal(ks[19], (L, MLA_WIDTH, D), MLA_WIDTH),
        'w_out': normal(ks[20], (L, D, D), D),
        'ffn2_norm': gain(ks[21], (L, D)),
        'ffn2_wi': normal(ks[22], (L, D, 2 * FFN_DIM), D),
        'ffn2_wo': normal(ks[23], (L, FFN_DIM, D), FFN_DIM),
    }

def second_block(x, positions, ffn1_norm, ffn1_wi, ffn1_wo, mix_norm, w_in, b_in, ml_conv_w, ml_conv_b,
              ml_out_norm, mla_q_norm, mla_kv_norm, mla_wq_up, mla_wkv_up, mla_q_gain, mla_k_gain,
              w_up_sb, w_up_ml, w_up_mla, w_out, ffn2_norm, ffn2_wi, ffn2_wo):
    b, s, d = x.shape
    for l in range(DEPTH):
        x = x + 0.5 * _swiglu(_rms_norm(x, ffn1_norm[l]), ffn1_wi[l], ffn1_wo[l])

        u = _rms_norm(x, mix_norm[l])
        c = _split_cols(u @ w_in[l] + b_in[l])

        y_sb = _from_heads(_stick_breaking_attention(
            _to_heads(c['sb_q'], SB_HEADS), _to_heads(c['sb_k'], SB_HEADS), _to_heads(c['sb_v'], SB_HEADS)))
        y_ml = _mlstm(c['ml_q'], c['ml_k'], c['ml_v'], c['ml_o'], c['ml_i'], c['ml_f'],
                      ml_conv_w[l], ml_conv_b[l], ml_out_norm[l])
        y_mla = _mla(c['mla_cq'], c['mla_ckv'], c['mla_kr'], positions, mla_q_norm[l], mla_kv_norm[l],
                     mla_wq_up[l], mla_wkv_up[l], mla_q_gain[l], mla_k_gain[l])

        g = jax.nn.sigmoid(c['gates'].astype(jnp.float32)).astype(x.dtype).reshape(b, s, N_BRANCH, d)
        merged = (g[:, :, 0] * (y_sb @ w_up_sb[l])
                  + g[:, :, 1] * (y_ml @ w_up_ml[l])
                  + g[:, :, 2] * (y_mla @ w_up_mla[l]))
        x = x + merged @ w_out[l]

        x = x + 0.5 * _swiglu(_rms_norm(x, ffn2_norm[l]), ffn2_wi[l], ffn2_wo[l])
    return x


def setup_inputs(seed=0):
    out = dict(first_inputs(seed))
    for name, value in second_inputs(seed + 1).items():
        if name != "x":
            out[name + "_2"] = value
    return out


def reference(
    x, c, ctx, c_ctx, w_mod, b_mod, ln_g, ln_b, ffn_w_in, ffn_w_out, na_w_qkv, na_w_o, na_rpb,
    wa_w_qkv, wa_w_o, wa_sinks, positions_2, ffn1_norm_2, ffn1_wi_2, ffn1_wo_2, mix_norm_2,
    w_in_2, b_in_2, ml_conv_w_2, ml_conv_b_2, ml_out_norm_2, mla_q_norm_2, mla_kv_norm_2,
    mla_wq_up_2, mla_wkv_up_2, mla_q_gain_2, mla_k_gain_2, w_up_sb_2, w_up_ml_2, w_up_mla_2,
    w_out_2, ffn2_norm_2, ffn2_wi_2, ffn2_wo_2,
):
    x = first_block(
        x, c, ctx, c_ctx, w_mod, b_mod, ln_g, ln_b, ffn_w_in, ffn_w_out, na_w_qkv, na_w_o,
        na_rpb, wa_w_qkv, wa_w_o, wa_sinks,
    )
    return second_block(
        x, positions_2, ffn1_norm_2, ffn1_wi_2, ffn1_wo_2, mix_norm_2, w_in_2, b_in_2,
        ml_conv_w_2, ml_conv_b_2, ml_out_norm_2, mla_q_norm_2, mla_kv_norm_2, mla_wq_up_2,
        mla_wkv_up_2, mla_q_gain_2, mla_k_gain_2, w_up_sb_2, w_up_ml_2, w_up_mla_2, w_out_2,
        ffn2_norm_2, ffn2_wi_2, ffn2_wo_2,
    )


_drawn_inputs = setup_inputs


def setup_inputs(seed=0):
    import zlib

    import numpy as np

    out = dict(_drawn_inputs(seed))
    spreads = {}
    factors = {'b_mod': 4.81,
     'na_rpb': 8.0,
     'wa_sinks': 8.0,
     'ffn1_norm_2': 4.368,
     'mix_norm_2': 3.165,
     'ml_conv_b_2': 50.69,
     'ml_out_norm_2': 7.252,
     'mla_q_norm_2': 8.0,
     'mla_kv_norm_2': 8.0,
     'mla_q_gain_2': 8.0,
     'mla_k_gain_2': 8.0,
     'ffn2_norm_2': 5.486}
    for name, (base, spread) in spreads.items():
        noise = np.random.default_rng([zlib.crc32(name.encode()), seed]).standard_normal(out[name].shape)
        drawn = base * np.exp(spread * noise) if base else spread * noise
        out[name] = __import__('jax').numpy.asarray(drawn.astype(out[name].dtype))
    for name, factor in factors.items():
        out[name] = (out[name] * factor).astype(out[name].dtype)
    return out
```

```python
from contextlib import ExitStack

import numpy as np
import concourse.bass as bass
from concourse import mybir

P = 128
D = 1024
KC = D // P
S = 256
T2 = 2 * S
FF = 2816
HALF = FF // 2
FC = HALF // P
FF2 = 1408
NH = 16
HD = 64
GRID_W = 64
ROWS = S // GRID_W
NA_KH, NA_KW = 8, 16
WA_KV = 4
WINDOW = 128
N_MOD = 9
MOD_UNITS = N_MOD * D // 256
ALPHA = 4 ** 0.25
ML_H, SB_H, MLA_H = 4, 4, 4
QK = 96
NEG = -1e30
LN_EPS, RMS_EPS = 1e-5, 1e-6

F32 = mybir.dt.float32
F32R = mybir.dt.float32r
I32 = mybir.dt.int32
ALU = mybir.AluOpType
ACT = mybir.ActivationFunctionType
AX = mybir.AxisListType


class Tally:

    def __init__(self, sem, name, book):
        self.sem, self.name, self.book, self.n = sem, name, book, 0

    def up(self, label=None):
        self.n += 1
        if label is not None:
            self.book[(self.name, label)] = self.n
        return self.sem, 1

    def here(self):
        return self.sem, self.n

    def at(self, *label):
        label = label[0] if len(label) == 1 else label
        if (self.name, label) not in self.book:
            self.book.setdefault("missing", set()).add((self.name, label))
        return self.sem, self.book.get((self.name, label), 1)


def columns(*widths):
    at, out = 0, {}
    for name, n in widths:
        out[name] = (at, n)
        at += n
    return out, at


CONST1, N_CONST1 = columns(("ident", P), ("mean1024", P), ("na_mask", 2 * S), ("wa_mask", 2 * S),
                           ("rope_perm", P), ("rope_cos", S), ("rope_sin", S), ("one", 1),
                           ("ln_eps", 1), ("rms_eps", 1))
CONST2, N_CONST2 = columns(("ones", P), ("mean256", P), ("mean128", P), ("mean96", P), ("tri_strict", P),
                           ("tri_incl", P), ("causal", 2 * S), ("causal_t", P), ("sb_mask", 384),
                           ("mla_perm", P), ("inv_freq", 1), ("half_pi", 1))
VEC1, N_VEC1 = columns(("b_mod", 2 * N_MOD * KC), ("ln_g", 6 * KC), ("ln_b", 6 * KC))
VEC2, N_VEC2 = columns(("ffn1_norm", KC), ("mix_norm", KC), ("ffn2_norm", KC), ("b_sbq", 2), ("b_sbk", 2),
                       ("b_mlqk", 8), ("b_mlo", 4), ("b_cq", 2), ("b_ckv", 1), ("b_kr", 1), ("b_gates", 24),
                       ("conv_w", 32), ("conv_b", 8), ("ml_gain", 4), ("q_norm", 2), ("kv_norm", 1),
                       ("q_gain", 1), ("k_gain", 1))
ROW2, N_ROW2 = columns(("b_sbv", 256), ("b_mlv", 512), ("b_if", 8))


def const_arrays():
    c1 = np.zeros((P, N_CONST1), np.float32)
    c2 = np.zeros((P, N_CONST2), np.float32)

    def put(c, cols, name, value):
        at, n = cols[name]
        value = np.asarray(value, np.float32)
        c[:value.shape[0], at:at + value.shape[1]] = value

    i = np.arange(P)
    put(c1, CONST1, "ident", np.eye(P))
    put(c1, CONST1, "mean1024", np.full((P, P), 1 / 1024))
    qc, kc = np.arange(P) % GRID_W, np.arange(2 * S) % GRID_W
    start = np.clip(qc - NA_KW // 2, 0, GRID_W - NA_KW)[:, None]
    put(c1, CONST1, "na_mask", np.where((kc >= start) & (kc < start + NA_KW), 0, NEG))
    q, k = np.arange(S).reshape(2, P), np.arange(S)
    near = np.abs(q[:, :, None] - k) <= WINDOW
    put(c1, CONST1, "wa_mask", np.where(near, 0, NEG).transpose(1, 0, 2).reshape(P, 2 * S))
    perm = np.zeros((P, P))
    for f in range(P):
        j = f % 32
        perm[f + 16 if j < 16 else f - 16, f] = -1 if j < 16 else 1
    put(c1, CONST1, "rope_perm", perm)
    inv = (np.float32(10000.0) ** (-np.arange(16, dtype=np.float32) / np.float32(16))).astype(np.float32)
    t = np.arange(S)
    pos = np.where((i % HD < 32)[:, None], t // GRID_W, t % GRID_W).astype(np.float32)
    ang = pos * inv[i % 16][:, None]
    put(c1, CONST1, "rope_cos", np.cos(ang))
    put(c1, CONST1, "rope_sin", np.sin(ang))
    put(c1, CONST1, "one", np.ones((P, 1)))
    put(c1, CONST1, "ln_eps", np.full((P, 1), LN_EPS))
    put(c1, CONST1, "rms_eps", np.full((P, 1), RMS_EPS))
    put(c2, CONST2, "ones", np.ones((P, P)))
    put(c2, CONST2, "mean256", np.full((P, P), 1 / 256))
    put(c2, CONST2, "mean128", np.full((P, P), 1 / 128))
    put(c2, CONST2, "mean96", np.full((QK, QK), 1 / QK))
    put(c2, CONST2, "tri_strict", i[:, None] > i[None])
    put(c2, CONST2, "tri_incl", i[:, None] <= i[None])
    put(c2, CONST2, "causal", np.where(k <= q[:, :, None], 0, NEG).transpose(1, 0, 2).reshape(P, 2 * S))
    put(c2, CONST2, "causal_t", np.where(i[:, None] <= i[None], 0, NEG))
    strict = i[:, None] < i[None]
    put(c2, CONST2, "sb_mask", np.concatenate([strict, np.ones((P, P)), strict], 1))
    perm = np.zeros((QK, QK))
    for f in range(HD, QK):
        j = f - HD
        perm[f + 16 if j < 16 else f - 16, f] = -1 if j < 16 else 1
    put(c2, CONST2, "mla_perm", perm)
    freq = np.zeros((QK, 1), np.float32)
    freq[HD:, 0] = inv[np.arange(32) % 16]
    put(c2, CONST2, "inv_freq", freq)
    put(c2, CONST2, "half_pi", np.full((P, 1), np.pi / 2))
    return c1, c2


class Phase:

    def __init__(self, array, index, n, kc):
        self.array, self.index, self.n, self.kc = array, index, n, kc
        self.size = kc * 256


def plan():
    phases = {"mod": Phase("w_mod", 0, 2 * MOD_UNITS, KC)}

    def ffn(name, arrays, at, halves):
        for half in range(halves):
            n = at * halves + half
            phases[f"{name}.in{half}"] = Phase(arrays[0], n * FC, FC, KC)
            phases[f"{name}.out{half}"] = Phase(arrays[1], n * 4, 4, FC)

    ffn("L0.ffn0", ("ffn_in", "ffn_out"), 0, 2)
    for j, what in enumerate("qkv"):
        phases[f"L0.{what}"] = Phase("na_qkv", 4 * j, 4, KC)
    phases["L0.wo"] = Phase("na_o", 0, 4, KC)
    ffn("L0.ffn1", ("ffn_in", "ffn_out"), 1, 2)
    ffn("L1.ffn0", ("ffn_in", "ffn_out"), 2, 2)
    phases["L1.q"] = Phase("wa_qkv", 0, 4, KC)
    phases["L1.k"] = Phase("wa_qkv", 4, 1, KC)
    phases["L1.v"] = Phase("wa_qkv", 5, 1, KC)
    phases["L1.wo"] = Phase("wa_o", 0, 4, KC)
    ffn("L1.ffn1", ("ffn_in", "ffn_out"), 3, 2)
    for l in range(2):
        ffn(f"M{l}.ffn0", ("ffn1_in", "ffn1_out"), l, 1)
        phases[f"M{l}.z"] = Phase("w_in", 13 * l, 13, KC)
        phases[f"M{l}.merge"] = Phase("w_merge", 16 * l, 16, KC)
        phases[f"M{l}.wo"] = Phase("w_out", 4 * l, 4, KC)
        ffn(f"M{l}.ffn1", ("ffn2_in", "ffn2_out"), l, 1)
    u = 0
    for ph in phases.values():
        ph.u0 = u
        u += ph.n
    return phases


def build(nc, A, book):
    phases = plan()
    unit_size = [ph.size for ph in phases.values() for _ in range(ph.n)]
    n_units = len(unit_size)
    ctx, block1, ffn1_mem, att_mem, block2, ffn2_mem, mix_mem, merge_mem = (ExitStack() for _ in range(8))

    def sb(name, shape, dt=F32, scope=ctx):
        return scope.enter_context(nc.sbuf_tensor(name, shape, dt))

    def sem(name):
        return ctx.enter_context(nc.semaphore(name))

    def tally(name):
        return Tally(sem(name), name, book)

    banks = ctx.enter_context(nc.psum_tensor("banks", [P, 8, 512], F32))
    raw = [sb(f"raw{i}", [P, FC * 256]) for i in range(2)]
    whi = [sb(f"whi{i}", [P, FC * 256], F32R) for i in range(2)]
    wlo = [sb(f"wlo{i}", [P, FC * 256], F32R) for i in range(2)]
    h = sb("h", [P, KC, T2])
    squares = sb("squares", [P, 2, T2])
    sums = sb("sums", [P, 2, T2])
    scaled = sb("scaled", [P, 2, T2])
    full_u = sb("full_u", [P, 2, T2])
    rstd = sb("rstd", [P, T2])
    var = sb("var", [P, T2])
    k1 = sb("k1", [P, N_CONST1])
    small = sb("small", [P, 160])
    v1 = sb("v1", [P, N_VEC1], scope=block1)
    mod_raw = sb("mod_raw", [P, 2 * MOD_UNITS, 8], scope=block1)
    mods = sb("mods", [P, 2, N_MOD * KC, 2], scope=block1)
    cvec = sb("cvec", [P, KC, 2], scope=block1)
    csilu = sb("csilu", [P, KC, 2], scope=block1)
    c4 = sb("c4", [P, KC, 4], F32R, scope=block1)
    sinks = sb("sinks", [P, NH], scope=block1)
    vS1 = sb("vS1", [P, 7, KC, 2], scope=block1)
    vS0 = sb("vS0", [P, 7, KC, 2], scope=block1)
    vG = sb("vG", [P, 6, KC, 2], scope=block1)
    gA = sb("gA", [P, 6, KC], scope=block1)
    bA = sb("bA", [P, 6, KC], scope=block1)
    uhi = sb("uhi", [P, KC, T2], F32R, scope=block1)
    ulo = sb("ulo", [P, KC, T2], F32R, scope=block1)
    fhi = sb("fhi", [P, FC, T2], F32R, scope=ffn1_mem)
    flo = sb("flo", [P, FC, T2], F32R, scope=ffn1_mem)
    silu_a = sb("silu_a", [P, 2, T2], scope=ffn1_mem)
    hidden = sb("hidden", [P, 2, T2], scope=ffn1_mem)
    ffn1_mem.close()
    qT = sb("qT", [P, KC, T2], scope=att_mem)
    kT = sb("kT", [P, KC, T2], scope=att_mem)
    vv = sb("vv", [P, 4, D], scope=att_mem)
    na_bias = sb("na_bias", [P, 2, T2], scope=att_mem)
    att_mem.close()
    block1.close()
    u2hi = sb("u2hi", [P, KC, S], F32R, scope=block2)
    u2lo = sb("u2lo", [P, KC, S], F32R, scope=block2)
    yhi = sb("yhi", [P, KC, S], F32R, scope=block2)
    ylo = sb("ylo", [P, KC, S], F32R, scope=block2)
    k2 = sb("k2", [P, N_CONST2], scope=block2)
    v2 = sb("v2", [P, 2, N_VEC2], scope=block2)
    rows2 = sb("rows2", [P, 2, N_ROW2], scope=block2)
    positions = sb("positions", [QK, S], I32, scope=block2)
    rope_c = sb("rope_c", [QK, S], scope=block2)
    rope_s = sb("rope_s", [QK, S], scope=block2)
    f2hi = sb("f2hi", [P, FC, S], F32R, scope=ffn2_mem)
    f2lo = sb("f2lo", [P, FC, S], F32R, scope=ffn2_mem)
    silu_a2 = sb("silu_a2", [P, 2, S], scope=ffn2_mem)
    hidden2 = sb("hidden2", [P, 2, S], scope=ffn2_mem)
    ffn2_mem.close()
    w_q = sb("w_q", [P, 2, 384], scope=mix_mem)
    w_kv = sb("w_kv", [P, 512], scope=mix_mem)
    sbq = sb("sbq", [P, 2, S], scope=mix_mem)
    sbk = sb("sbk", [P, 2, S], scope=mix_mem)
    sbv = sb("sbv", [P, 2, 256], scope=mix_mem)
    conv_in = sb("conv_in", [P, KC, S + 3], scope=mix_mem)
    mlv = sb("mlv", [P, 2, 512], scope=mix_mem)
    osig = sb("osig", [P, 4, S], scope=mix_mem)
    cq = sb("cq", [P, 3, S], scope=mix_mem)
    kr = sb("kr", [P, S], scope=mix_mem)
    iff = sb("iff", [P, 2, 8], scope=mix_mem)
    qk = sb("qk", [P, 8, S], scope=mix_mem)
    mla_v = sb("mla_v", [P, 2, 256], scope=mix_mem)
    mix_mem.close()
    gate = sb("gate", [P, 6, S], scope=merge_mem)
    gated = sb("gated", [P, 2, 3, S], scope=merge_mem)
    mhi = sb("mhi", [P, KC, S], F32R, scope=merge_mem)
    mlo = sb("mlo", [P, KC, S], F32R, scope=merge_mem)
    merge_mem.close()
    block2.close()
    mlqk = h[:, :, S:T2]
    probs, probs_t = scaled, full_u

    def c(name):
        table, cols = (k1, CONST1) if name in CONST1 else (k2, CONST2)
        at, n = cols[name]
        return table[:, at:at + n]

    def vec2(l, name, k=0, n=1):
        at = VEC2[name][0] + k
        return v2[:, l, at:at + n]

    ident = c("ident")

    landed = [sem("weights_landed_0"), sem("weights_landed_1")]
    hi_done = sem("weights_hi_done")
    lo_done = sem("weights_lo_done")
    product = sem("product_done")
    evicted = sem("product_evicted")
    inputs_loaded = sem("inputs_loaded")
    block2_loaded = sem("block2_inputs_loaded")
    mla_loaded = sem("mla_weights_loaded")
    bias_loaded = [sem("na_bias_loaded_0"), sem("na_bias_loaded_1")]
    stored = sem("output_stored")
    f_silu, f_hi, f_split = sem("ffn_silu_done"), sem("ffn_hidden_hi_done"), sem("ffn_hidden_split_done")
    PE_, ACT_, DVE_, POOL_ = tally("pe_step"), tally("act_step"), tally("dve_step"), tally("pool_step")
    N_INPUTS, N_BLOCK2 = 5, 4

    def plus(x, k, it):
        return x if it is None else x + k * it

    def load(sp, ph, i, u, it):
        if u >= 2:
            sp.wait_ge(lo_done, plus(u - 1, 2, it))
        sp.dma_start(raw[u % 2][:, 0:ph.size], A[ph.array][ph.index + i]).then_inc(landed[u % 2], 16)

    def sweep_loads(sp, ph):
        sweep(sp, ph, lambda u, i, it: load(sp, ph, i, u, it))

    def split_hi(act, u, it=None):
        if u >= n_units:
            return
        act.wait_ge(landed[u % 2], plus(16 * (u // 2 + 1), 16, it))
        if u >= 2:
            act.wait_ge(product, plus(2 * (u - 1), 4, it))
        act.copy(whi[u % 2][:, 0:unit_size[u]], raw[u % 2][:, 0:unit_size[u]]).then_inc(hi_done, 1)

    def split_lo(dve, u, it=None):
        if u >= n_units:
            return
        n = unit_size[u]
        dve.wait_ge(hi_done, plus(u + 1, 2, it))
        dve.tensor_tensor(wlo[u % 2][:, 0:n], raw[u % 2][:, 0:n], whi[u % 2][:, 0:n].bitcast(F32),
                          ALU.subtract).then_inc(lo_done, 1)

    def sweep(e, ph, one):
        first = 1 if ph.u0 else 2
        for i in range(first):
            one(ph.u0 + i, i, None)
        pairs = (ph.n - first - 1) // 2 if ph.n >= 8 else 0
        if pairs:
            with e.Fori(0, pairs) as it:
                for j in range(2):
                    one(ph.u0 + first + j, 2 * it + (first + j), it)
        for i in range(first + 2 * pairs, ph.n):
            one(ph.u0 + i, i, None)

    def start_unit(pe, u, it=None, per=2):
        pe.wait_ge(lo_done, plus(u + 1, per, it))
        if u >= 2:
            pe.wait_ge(evicted, plus(u - 1, per, it))

    def bank(u, half):
        return 2 * (u % 2) + half

    def cols(t, u, k, a, b):
        return t[u % 2][:, k * 256 + a:k * 256 + b]

    def feature_major(pe, u, half, chunks, x_hi, x_lo, T, out=None, arrived=None):
        out = banks[:, bank(u, half), 0:T] if out is None else out
        for n, k in enumerate(chunks):
            if arrived is not None:
                pe.wait_ge(*arrived(k))
            w_hi, w_lo = cols(whi, u, k, half * P, half * P + P), cols(wlo, u, k, half * P, half * P + P)
            pe.matmul(out, w_hi, x_hi[:, k, 0:T], start=(n == 0), stop=False)
            pe.matmul(out, w_hi, x_lo[:, k, 0:T], start=False, stop=False)
            mm = pe.matmul(out, w_lo, x_hi[:, k, 0:T], start=False, stop=(n == len(chunks) - 1))
        return mm

    def token_major(pe, u, out, tile, a, b, x_hi, x_lo):
        ts = slice(tile * P, tile * P + P)
        for k in range(KC):
            pe.matmul(out, x_hi[:, k, ts], cols(whi, u, k, a, b), start=(k == 0), stop=False)
            pe.matmul(out, x_hi[:, k, ts], cols(wlo, u, k, a, b), start=False, stop=False)
            mm = pe.matmul(out, x_lo[:, k, ts], cols(whi, u, k, a, b), start=False, stop=(k == KC - 1))
        return mm

    def mod_pe(pe):
        pe.wait_ge(*DVE_.at("c split"))

        def one(u, i, it):
            start_unit(pe, u, it)
            for half in range(2):
                out = banks[:, bank(u, 0), 4 * half:4 * half + 4]
                for k in range(KC):
                    pe.matmul(out, cols(whi, u, k, half * P, half * P + P), c4[:, k, :],
                              start=(k == 0), stop=False)
                    mm = pe.matmul(out, cols(wlo, u, k, half * P, half * P + P), c4[:, k, :],
                                   start=False, stop=(k == KC - 1))
                mm.then_inc(product, 1)
        sweep(pe, phases["mod"], one)

    def mod_act(act):
        act.wait_ge(inputs_loaded, 16 * N_INPUTS)
        act.activation(csilu[:], cvec[:], ACT.Silu).then_inc(*ACT_.up("c silu"))
        split_hi(act, 0)
        sweep(act, phases["mod"], lambda u, i, it: split_hi(act, u + 1, it))

    def mod_dve(dve):
        dve.wait_ge(*ACT_.at("c silu"))
        dve.tensor_copy(c4[:, :, 0:2], csilu[:]).then_inc(*DVE_.up())
        dve.wait_ge(*DVE_.here())
        dve.tensor_tensor(c4[:, :, 2:4], csilu[:], c4[:, :, 0:2].bitcast(F32), ALU.subtract)\
            .then_inc(*DVE_.up("c split"))
        split_lo(dve, 0)

        def one(u, i, it):
            split_lo(dve, u + 1, it)
            dve.wait_ge(product, plus(2 * (u + 1), 4, it))
            dve.tensor_copy(mod_raw[:, i, :], banks[:, bank(u, 0), 0:8]).then_inc(evicted, 1)
        sweep(dve, phases["mod"], one)
        dve.wait_ge(evicted, 2 * MOD_UNITS)
        dve.wait_ge(inputs_loaded, 16 * N_INPUTS)
        parts = mod_raw[:].rearrange("p u (g c v) -> p (u g) c v", g=2, c=2)
        mv = mods[:].rearrange("p l m v -> p (l m) v")
        at, n = VEC1["b_mod"]
        bias = v1[:, at:at + n].rearrange("p (m o) -> p m o", o=1)
        dve.tensor_tensor(mv, parts[:, :, 0, :], parts[:, :, 1, :], ALU.add).then_inc(*DVE_.up())
        dve.wait_ge(*DVE_.here())
        for v in range(2):
            dve.tensor_tensor(mv[:, :, v:v + 1], mv[:, :, v:v + 1], bias, ALU.add).then_inc(*DVE_.up())
        dve.wait_ge(*DVE_.here())
        ag, ab = VEC1["ln_g"][0], VEC1["ln_b"][0]
        for s in range(7):
            l, j = s // 3, s % 3
            for v in range(2):
                g = v1[:, ag + KC * (s - 1):ag + KC * s]
                b = v1[:, ab + KC * (s - 1):ab + KC * s]
                s1, s0 = vS1[:, s, :, v], vS0[:, s, :, v]
                if s == 6:
                    dve.tensor_copy(s1, g).then_inc(*DVE_.up())
                    dve.tensor_copy(s0, b).then_inc(*DVE_.up())
                    continue
                shift, scale, gated_by = (mods[:, l, (3 * j + m) * KC:(3 * j + m + 1) * KC, v] for m in range(3))
                dve.tensor_scalar(s1, scale, 1.0, None, ALU.add).then_inc(*DVE_.up())
                dve.wait_ge(*DVE_.here())
                if s == 0:
                    dve.tensor_copy(s0, shift).then_inc(*DVE_.up())
                else:
                    dve.tensor_tensor(s0, b, s1, ALU.mult).then_inc(*DVE_.up())
                    dve.wait_ge(*DVE_.here())
                    dve.tensor_tensor(s0, s0, shift, ALU.add).then_inc(*DVE_.up())
                    dve.tensor_tensor(s1, s1, g, ALU.mult).then_inc(*DVE_.up())
                dve.tensor_scalar(vG[:, s, :, v], gated_by, 1.0 if j == 1 else 0.5, None, ALU.mult)\
                    .then_inc(*DVE_.up())
        dve.tensor_scalar(gA[:].rearrange("p s k -> p (s k)"), v1[:, ag:ag + 6 * KC], ALPHA, None, ALU.mult)\
            .then_inc(*DVE_.up())
        dve.tensor_scalar(bA[:].rearrange("p s k -> p (s k)"), v1[:, ab:ab + 6 * KC], ALPHA, None, ALU.mult)\
            .then_inc(*DVE_.up("vectors"))

    def kinds(T):
        return ((0, 0, S), (1, S, T2)) if T == T2 else ((0, 0, S),)

    def squares_act(act, s, T, source, ccs):
        for cc in ccs:
            act.wait_ge(*source(cc))
            if cc >= 2:
                act.wait_ge(*POOL_.at("sq sum", s, cc - 2))
            act.activation(squares[:, cc % 2, 0:T], h[:, cc, 0:T], ACT.Square).then_inc(*ACT_.up(("sq", s, cc)))

    def sums_pool(pool, s, T, source, mean):
        for cc in range(KC):
            if mean:
                pool.wait_ge(*source(cc))
                if cc == 0:
                    pool.tensor_copy(sums[:, 0, 0:T], h[:, 0, 0:T]).then_inc(*POOL_.up(("sum", s, cc)))
                else:
                    pool.wait_ge(*POOL_.at("sum", s, cc - 1))
                    pool.tensor_tensor(sums[:, 0, 0:T], sums[:, 0, 0:T], h[:, cc, 0:T], ALU.add)\
                        .then_inc(*POOL_.up(("sum", s, cc)))
            pool.wait_ge(*ACT_.at("sq", s, cc))
            if cc == 0:
                pool.tensor_copy(sums[:, 1, 0:T], squares[:, 0, 0:T]).then_inc(*POOL_.up(("sq sum", s, cc)))
            else:
                pool.wait_ge(*POOL_.at("sq sum", s, cc - 1))
                pool.tensor_tensor(sums[:, 1, 0:T], sums[:, 1, 0:T], squares[:, cc % 2, 0:T], ALU.add)\
                    .then_inc(*POOL_.up(("sq sum", s, cc)))

    def means_pe(pe, s, T, mean):
        pe.wait_ge(*POOL_.at("sq sum", s, KC - 1))
        if mean:
            pe.matmul(banks[:, 4, 0:T], c("mean1024"), sums[:, 0, 0:T], start=True, stop=True)
        pe.matmul(banks[:, 5, 0:T], c("mean1024"), sums[:, 1, 0:T], start=True, stop=True)\
            .then_inc(*PE_.up(("means", s)))

    def rstd_act(act, s, T, mean):
        act.wait_ge(*PE_.at("means", s))
        if mean:
            act.activation(var[:, 0:T], banks[:, 4, 0:T], ACT.Square).then_inc(*ACT_.up(("mean2", s)))
            act.wait_ge(*DVE_.at("var", s))
            act.activation(var[:, 0:T], var[:, 0:T], ACT.Ln, bias=c("ln_eps")).then_inc(*ACT_.up())
        else:
            act.activation(var[:, 0:T], banks[:, 5, 0:T], ACT.Ln, bias=c("rms_eps")).then_inc(*ACT_.up())
        act.wait_ge(*ACT_.here())
        act.activation(rstd[:, 0:T], var[:, 0:T], ACT.Exp, scale=-0.5).then_inc(*ACT_.up(("rstd", s)))

    def centre_dve(dve, s, T):
        dve.wait_ge(*ACT_.at("mean2", s))
        dve.tensor_tensor(var[:, 0:T], banks[:, 5, 0:T], var[:, 0:T], ALU.subtract).then_inc(*DVE_.up())
        dve.wait_ge(*DVE_.here())
        dve.tensor_scalar(var[:, 0:T], var[:, 0:T], 0.0, None, ALU.max).then_inc(*DVE_.up(("var", s)))
        for cc in range(KC):
            dve.tensor_tensor(h[:, cc, 0:T], h[:, cc, 0:T], banks[:, 4, 0:T], ALU.subtract)\
                .then_inc(*DVE_.up(("centred", s, cc)))

    def layer_input_act(act, s, T, ready, scale, shift, x_hi, src=None):
        for cc in range(KC):
            if ready is not None:
                act.wait_ge(*ready(cc))
            if cc >= 2:
                act.wait_ge(*DVE_.at("u", s, cc - 2))
            x = h[:, cc] if src is None else src[:, cc % 2]
            for kind, a, b in kinds(T):
                args = dict(scale=scale(cc, kind)) | ({} if shift is None else dict(bias=shift(cc, kind)))
                act.activation(full_u[:, cc % 2, a:b], x[:, a:b], ACT.Identity, **args).then_inc(*ACT_.up())
                act.activation(x_hi[:, cc, a:b], x[:, a:b], ACT.Identity, **args)\
                    .then_inc(*ACT_.up(("u hi", s, cc)))

    def low_dve(dve, s, T, cc, x_hi, x_lo):
        dve.wait_ge(*ACT_.at("u hi", s, cc))
        dve.tensor_tensor(x_lo[:, cc, 0:T], full_u[:, cc % 2, 0:T], x_hi[:, cc, 0:T].bitcast(F32),
                          ALU.subtract).then_inc(*DVE_.up(("u", s, cc)))

    def residual_pool(pool, s, T):
        for cc in range(KC):
            pool.wait_ge(*ACT_.at("u hi", s, cc))
            if s == 0:
                pool.tensor_scalar(h[:, cc, 0:T], h[:, cc, 0:T], ALPHA, None, ALU.mult)\
                    .then_inc(*POOL_.up(("h", s, cc)))
            else:
                pool.tensor_scalar(h[:, cc, 0:T], h[:, cc, 0:T], gA[:, s - 1, cc:cc + 1],
                                   bA[:, s - 1, cc:cc + 1], ALU.mult, ALU.add).then_inc(*POOL_.up(("h", s, cc)))

    def last_evicted(ph):
        return lambda cc: (evicted, ph.u0 + cc // 2 + 1)

    def scale1(s):
        return lambda cc, kind: vS1[:, s, cc, kind:kind + 1]

    def shift1(s):
        return lambda cc, kind: vS0[:, s, cc, kind:kind + 1]

    def norm1_dve(dve, s, T):
        centre_dve(dve, s, T)
        dve.wait_ge(*ACT_.at("rstd", s))
        for cc in range(KC + 1):
            if cc < KC:
                dve.wait_ge(*DVE_.at("centred", s, cc))
                dve.tensor_tensor(h[:, cc, 0:T], h[:, cc, 0:T], rstd[:, 0:T], ALU.mult)\
                    .then_inc(*DVE_.up(("n", s, cc)))
            if cc and s < 6:
                low_dve(dve, s, T, cc - 1, uhi, ulo)

    def norm1_act(act, s, T):
        rstd_act(act, s, T, True)
        if s < 6:
            layer_input_act(act, s, T, lambda cc: DVE_.at("n", s, cc), scale1(s), shift1(s), uhi)
            return
        for cc in range(KC):
            act.wait_ge(*DVE_.at("n", s, cc))
            act.activation(h[:, cc, 0:T], h[:, cc, 0:T], ACT.Identity, scale=vS1[:, s, cc, 0:1],
                           bias=vS0[:, s, cc, 0:1]).then_inc(*ACT_.up(("h", s, cc)))

    def norm2_dve(dve, s, x_hi, x_lo):
        dve.wait_ge(*ACT_.at("rstd", s))
        for cc in range(KC + 1):
            if cc < KC:
                if cc >= 2:
                    dve.wait_ge(*ACT_.at("u hi", s, cc - 2))
                dve.tensor_tensor(scaled[:, cc % 2, 0:S], h[:, cc, 0:S], rstd[:, 0:S], ALU.mult)\
                    .then_inc(*DVE_.up(("n", s, cc)))
            if cc:
                low_dve(dve, s, S, cc - 1, x_hi, x_lo)

    def norm2_act(act, s, l, name, x_hi):
        rstd_act(act, s, S, False)
        layer_input_act(act, s, S, lambda cc: DVE_.at("n", s, cc), lambda cc, kind: vec2(l, name, cc), None,
                        x_hi, src=scaled)

    seen, at = {}, 0
    for name, ph in phases.items():
        if ".in" in name:
            seen[name] = at
            at += ph.n
    WIDE = dict(hi=fhi, lo=flo, a=silu_a, full=hidden)
    NARROW = dict(hi=f2hi, lo=f2lo, a=silu_a2, full=hidden2)

    def ffn_in_pe(pe, name, s, T, x_hi, x_lo):
        ph = phases[name]

        def one(u, i, it):
            start_unit(pe, u, it)
            for half in range(2):
                first = u == ph.u0 and half == 0 and name.endswith("0")
                feature_major(pe, u, half, range(KC), x_hi, x_lo, T,
                              arrived=(lambda k: DVE_.at("u", s, k)) if first else None).then_inc(product, 1)
        sweep(pe, ph, one)

    def ffn_in_act(act, name, T, buf):
        ph = phases[name]

        def one(u, i, it):
            f = seen[name] + u - ph.u0
            split_hi(act, u + 1, it)
            act.wait_ge(product, plus(2 * u + 1, 4, it))
            act.wait_ge(evicted, plus(u - 1, 2, it))
            act.activation(buf["a"][:, u % 2, 0:T], banks[:, bank(u, 0), 0:T], ACT.Silu).then_inc(f_silu, 1)
            act.wait_ge(evicted, plus(u + 1, 2, it))
            act.copy(buf["hi"][:, i, 0:T], buf["full"][:, u % 2, 0:T]).then_inc(f_hi, 1)
        sweep(act, ph, one)

    def ffn_in_dve(dve, name, T, buf):
        ph = phases[name]

        def one(u, i, it):
            f = seen[name] + u - ph.u0
            split_lo(dve, u + 1, it)
            dve.wait_ge(product, plus(2 * u + 2, 4, it))
            dve.wait_ge(f_silu, plus(f + 1, 2, it))
            if f >= 2:
                dve.wait_ge(f_split, plus(f - 1, 2, it))
            dve.tensor_tensor(buf["full"][:, u % 2, 0:T], buf["a"][:, u % 2, 0:T], banks[:, bank(u, 1), 0:T],
                              ALU.mult).then_inc(evicted, 1)
            dve.wait_ge(f_hi, plus(f + 1, 2, it))
            dve.tensor_tensor(buf["lo"][:, i, 0:T], buf["full"][:, u % 2, 0:T],
                              buf["hi"][:, i, 0:T].bitcast(F32), ALU.subtract).then_inc(f_split, 1)
        sweep(dve, ph, one)

    def ffn_out_pe(pe, name, T, buf):
        ph, before = phases[name], seen[name.replace("out", "in")]
        for i in range(ph.n):
            start_unit(pe, ph.u0 + i)
            for half in range(2):
                feature_major(pe, ph.u0 + i, half, range(FC), buf["hi"], buf["lo"], T,
                              arrived=(lambda k: (f_split, before + k + 1)) if i + half == 0 else None)\
                    .then_inc(product, 1)

    def out_pe(pe, name, T, x_hi, x_lo, arrived):
        ph = phases[name]
        for i in range(ph.n):
            start_unit(pe, ph.u0 + i)
            for half in range(2):
                feature_major(pe, ph.u0 + i, half, range(KC), x_hi, x_lo, T,
                              arrived=arrived if i + half == 0 else None).then_inc(product, 1)

    def out_act(act, name, s=None, T=None):
        ph = phases[name]
        for i in range(ph.n):
            split_hi(act, ph.u0 + i + 1)
            if s is not None:
                squares_act(act, s, T, last_evicted(ph), (2 * i, 2 * i + 1))

    def out_dve(dve, name, T, gated_by, ready):
        ph = phases[name]
        for i in range(ph.n):
            u = ph.u0 + i
            split_lo(dve, u + 1)
            for half in range(2):
                cc = 2 * i + half
                dve.wait_ge(product, 2 * u + half + 1)
                if ready is not None:
                    dve.wait_ge(*ready(cc))
                for kind, a, b in kinds(T):
                    ins = dve.scalar_tensor_tensor(h[:, cc, a:b], banks[:, bank(u, half), a:b], gated_by(cc, kind),
                                                   h[:, cc, a:b], ALU.mult, ALU.add)
            ins.then_inc(evicted, 1)

    def gate1(s):
        return lambda cc, kind: vG[:, s, cc, kind:kind + 1]

    def block1_ffn(engine, e, tag, s, T):
        after = dict(s=s + 1, T=T)
        if engine == "pe":
            for half in range(2):
                ffn_in_pe(e, f"{tag}.in{half}", s, T, uhi, ulo)
                ffn_out_pe(e, f"{tag}.out{half}", T, WIDE)
            means_pe(e, s + 1, T, True)
        if engine == "act":
            for half in range(2):
                ffn_in_act(e, f"{tag}.in{half}", T, WIDE)
                out_act(e, f"{tag}.out{half}", **(after if half else {}))
        if engine == "dve":
            for half in range(2):
                ffn_in_dve(e, f"{tag}.in{half}", T, WIDE)
                out_dve(e, f"{tag}.out{half}", T, gate1(s),
                        last_evicted(phases[f"{tag}.out0"]) if half else lambda cc: POOL_.at("h", s, cc))
        if engine == "pool":
            sums_pool(e, s + 1, T, last_evicted(phases[f"{tag}.out1"]), True)

    SCORE_BANKS = (0, 1, 4, 5)

    def score_bank(n):
        return SCORE_BANKS[n % 4]

    def attention_pe(pe, tag, tiles):
        def scores(n):
            t = tiles[n]
            if n >= 4:
                pe.wait_ge(*ACT_.at(tag, "exp", n - 4))
            pe.matmul(banks[:, score_bank(n), 0:t["n"]], t["q"], t["k"], start=True, stop=True)\
                .then_inc(*PE_.up((tag, "scores", n)))

        def transposes(n):
            t = tiles[n]
            pe.wait_ge(*DVE_.at(tag, "probs", n))
            if n >= 2:
                pe.wait_ge(*ACT_.at(tag, "probs_t", n - 2))
            for j in range(t["n"] // P):
                mm = pe.transpose(banks[:, 2 + n % 2, j * P:(j + 1) * P], probs[:, n % 2, j * P:(j + 1) * P], ident)
            mm.then_inc(*PE_.up((tag, "transposed", n)))

        def values(n):
            t = tiles[n]
            pe.wait_ge(*ACT_.at(tag, "probs_t", n))
            if t["first"] and t["group"] >= 2:
                pe.wait_ge(*DVE_.at(tag, "out", t["group"] - 2))
            p0, a = t["at"]
            for j, v in enumerate(t["v"]):
                mm = pe.matmul(banks[p0:p0 + HD, 6 + t["group"] % 2, a:a + P], v, probs_t[:, n % 2, j * P:(j + 1) * P],
                               start=(j == 0), stop=(j == len(t["v"]) - 1))
            mm.then_inc(*PE_.up((tag, "values", n)))

        N = len(tiles)
        scores(0)
        scores(1)
        for n in range(N + 2):
            if n + 2 < N:
                scores(n + 2)
            if 1 <= n <= N:
                transposes(n - 1)
            if n >= 2:
                values(n - 2)

    def attention_act(act, tag, tiles, y_hi):
        N = len(tiles)
        for n in range(N + 3):
            if n < N:
                t = tiles[n]
                act.wait_ge(*DVE_.at(tag, "max", n))
                if n >= 2:
                    act.wait_ge(*PE_.at(tag, "transposed", n - 2))
                act.activation(probs[:, n % 2, 0:t["n"]], banks[:, score_bank(n), 0:t["n"]], ACT.Exp,
                               bias=small[:, n % 4:n % 4 + 1], accum_out=small[:, 4 + n % 4:5 + n % 4])\
                    .then_inc(*ACT_.up((tag, "exp", n)))
                if t["sink"] is not None:
                    act.activation(small[:, 8 + n % 4:9 + n % 4], t["sink"], ACT.Exp, bias=small[:, n % 4:n % 4 + 1])\
                        .then_inc(*ACT_.up((tag, "sink", n)))
            if 1 <= n <= N:
                m = n - 1
                act.wait_ge(*PE_.at(tag, "transposed", m))
                if m >= 2:
                    act.wait_ge(*PE_.at(tag, "values", m - 2))
                w = tiles[m]["n"]
                act.copy(probs_t[:, m % 2, 0:w], banks[:, 2 + m % 2, 0:w]).then_inc(*ACT_.up((tag, "probs_t", m)))
            if n >= 3 and tiles[n - 3]["last"]:
                t = tiles[n - 3]
                act.wait_ge(*PE_.at(tag, "values", n - 3))
                w = t["width"]
                act.copy(y_hi[:, t["chunk"], 0:w], banks[:, 6 + t["group"] % 2, 0:w])\
                    .then_inc(*ACT_.up((tag, "out", t["group"])))

    def attention_dve(dve, tag, tiles, y_hi, y_lo):
        N = len(tiles)
        for n in range(N + 3):
            if n < N:
                t = tiles[n]
                sc = banks[:, score_bank(n), 0:t["n"]]
                dve.wait_ge(*PE_.at(tag, "scores", n))
                if t["added"] is not None:
                    if t["added ready"] is not None:
                        dve.wait_ge(*t["added ready"])
                    w = t["added"].shape[-1]
                    part = banks[:, score_bank(n), 0:w]
                    dve.scalar_tensor_tensor(part, part, t["scale"], t["added"], ALU.mult, ALU.add)\
                        .then_inc(*DVE_.up((tag, "added", n)))
                    dve.wait_ge(*DVE_.here())
                nmax = small[:, n % 4:n % 4 + 1]
                if t["sink"] is None:
                    dve.tensor_reduce(nmax, sc, AX.X, ALU.max, negate=True).then_inc(*DVE_.up((tag, "max", n)))
                else:
                    dve.tensor_reduce(nmax, sc, AX.X, ALU.max).then_inc(*DVE_.up())
                    dve.wait_ge(*DVE_.here())
                    dve.tensor_scalar(nmax, nmax, t["sink"], -1.0, ALU.max, ALU.mult)\
                        .then_inc(*DVE_.up((tag, "max", n)))
            if 1 <= n <= N:
                m = n - 1
                t = tiles[m]
                total, inv = small[:, 4 + m % 4:5 + m % 4], small[:, 12 + m % 4:13 + m % 4]
                dve.wait_ge(*ACT_.at(tag, "exp", m))
                if t["sink"] is not None:
                    dve.wait_ge(*ACT_.at(tag, "sink", m))
                    dve.tensor_tensor(total, total, small[:, 8 + m % 4:9 + m % 4], ALU.add).then_inc(*DVE_.up())
                    dve.wait_ge(*DVE_.here())
                dve.reciprocal(inv, total).then_inc(*DVE_.up())
                dve.wait_ge(*DVE_.here())
                pr = probs[:, m % 2, 0:t["n"]]
                dve.tensor_scalar(pr, pr, inv, None, ALU.mult).then_inc(*DVE_.up((tag, "probs", m)))
            if n >= 3 and tiles[n - 3]["last"]:
                t = tiles[n - 3]
                dve.wait_ge(*ACT_.at(tag, "out", t["group"]))
                w = t["width"]
                dve.tensor_tensor(y_lo[:, t["chunk"], 0:w], banks[:, 6 + t["group"] % 2, 0:w],
                                  y_hi[:, t["chunk"], 0:w].bitcast(F32), ALU.subtract)\
                    .then_inc(*DVE_.up((tag, "out", t["group"])))

    def na_tiles():
        tiles = []
        for hd in range(NH):
            ck, p0 = hd // 2, HD * (hd % 2)
            for t in range(4):
                k0 = 0 if t < 2 else S
                tiles.append(dict(
                    q=qT[p0:p0 + HD, ck, t * P:(t + 1) * P], k=kT[p0:p0 + HD, ck, k0:T2], n=T2 - k0,
                    added=na_bias[:, hd % 2, t * S:(t + 1) * S] if t < 2 else None, scale=1.0,
                    sink=None, v=[vv[:, kt, hd * HD:(hd + 1) * HD] for kt in range(k0 // P, 4)],
                    group=ck, chunk=ck, at=(p0, t * P), first=(hd % 2 == 0 and t == 0),
                    last=(hd % 2 == 1 and t == 3), width=T2))
                tiles[-1]["added ready"] = POOL_.at("bias", hd) if t == 0 else None
        return tiles

    def wa_tiles():
        tiles = []
        for ck in range(KC):
            for side in range(2):
                hd = 8 * (ck // 4) + ck % 4 + 4 * side
                kv, p0 = 2 * (ck // 4) + side, HD * side
                for t in range(2):
                    tiles.append(dict(
                        q=qT[p0:p0 + HD, ck, t * P:(t + 1) * P], k=kT[p0:p0 + HD, ck // 4, 0:T2], n=T2,
                        added=c("wa_mask")[:, t * S:(t + 1) * S], scale=1.0, sink=sinks[:, hd:hd + 1],
                        v=[vv[:, kt, kv * HD:(kv + 1) * HD] for kt in range(4)], group=ck, chunk=ck,
                        at=(p0, t * P), first=(side == 0 and t == 0), last=(side == 1 and t == 1), width=S))
                    tiles[-1]["added ready"] = None
        return tiles

    def mla_tiles():
        tiles = []
        for hd in range(MLA_H):
            for t in range(2):
                n = (t + 1) * P
                tiles.append(dict(
                    q=qk[0:QK, hd, t * P:(t + 1) * P], k=qk[0:QK, 4 + hd, 0:n], n=n,
                    added=c("causal")[:, t * S:t * S + n], scale=QK ** -0.5, sink=None,
                    v=[mla_v[:, kt, hd * HD:(hd + 1) * HD] for kt in range(t + 1)], group=hd // 2,
                    chunk=6 + hd // 2, at=(HD * (hd % 2), t * P), first=(hd % 2 == 0 and t == 0),
                    last=(hd % 2 == 1 and t == 1), width=S))
                tiles[-1]["added ready"] = None
        return tiles

    def qkv_pe(pe, tag, s, Tq):
        for what, T in (("q", Tq), ("k", T2)):
            ph = phases[f"{tag}.{what}"]
            for i in range(ph.n):
                start_unit(pe, ph.u0 + i)
                for half in range(2):
                    first = what == "q" and i + half == 0
                    feature_major(pe, ph.u0 + i, half, range(KC), uhi, ulo, T,
                                  arrived=(lambda k: DVE_.at("u", s, k)) if first else None).then_inc(product, 1)
        ph = phases[f"{tag}.v"]
        for i in range(ph.n):
            u = ph.u0 + i
            start_unit(pe, u)
            for tile in range(4):
                out = banks[:, bank(u, tile // 2), (tile % 2) * 256:(tile % 2) * 256 + 256]
                mm = token_major(pe, u, out, tile, 0, 256, uhi, ulo)
                if tile % 2:
                    mm.then_inc(product, 1)

    def qkv_act(act, tag, Tq):
        for what, T, dst, scale in (("q", Tq, qT, HD ** -0.5), ("k", T2, kT, 1.0)):
            ph = phases[f"{tag}.{what}"]
            for i in range(ph.n):
                u = ph.u0 + i
                split_hi(act, u + 1)
                for half in range(2):
                    act.wait_ge(product, 2 * u + half + 1)
                    ins = act.activation(dst[:, 2 * i + half, 0:T], banks[:, bank(u, half), 0:T], ACT.Copy, scale=scale)
                ins.then_inc(evicted, 1)
        ph = phases[f"{tag}.v"]
        for i in range(ph.n):
            u = ph.u0 + i
            split_hi(act, u + 1)
            for half in range(2):
                act.wait_ge(product, 2 * u + half + 1)
                ins = act.copy(vv[:, 2 * half:2 * half + 2, i * 256:(i + 1) * 256],
                               banks[:, bank(u, half), :].rearrange("p (t n) -> p t n", t=2))
            ins.then_inc(evicted, 1)

    def qkv_dve(dve, tag):
        for what in "qkv":
            ph = phases[f"{tag}.{what}"]
            for i in range(ph.n):
                split_lo(dve, ph.u0 + i + 1)

    def qkv_done(e, tag):
        ph = phases[f"{tag}.v"]
        e.wait_ge(evicted, ph.u0 + ph.n)

    def wa_rope_pe(pe):
        for j in range(10):
            src = qT[:, j, 0:S] if j < KC else kT[:, j - KC, 0:S]
            if j >= 4:
                pe.wait_ge(*DVE_.at("rotated", j - 4))
            pe.matmul(banks[:, 4 + j % 4, 0:S], c("rope_perm"), src, start=True, stop=True)\
                .then_inc(*PE_.up(("swapped", j)))
        pe.wait_ge(*DVE_.at("rotated", 9))

    def wa_rope_dve(dve):
        qkv_done(dve, "L1")
        for j in range(10):
            x = qT[:, j, 0:S] if j < KC else kT[:, j - KC, 0:S]
            t = squares[:, j % 2, 0:S]
            dve.wait_ge(*PE_.at("swapped", j))
            dve.tensor_tensor(t, banks[:, 4 + j % 4, 0:S], c("rope_sin"), ALU.mult).then_inc(*DVE_.up())
            dve.tensor_tensor(x, x, c("rope_cos"), ALU.mult).then_inc(*DVE_.up())
            dve.wait_ge(*DVE_.here())
            dve.tensor_tensor(x, x, t, ALU.add).then_inc(*DVE_.up(("rotated", j)))

    def bias_pool(pool):
        pool.wait_ge(evicted, phases["L0.q"].u0 + 1)
        for hd in range(NH + 1):
            if hd < NH:
                if hd >= 2:
                    pool.wait_ge(*DVE_.at("L0", "added", 4 * (hd - 2) + 1))
                pool.dma_start(na_bias[:, hd % 2, :], A["na_rpb"][hd]).then_inc(bias_loaded[hd % 2], 16)
            if hd >= 1:
                m = hd - 1
                pool.wait_ge(bias_loaded[m % 2], 16 * (m // 2 + 1))
                pool.tensor_tensor(na_bias[:, m % 2, :], na_bias[:, m % 2, :], c("na_mask"), ALU.add)\
                    .then_inc(*POOL_.up(("bias", m)))

    def z_pe(pe, l, s):
        ph = phases[f"M{l}.z"]
        for i in range(ph.n):
            u = ph.u0 + i
            start_unit(pe, u)
            if i in (2, 7, 8):
                for tile in range(2):
                    token_major(pe, u, banks[:, bank(u, tile), 0:256], tile, 0, 256, u2hi, u2lo)\
                        .then_inc(product, 1)
                continue
            for half in range(2):
                mm = feature_major(pe, u, half, range(KC), u2hi, u2lo, S,
                                   arrived=(lambda k: DVE_.at("u", s, k)) if i + half == 0 else None)
                if i == 12 and half == 1:
                    for tile in range(2):
                        mm = token_major(pe, u, banks[:, bank(u, 1), 256 + 8 * tile:264 + 8 * tile], tile,
                                         P, P + 8, u2hi, u2lo)
                mm.then_inc(product, 1)

    def z_act(act, l):
        ph = phases[f"M{l}.z"]
        for i in range(ph.n):
            u = ph.u0 + i
            split_hi(act, u + 1)
            if i in (2, 7, 8):
                continue
            if i:
                act.wait_ge(evicted, u)
            for half in range(2):
                ps = banks[:, bank(u, half), 0:S]
                act.wait_ge(product, 2 * u + half + 1)
                if i == 0:
                    act.wait_ge(*DVE_.at("sbq bias"))
                    ins = act.activation(sbq[:, half], ps, ACT.Identity, scale=HD ** -0.5, bias=vec2(l, "b_sbq", half))
                elif i == 1:
                    ins = act.activation(sbk[:, half], ps, ACT.Identity, bias=vec2(l, "b_sbk", half))
                elif i < 7:
                    cc = 2 * (i - 3) + half
                    ins = act.activation(conv_in[:, cc, 3:], ps, ACT.Identity, bias=vec2(l, "b_mlqk", cc))
                elif i < 11:
                    cc = 2 * (i - 9) + half
                    ins = act.activation(osig[:, cc], ps, ACT.Sigmoid, bias=vec2(l, "b_mlo", cc))
                elif i == 11:
                    ins = act.activation(cq[:, half], ps, ACT.Identity, bias=vec2(l, "b_cq", half))
                elif half == 0:
                    ins = act.activation(cq[:, 2], ps, ACT.Identity, bias=vec2(l, "b_ckv"))
                else:
                    ins = act.activation(kr[HD:QK, :], banks[HD:QK, bank(u, 1), 0:S], ACT.Identity,
                                         bias=vec2(l, "b_kr")[HD:QK])
            if i < 12:
                ins.then_inc(evicted, 1)
            else:
                ins.then_inc(*ACT_.up(("kr", l)))

    def z_dve(dve, l):
        ph = phases[f"M{l}.z"]
        for i in range(ph.n):
            u = ph.u0 + i
            split_lo(dve, u + 1)
            if i in (2, 7, 8, 12):
                dve.wait_ge(evicted, u)
            if i in (2, 7, 8):
                for tile in range(2):
                    dst = sbv[:, tile, :] if i == 2 else mlv[:, tile, (i - 7) * 256:(i - 6) * 256]
                    at = ROW2["b_sbv"][0] if i == 2 else ROW2["b_mlv"][0] + (i - 7) * 256
                    dve.wait_ge(product, 2 * u + tile + 1)
                    ins = dve.tensor_tensor(dst, banks[:, bank(u, tile), 0:256], rows2[:, l, at:at + 256], ALU.add)
                ins.then_inc(evicted, 1)
            if i == 12:
                dve.wait_ge(*ACT_.at("kr", l))
                at = ROW2["b_if"][0]
                for tile in range(2):
                    ins = dve.tensor_tensor(iff[:, tile], banks[:, bank(u, 1), 256 + 8 * tile:264 + 8 * tile],
                                            rows2[:, l, at:at + 8], ALU.add)
                ins.then_inc(evicted, 1)

    def z_done(e, l):
        ph = phases[f"M{l}.z"]
        e.wait_ge(evicted, ph.u0 + ph.n)

    def sb_bufs(r):
        return (banks[:, 2 * r:2 * r + 2, 0:384], banks[:, 4 + 2 * r:6 + 2 * r, 0:384],
                squares[:, :, 0:384], sums[:, :, 0:384], scaled[:, :, 0:384], full_u[:, :, 0:384])

    def sb_pe(pe, l):
        z_done(pe, l)
        for r in range(2):
            for hh in range(2):
                rows = slice(HD * hh, HD * hh + HD)
                pe.matmul(banks[:, 2 * r + hh, 0:256], sbk[rows, r, 0:P], sbq[rows, r, :], start=True, stop=True)
                mm = pe.matmul(banks[:, 2 * r + hh, 256:384], sbk[rows, r, P:S], sbq[rows, r, P:S],
                               start=True, stop=True)
            mm.then_inc(*PE_.up(("sb z", l, r)))
        for r in range(2):
            log_keep, w = sums, full_u
            pe.wait_ge(*DVE_.at("sb keep", l, r))
            for hh in range(2):
                pe.matmul(banks[:, 4 + 2 * r + hh, 0:384], c("tri_strict"), log_keep[:, hh, 0:384],
                          start=True, stop=True)
                mm = pe.matmul(banks[:, 4 + 2 * r + hh, P:S], c("ones"), log_keep[:, hh, 256:384],
                               start=False, stop=True, skip_group_check=True)
            mm.then_inc(*PE_.up(("sb later", l, r)))
            pe.wait_ge(*DVE_.at("sb w", l, r))
            for hh in range(2):
                hd = 2 * r + hh
                out = banks[HD * hh:HD * hh + HD, 2 * r, :]
                pe.matmul(out[:, 0:S], sbv[:, 0, hd * HD:(hd + 1) * HD], w[:, hh, 0:256], start=True, stop=True)
                mm = pe.matmul(out[:, P:S], sbv[:, 1, hd * HD:(hd + 1) * HD], w[:, hh, 256:384],
                               start=False, stop=True, skip_group_check=True)
            mm.then_inc(*PE_.up(("sb out", l, r)))

    def sb_act(act, l):
        for r in range(2):
            z, later, e, keep, zl, w = sb_bufs(r)
            act.wait_ge(*PE_.at("sb z", l, r))
            act.activation(e, z, ACT.Abs).then_inc(*ACT_.up())
            act.wait_ge(*ACT_.here())
            act.activation(e, e, ACT.Exp, scale=-1.0).then_inc(*ACT_.up())
            act.wait_ge(*ACT_.here())
            act.activation(e, e, ACT.Ln, bias=c("one")).then_inc(*ACT_.up(("sb ln", l, r)))
            act.wait_ge(*DVE_.at("sb logw", l, r))
            act.activation(w, zl, ACT.Exp).then_inc(*ACT_.up(("sb exp", l, r)))
            act.wait_ge(*PE_.at("sb out", l, r))
            act.copy(yhi[:, r, :], banks[:, 2 * r, 0:S]).then_inc(*ACT_.up(("sb y", l, r)))

    def sb_dve(dve, l):
        mask = c("sb_mask")
        for r in range(2):
            z, later, e, keep, zl, w = sb_bufs(r)
            dve.wait_ge(*ACT_.at("sb ln", l, r))
            dve.scalar_tensor_tensor(keep, z, 0.0, e, ALU.max, ALU.add).then_inc(*DVE_.up())
            dve.wait_ge(*DVE_.here())
            dve.tensor_tensor(zl, z, keep, ALU.subtract).then_inc(*DVE_.up())
            dve.wait_ge(*DVE_.here())
            for hh in range(2):
                dve.scalar_tensor_tensor(keep[:, hh], keep[:, hh], -1.0, mask, ALU.mult, ALU.mult)\
                    .then_inc(*DVE_.up(("sb keep", l, r)))
            dve.wait_ge(*PE_.at("sb later", l, r))
            dve.tensor_tensor(zl, later, zl, ALU.add).then_inc(*DVE_.up(("sb logw", l, r)))
            dve.wait_ge(*ACT_.at("sb exp", l, r))
            for hh in range(2):
                dve.tensor_tensor(w[:, hh], w[:, hh], mask, ALU.mult).then_inc(*DVE_.up(("sb w", l, r)))
            dve.wait_ge(*ACT_.at("sb y", l, r))
            dve.tensor_tensor(ylo[:, r, :], banks[:, 2 * r, 0:S], yhi[:, r, :].bitcast(F32), ALU.subtract)\
                .then_inc(*DVE_.up(("y", l, r)))

    def slot(n, w=8):
        return small[:, 16 + 8 * n:16 + 8 * n + w]

    LF, CUM, FTOT, R_, M_, RMAX, NEGM, EXPARG, EXPS, DEN, RDEN, SS, MNEW, ABS = 0, 1, 2, 3, 4, 5, 6, 7, 9, 11, 13, 14, 15, 16

    def tc(ap):
        return ap.rearrange("p (t c) -> p t c", t=2)

    sT, w_buf, n_buf = squares, scaled, sums

    def flat(t):
        return t[:].rearrange("p a b -> p (a b)")

    def ml_pe(pe, l):
        tri, ones, q, k = c("tri_incl"), c("ones"), mlqk[:, 0:4], mlqk[:, 4:8]
        pe.wait_ge(*DVE_.at("ml lf", l))
        pe.matmul(banks[:, 4, 0:8], tri, slot(LF), start=True, stop=True)
        pe.matmul(banks[:, 4, 8:16], ones, slot(LF), start=True, stop=True).then_inc(*PE_.up(("ml cum", l)))
        pe.wait_ge(*DVE_.at("ml diag r", l))
        for t in range(2):
            mm = pe.matmul(banks[:, 4 + t, :], ones, sT[:, t, :], start=True, stop=True)
        mm.then_inc(*PE_.up(("ml r rows", l)))
        pe.wait_ge(*ACT_.at("ml k", l))
        for t in range(2):
            for hd in range(4):
                ts = slice(t * P, t * P + P)
                mm = pe.matmul(banks[:, 6 + t, hd * P:(hd + 1) * P], k[:, hd, ts], q[:, hd, ts],
                               start=True, stop=True)
        mm.then_inc(*PE_.up(("ml kq", l)))
        pe.wait_ge(*DVE_.at("y", l, 1))
        for hd in range(4):
            mm = pe.transpose(banks[:, 0, hd * P:(hd + 1) * P], k[:, hd, 0:P], ident)
        mm.then_inc(*PE_.up(("ml k tokens", l)))
        pe.wait_ge(*DVE_.at("ml diag m", l))
        for t in range(2):
            mm = pe.matmul(banks[:, 4 + t, :], ones, sT[:, t, :], start=True, stop=True)
        mm.then_inc(*PE_.up(("ml m rows", l)))
        pe.wait_ge(*ACT_.at("ml k end", l))
        for hd in range(4):
            kd = full_u[:, 0, hd * P:(hd + 1) * P]
            pe.matmul(banks[:, 1, hd * P:(hd + 1) * P], kd, mlv[:, 0, hd * P:(hd + 1) * P], start=True, stop=True)
            mm = pe.matmul(banks[:, 2, hd:hd + 1], kd, ones[:, 0:1], start=True, stop=True)
        mm.then_inc(*PE_.up(("ml state", l)))
        pe.wait_ge(*ACT_.at("ml state", l))
        for hd in range(4):
            pe.matmul(banks[:, 3, hd * P:(hd + 1) * P], q[:, hd, P:S], full_u[:, 1, hd * P:(hd + 1) * P],
                      start=True, stop=True)
            mm = pe.matmul(banks[:, 0, 8 + hd:9 + hd], q[:, hd, P:S], slot(ABS)[:, hd:hd + 1], start=True, stop=True)
        pe.wait_ge(*DVE_.at("ml scores", l))
        for j in range(8):
            t, hd = j // 4, j % 4
            s_ = flat(sT)[:, j * P:(j + 1) * P]
            pe.matmul(banks[:, 4 + t, hd * P:(hd + 1) * P], s_, mlv[:, t, hd * P:(hd + 1) * P], start=True, stop=True)
            mm = pe.matmul(banks[:, 0, j:j + 1], s_, ones[:, 0:1], start=True, stop=True)
        mm.then_inc(*PE_.up(("ml num", l)))
        pe.wait_ge(*DVE_.at("ml h", l))
        for j in range(8):
            t, hd = j // 4, j % 4
            at = (hd % 2) * S + t * P
            mm = pe.transpose(banks[:, 6 + hd // 2, at:at + P], flat(n_buf)[:, j * P:(j + 1) * P], ident)
        mm.then_inc(*PE_.up(("ml h features", l)))

    def ml_act(act, l):
        f = iff[:, :, 4:8]
        z_done(act, l)
        ab = tc(slot(ABS))
        act.activation(ab, f, ACT.Abs).then_inc(*ACT_.up())
        act.wait_ge(*ACT_.here())
        act.activation(ab, ab, ACT.Exp, scale=-1.0).then_inc(*ACT_.up())
        act.wait_ge(*ACT_.here())
        act.activation(ab, ab, ACT.Ln, bias=c("one")).then_inc(*ACT_.up(("ml ln", l)))
        act.wait_ge(*DVE_.at("ml conv", l))
        for g in range(2):
            x = mlqk[:, 4 * g:4 * g + 4]
            act.activation(x, x, ACT.Silu).then_inc(*ACT_.up())
        act.wait_ge(*ACT_.here())
        act.mul(mlqk[:, 4:8], mlqk[:, 4:8], 128 ** -0.5).then_inc(*ACT_.up(("ml k", l)))
        act.wait_ge(*DVE_.at("ml args", l))
        act.activation(slot(EXPS, 16), slot(EXPARG, 16), ACT.Exp).then_inc(*ACT_.up(("ml exps", l)))
        act.wait_ge(*ACT_.here())
        act.wait_ge(*PE_.at("ml k tokens", l))
        act.wait_ge(*PE_.at("sb out", l, 1))
        for hd in range(4):
            act.activation(full_u[:, 0, hd * P:(hd + 1) * P], banks[:, 0, hd * P:(hd + 1) * P], ACT.Copy,
                           scale=slot(EXPS)[:, hd:hd + 1]).then_inc(*ACT_.up(("ml k end", l)))
        act.wait_ge(*DVE_.at("ml m masked", l))
        for j in range(8):
            w = flat(w_buf)[:, j * P:(j + 1) * P]
            act.activation(w, w, ACT.Exp, bias=slot(R_)[:, j:j + 1]).then_inc(*ACT_.up(("ml w", l)))
        act.wait_ge(*PE_.at("ml state", l))
        act.copy(full_u[:, 1, :], banks[:, 1, :]).then_inc(*ACT_.up())
        act.copy(slot(ABS)[:, 0:4], banks[:, 2, 0:4]).then_inc(*ACT_.up(("ml state", l)))
        act.wait_ge(*DVE_.at("ml ss", l))
        act.activation(slot(SS), slot(SS), ACT.Ln, scale=1 / 128, bias=c("rms_eps")).then_inc(*ACT_.up())
        act.wait_ge(*ACT_.here())
        act.activation(slot(SS), slot(SS), ACT.Exp, scale=-0.5).then_inc(*ACT_.up(("ml rms", l)))
        for hd in range(4):
            act.wait_ge(*DVE_.at("ml y", l, hd))
            act.copy(yhi[:, 2 + hd, :], flat(w_buf)[:, hd * S:(hd + 1) * S]).then_inc(*ACT_.up(("ml y hi", l, hd)))

    def ml_dve(dve, l):
        tt, up = dve.tensor_tensor, DVE_.up
        for tap in range(4):
            for cc in range(KC):
                x, w = conv_in[:, cc, tap:tap + S], vec2(l, "conv_w", 8 * tap + cc)
                if tap == 0:
                    dve.wait_ge(*POOL_.at("conv pad", l))
                    dve.tensor_scalar(mlqk[:, cc], x, w, vec2(l, "conv_b", cc), ALU.mult, ALU.add)\
                        .then_inc(*up(("ml tap", l, tap, cc)))
                else:
                    dve.wait_ge(*DVE_.at("ml tap", l, tap - 1, cc))
                    dve.scalar_tensor_tensor(mlqk[:, cc], x, w, mlqk[:, cc], ALU.mult, ALU.add)\
                        .then_inc(*up(("ml tap", l, tap, cc)))
        DVE_.book[("dve_step", ("ml conv", l))] = DVE_.n
        dve.wait_ge(*ACT_.at("ml ln", l))
        dve.scalar_tensor_tensor(tc(slot(LF)), iff[:, :, 4:8], 0.0, tc(slot(ABS)), ALU.min, ALU.subtract)\
            .then_inc(*up(("ml lf", l)))
        dve.wait_ge(*PE_.at("ml cum", l))
        dve.tensor_copy(slot(CUM, 16), banks[:, 4, 0:16]).then_inc(*up())
        dve.wait_ge(*DVE_.here())
        tt(tc(slot(R_)), iff[:, :, 0:4], tc(slot(CUM)), ALU.subtract).then_inc(*up())
        dve.wait_ge(*DVE_.here())
        for j in range(8):
            dve.tensor_scalar(flat(sT)[:, j * P:(j + 1) * P], ident, slot(R_)[:, j:j + 1], None, ALU.mult)\
                .then_inc(*up(("ml diag r", l)))
        dve.wait_ge(*PE_.at("ml r rows", l))
        rows = banks[:, 4:6, :].rearrange("p t (c s) -> p (t c) s", c=4)
        dve.tensor_reduce(slot(RMAX), rows, AX.X, ALU.max).then_inc(*up())
        causal = c("causal")[:, 0:P]
        wb = flat(w_buf).rearrange("p (j s) -> p j s", j=8)
        for j in range(8):
            tt(wb[:, j], rows[:, j], causal, ALU.add).then_inc(*up())
        dve.wait_ge(*DVE_.here())
        dve.tensor_reduce(slot(M_), wb, AX.X, ALU.max).then_inc(*up())
        dve.wait_ge(*DVE_.here())
        dve.tensor_scalar(slot(M_)[:, 0:4], slot(M_)[:, 0:4], 0.0, None, ALU.max).then_inc(*up())
        dve.scalar_tensor_tensor(slot(MNEW)[:, 0:4], slot(RMAX)[:, 0:4], 0.0, slot(FTOT)[:, 0:4], ALU.max, ALU.add)\
            .then_inc(*up())
        dve.wait_ge(*DVE_.here())
        tt(slot(M_)[:, 4:8], slot(M_)[:, 4:8], slot(MNEW)[:, 0:4], ALU.max).then_inc(*up())
        args = slot(EXPARG, 16)
        tt(args[:, 0:4], slot(FTOT)[:, 0:4], slot(MNEW)[:, 0:4], ALU.subtract).then_inc(*up())
        dve.wait_ge(*DVE_.here())
        tt(args[:, 0:4], args[:, 0:4], slot(R_)[:, 0:4], ALU.add).then_inc(*up())
        tt(args[:, 4:8], slot(MNEW)[:, 0:4], slot(M_)[:, 4:8], ALU.subtract).then_inc(*up())
        dve.scalar_tensor_tensor(args[:, 8:16], slot(CUM), -1.0, slot(M_), ALU.mult, ALU.subtract)\
            .then_inc(*up(("ml args", l)))
        dve.tensor_scalar(slot(NEGM), slot(M_), -1.0, None, ALU.mult).then_inc(*up())
        dve.wait_ge(*DVE_.here())
        for j in range(8):
            dve.tensor_scalar(flat(sT)[:, j * P:(j + 1) * P], ident, slot(NEGM)[:, j:j + 1], None, ALU.mult)\
                .then_inc(*up(("ml diag m", l)))
        dve.wait_ge(*PE_.at("ml m rows", l))
        for j in range(8):
            tt(wb[:, j], rows[:, j], c("causal_t"), ALU.add).then_inc(*up(("ml m masked", l)))
        dve.wait_ge(*ACT_.at("ml w", l))
        dve.wait_ge(*PE_.at("ml kq", l))
        kq = banks[:, 6:8, :]
        tt(sT[:], kq, w_buf[:], ALU.mult).then_inc(*up(("ml scores", l)))
        dve.wait_ge(*PE_.at("ml num", l))
        dve.wait_ge(*ACT_.at("ml exps", l))
        nb = flat(n_buf).rearrange("p (j s) -> p j s", j=8)
        w_inter = slot(EXPS)[:, 4:8]
        dve.tensor_copy(slot(DEN, 12), banks[:, 0, 0:12]).then_inc(*up())
        dve.tensor_copy(nb[:, 0:4], banks[:, 4, :].rearrange("p (c s) -> p c s", c=4)).then_inc(*up())
        dve.tensor_copy(nb[:, 4:8], banks[:, 5, :].rearrange("p (c s) -> p c s", c=4)).then_inc(*up())
        dve.wait_ge(*DVE_.here())
        for hd in range(4):
            dve.scalar_tensor_tensor(nb[:, 4 + hd], banks[:, 3, hd * P:(hd + 1) * P], w_inter[:, hd:hd + 1],
                                     nb[:, 4 + hd], ALU.mult, ALU.add).then_inc(*up())
        den = slot(DEN, 12)
        tt(den[:, 8:12], den[:, 8:12], w_inter, ALU.mult).then_inc(*up())
        dve.wait_ge(*DVE_.here())
        tt(den[:, 4:8], den[:, 4:8], den[:, 8:12], ALU.add).then_inc(*up())
        dve.wait_ge(*DVE_.here())
        dve.tensor_scalar(slot(RDEN), den[:, 0:8], -1.0, None, ALU.mult).then_inc(*up())
        dve.wait_ge(*DVE_.here())
        tt(den[:, 0:8], den[:, 0:8], slot(RDEN), ALU.max).then_inc(*up())
        dve.wait_ge(*DVE_.here())
        tt(den[:, 0:8], den[:, 0:8], slot(EXPS, 16)[:, 8:16], ALU.max).then_inc(*up())
        dve.wait_ge(*DVE_.here())
        dve.reciprocal(slot(RDEN), den[:, 0:8]).then_inc(*up())
        dve.wait_ge(*DVE_.here())
        for j in range(8):
            dve.tensor_scalar(nb[:, j], nb[:, j], slot(RDEN)[:, j:j + 1], None, ALU.mult).then_inc(*up())
        dve.wait_ge(*DVE_.here())
        tt(wb, nb, nb, ALU.mult).then_inc(*up())
        dve.wait_ge(*DVE_.here())
        dve.tensor_reduce(slot(SS), wb, AX.X, ALU.add).then_inc(*up(("ml ss", l)))
        dve.wait_ge(*ACT_.at("ml rms", l))
        for j in range(8):
            dve.tensor_scalar(nb[:, j], nb[:, j], slot(SS)[:, j:j + 1], None, ALU.mult).then_inc(*up(("ml h", l)))
        dve.wait_ge(*PE_.at("ml h features", l))
        for hd in range(5):
            if hd < 4:
                ps = banks[:, 6 + hd // 2, (hd % 2) * S:(hd % 2) * S + S]
                dve.scalar_tensor_tensor(flat(w_buf)[:, hd * S:(hd + 1) * S], ps, vec2(l, "ml_gain", hd), osig[:, hd],
                                         ALU.mult, ALU.mult).then_inc(*up(("ml y", l, hd)))
            if hd:
                g = hd - 1
                dve.wait_ge(*ACT_.at("ml y hi", l, g))
                tt(ylo[:, 2 + g, :], flat(w_buf)[:, g * S:(g + 1) * S], yhi[:, 2 + g, :].bitcast(F32), ALU.subtract)\
                    .then_inc(*up(("y", l, 2 + g)))

    rot = conv_in[0:QK, :, 0:S]

    def mla_pe(pe, l):
        pe.wait_ge(*ACT_.at("mla sq", l))
        sq = flat(squares)
        pe.matmul(banks[:, 0, 0:S], c("mean256"), sq[:, 0:S], start=True, stop=False)
        pe.matmul(banks[:, 0, 0:S], c("mean256"), sq[:, S:2 * S], start=False, stop=True)
        pe.matmul(banks[:, 0, S:2 * S], c("mean128"), sq[:, 2 * S:3 * S], start=True, stop=True)\
            .then_inc(*PE_.up(("mla ms", l)))
        pe.wait_ge(*DVE_.at("mla latents", l))
        pe.wait_ge(mla_loaded, 32 * (l + 1))
        for hd in range(4):
            out = (hd % 2) * S
            for k in range(2):
                pe.matmul(banks[0:QK, 1 + hd // 2, out:out + S], w_q[:, k, hd * QK:(hd + 1) * QK], cq[:, k],
                          start=(k == 0), stop=(k == 1))
            pe.matmul(banks[0:HD, 3 + hd // 2, out:out + S], w_kv[:, hd * P:hd * P + HD], cq[:, 2],
                      start=True, stop=True)
        wv = w_kv[:].rearrange("p (h two d) -> p h two d", h=4, two=2)[:, :, 1, :]
        for t in range(2):
            mm = pe.matmul(banks[:, 5, t * S:(t + 1) * S], cq[:, 2, t * P:(t + 1) * P], wv, start=True, stop=True)
        mm.then_inc(*PE_.up(("mla qkv", l)))
        pe.wait_ge(*ACT_.at("mla head sq", l))
        for j in range(4):
            mm = pe.matmul(banks[0:QK, j, :], c("mean96")[0:QK, 0:QK], rot[:, 2 * j:2 * j + 2, :], start=True, stop=True)
        mm.then_inc(*PE_.up(("mla head ms", l)))
        pe.wait_ge(*DVE_.at("mla heads", l))
        for j in range(4):
            mm = pe.matmul(banks[0:QK, 4 + j, :], c("mla_perm")[0:QK, 0:QK], qk[0:QK, 2 * j:2 * j + 2, :],
                           start=True, stop=True)
        mm.then_inc(*PE_.up(("mla swapped", l)))
        pe.wait_ge(*DVE_.at("mla rotated", l))
        attention_pe(pe, f"M{l}", mla_tiles())

    def mla_act(act, l):
        act.activation(flat(squares)[:, 0:3 * S], cq[:].rearrange("p a b -> p (a b)"), ACT.Square)\
            .then_inc(*ACT_.up(("mla sq", l)))
        act.wait_ge(*PE_.at("mla ms", l))
        act.activation(var[:], banks[:, 0, :], ACT.Ln, bias=c("rms_eps")).then_inc(*ACT_.up())
        act.wait_ge(*ACT_.here())
        act.activation(rstd[:], var[:], ACT.Exp, scale=-0.5).then_inc(*ACT_.up(("mla rms", l)))
        act.wait_ge(*PE_.at("mla qkv", l))
        for j in range(2):
            act.copy(qk[0:QK, 2 * j:2 * j + 2, :], banks[0:QK, 1 + j, :].rearrange("p (h t) -> p h t", h=2))\
                .then_inc(*ACT_.up())
            act.copy(qk[0:HD, 4 + 2 * j:6 + 2 * j, :], banks[0:HD, 3 + j, :].rearrange("p (h t) -> p h t", h=2))\
                .then_inc(*ACT_.up(("mla copied", l)))
        act.wait_ge(*POOL_.at("mla kr", l))
        act.wait_ge(*ACT_.here())
        act.activation(rot, qk[0:QK], ACT.Square).then_inc(*ACT_.up(("mla head sq", l)))
        act.wait_ge(*PE_.at("mla head ms", l))
        ms = banks[0:QK, 0:4, :].rearrange("p b (h t) -> p (b h) t", h=2)
        act.activation(rot, ms, ACT.Ln, bias=c("rms_eps")[0:QK]).then_inc(*ACT_.up())
        act.wait_ge(*ACT_.here())
        act.activation(rot, rot, ACT.Exp, scale=-0.5).then_inc(*ACT_.up(("mla head rms", l)))
        attention_act(act, f"M{l}", mla_tiles(), yhi)

    def mla_dve(dve, l):
        up = DVE_.up
        dve.wait_ge(*ACT_.at("mla rms", l))
        for k in range(3):
            gain = vec2(l, "q_norm", k) if k < 2 else vec2(l, "kv_norm")
            rs = rstd[:, 0:S] if k < 2 else rstd[:, S:2 * S]
            dve.scalar_tensor_tensor(cq[:, k], cq[:, k], gain, rs, ALU.mult, ALU.mult)\
                .then_inc(*up(("mla latents", l)))
        dve.wait_ge(*PE_.at("mla qkv", l))
        dve.tensor_copy(mla_v[:].rearrange("p t n -> p (t n)"), banks[:, 5, :]).then_inc(*up(("mla v", l)))
        dve.wait_ge(*ACT_.at("mla head rms", l))
        for g, name in ((0, "q_gain"), (1, "k_gain")):
            x = qk[0:QK, 4 * g:4 * g + 4, :]
            dve.scalar_tensor_tensor(x, x, vec2(l, name)[0:QK], rot[:, 4 * g:4 * g + 4, :], ALU.mult, ALU.mult)\
                .then_inc(*up(("mla heads", l)))
        dve.wait_ge(*PE_.at("mla swapped", l))
        swapped = banks[0:QK, 4:8, :].rearrange("p b (h t) -> p (b h) t", h=2)
        for j in range(8):
            dve.tensor_tensor(rot[:, j], swapped[:, j], rope_s[:], ALU.mult).then_inc(*up())
            dve.tensor_tensor(qk[0:QK, j], qk[0:QK, j], rope_c[:], ALU.mult).then_inc(*up())
        dve.wait_ge(*DVE_.here())
        dve.tensor_tensor(qk[0:QK], qk[0:QK], rot, ALU.add).then_inc(*up(("mla rotated", l)))
        attention_dve(dve, f"M{l}", mla_tiles(), yhi, ylo)

    def mix_pool(pool, l):
        ph = phases[f"M{l}.ffn0.out0"]
        pool.wait_ge(evicted, ph.u0 + ph.n)
        pool.memset(conv_in[:, :, 0:3], 0.0).then_inc(*POOL_.up(("conv pad", l)))
        z_done(pool, l)
        pool.wait_ge(*ACT_.at("kr", l))
        for hd in range(4):
            pool.wait_ge(*POOL_.here())
            pool.tensor_copy(qk[HD:QK, 4 + hd, :], kr[HD:QK, :]).then_inc(*POOL_.up(("mla kr", l)))

    def rope_tables_dve(dve):
        ang, turns, red = sums[0:QK, 0, 0:S], sums[0:QK, 1, 0:S], (squares[0:QK, 0, 0:S], squares[0:QK, 1, 0:S])
        up, TURN, MAGIC = DVE_.up, 2 * np.pi, float(1.5 * 2 ** 23)
        first = float(np.float32(6.28125))
        second = float(np.float32(np.round((TURN - first) * 2 ** 21) / 2 ** 21))
        third = float(np.float32(TURN - first - second))
        dve.wait_ge(block2_loaded, 16 * N_BLOCK2)
        dve.tensor_copy(ang, positions[:]).then_inc(*up())
        dve.wait_ge(*DVE_.here())
        dve.tensor_scalar(ang, ang, c("inv_freq")[0:QK], None, ALU.mult).then_inc(*up())
        dve.wait_ge(*DVE_.here())
        for j, quarter in enumerate((0.0, 0.25)):
            r = red[j]
            dve.tensor_scalar(turns, ang, float(1 / TURN), quarter, ALU.mult, ALU.add).then_inc(*up())
            dve.wait_ge(*DVE_.here())
            dve.tensor_scalar(turns, turns, MAGIC, None, ALU.add).then_inc(*up())
            dve.wait_ge(*DVE_.here())
            dve.tensor_scalar(turns, turns, MAGIC, None, ALU.subtract).then_inc(*up())
            dve.wait_ge(*DVE_.here())
            dve.scalar_tensor_tensor(r, turns, -first, ang, ALU.mult, ALU.add).then_inc(*up())
            for x in (second, third):
                dve.wait_ge(*DVE_.here())
                dve.scalar_tensor_tensor(r, turns, -x, r, ALU.mult, ALU.add).then_inc(*up())
            dve.wait_ge(*DVE_.here())
            dve.tensor_scalar(r, r, float(quarter * TURN), 3.1415925, ALU.add, ALU.min).then_inc(*up())
            dve.wait_ge(*DVE_.here())
            dve.tensor_scalar(r, r, -3.1415925, None, ALU.max).then_inc(*up("reduced"))
        for l in range(2):
            b = vec2(l, "b_sbq", 0, 2)
            dve.tensor_scalar(b, b, HD ** -0.5, None, ALU.mult).then_inc(*up("sbq bias"))

    def rope_tables_act(act):
        act.wait_ge(*DVE_.at("reduced"))
        act.activation(rope_s[:], squares[0:QK, 0, 0:S], ACT.Sin).then_inc(*ACT_.up())
        act.activation(rope_c[:], squares[0:QK, 1, 0:S], ACT.Sin).then_inc(*ACT_.up("rope tables"))

    def merge_loop(e, l, one):
        ph = phases[f"M{l}.merge"]
        with e.Fori(0, 4) as it:
            for j in range(4):
                one(ph.u0 + j, j, it)

    def merge_pe(pe, l):
        for r in range(KC):
            if r < 6:
                pe.wait_ge(*DVE_.at("y", l, r))
        for g in range(2):
            pe.wait_ge(*DVE_.at(f"M{l}", "out", g))

        def one(u, j, it):
            start_unit(pe, u, it, per=4)
            for half in range(2):
                if j < 3:
                    feature_major(pe, u, half, range(KC), u2hi, u2lo, S).then_inc(product, 1)
                    continue
                b = bank(u, half)
                feature_major(pe, u, half, range(0, 2), yhi, ylo, S, out=banks[:, b, 0:S])
                feature_major(pe, u, half, range(2, 6), yhi, ylo, S, out=banks[:, b, S:2 * S])
                feature_major(pe, u, half, range(6, 8), yhi, ylo, S, out=banks[:, 4 + half, 0:S])\
                    .then_inc(product, 1)
        merge_loop(pe, l, one)

    def split_hi_merge(act, u, it):
        act.wait_ge(landed[u % 2], 16 * (u // 2 + 1) + 32 * it)
        act.wait_ge(product, 2 * (u - 1) + 8 * it)
        act.copy(whi[u % 2][:, 0:KC * 256], raw[u % 2][:, 0:KC * 256]).then_inc(hi_done, 1)

    def merge_act(act, l):
        def one(u, j, it):
            split_hi_merge(act, u + 1, it)
            if j == 3:
                for half in range(2):
                    act.wait_ge(merged_full, 16 * l + 2 * half + 2 + 4 * it)
                    ins = act.copy(mhi[:, 2 * it + half, :], gated[:, half, 0, :])
                    ins.then_inc(merged_hi, 1)
                return
            if j == 0:
                act.wait_ge(evicted, u + 4 * it)
            for half in range(2):
                act.wait_ge(product, 2 * u + half + 1 + 8 * it)
                at = VEC2["b_gates"][0] + 8 * j + half
                ins = act.activation(gate[:, 2 * j + half, :], banks[:, bank(u, half), 0:S], ACT.Sigmoid,
                                     bias=v2[:, l, bass.ds(at + 2 * it, 1)])
            ins.then_inc(evicted, 1)
        merge_loop(act, l, one)

    merged_hi = sem("merged_hi_done")
    merged_lo = sem("merged_lo_done")
    merged_full = sem("merged_full_done")
    gated_done = sem("branches_gated")

    def merge_dve(dve, l):
        def one(u, j, it):
            dve.wait_ge(hi_done, u + 2 + 4 * it)
            v = (u + 1) % 2
            dve.tensor_tensor(wlo[v][:, 0:KC * 256], raw[v][:, 0:KC * 256], whi[v][:, 0:KC * 256].bitcast(F32),
                              ALU.subtract).then_inc(lo_done, 1)
            if j < 3:
                return
            dve.wait_ge(evicted, u + 4 * it)
            for half in range(2):
                dve.wait_ge(product, 2 * u + half + 1 + 8 * it)
                for b in range(3):
                    src = banks[:, bank(u, half), b * S:(b + 1) * S] if b < 2 else banks[:, 4 + half, 0:S]
                    ins = dve.tensor_tensor(gated[:, half, b, :], gate[:, 2 * b + half, :], src, ALU.mult)
                    if b < 2 or half == 0:
                        ins.then_inc(gated_done, 1)
                    else:
                        ins.then_inc(evicted, 1)
            for half in range(2):
                dve.wait_ge(merged_hi, 8 * l + half + 1 + 2 * it)
                dve.tensor_tensor(mlo[:, 2 * it + half, :], gated[:, half, 0, :],
                                  mhi[:, 2 * it + half, :].bitcast(F32), ALU.subtract).then_inc(merged_lo, 1)
        merge_loop(dve, l, one)

    def merge_pool(pool, l):
        pool.wait_ge(*POOL_.here())
        u = phases[f"M{l}.merge"].u0 + 3
        with pool.Fori(0, 4) as it:
            for half in range(2):
                if half == 0:
                    pool.wait_ge(gated_done, 20 * l + 3 + 5 * it)
                else:
                    pool.wait_ge(evicted, u + 1 + 4 * it)
                pool.tensor_tensor(gated[:, half, 0, :], gated[:, half, 0, :], gated[:, half, 1, :], ALU.add)\
                    .then_inc(merged_full, 1)
                pool.wait_ge(merged_full, 16 * l + 2 * half + 1 + 4 * it)
                pool.tensor_tensor(gated[:, half, 0, :], gated[:, half, 0, :], gated[:, half, 2, :], ALU.add)\
                    .then_inc(merged_full, 1)

    block = ctx.enter_context(nc.Block())

    @block.sync
    def _(sp):
        sp.dma_start(cvec[:], A["cvec"]).then_inc(inputs_loaded, 16)
        sp.dma_start(v1[:], A["vec1"]).then_inc(inputs_loaded, 16)
        sp.dma_start(k1[:], A["const1"]).then_inc(inputs_loaded, 16)
        sp.dma_start(sinks[:], A["wa_sinks"]).then_inc(inputs_loaded, 16)
        sp.dma_start(h[:], A["x"]).then_inc(inputs_loaded, 16)
        for name, ph in phases.items():
            if name in ("M0.z", "M1.z"):
                out, l = phases[name.replace("z", "ffn0.out0")], int(name[1])
                sweep_loads(sp, ph)
                sp.wait_ge(evicted, out.u0 + out.n)
                sp.dma_start(w_q[:], A["mla_wq_up"][l]).then_inc(mla_loaded, 16)
                sp.dma_start(w_kv[:], A["mla_wkv_up"][l]).then_inc(mla_loaded, 16)
                continue
            sweep_loads(sp, ph)
        sp.wait_ge(evicted, n_units)
        sp.dma_start(A["out"], h[:, :, 0:S]).then_inc(stored, 16)
        sp.wait_ge(stored, 16)

    @block.tensor
    def _(pe):
        mod_pe(pe)
        block1_ffn("pe", pe, "L0.ffn0", 0, T2)
        qkv_pe(pe, "L0", 1, T2)
        qkv_done(pe, "L0")
        attention_pe(pe, "L0", na_tiles())
        out_pe(pe, "L0.wo", T2, uhi, ulo, lambda k: DVE_.at("L0", "out", k))
        means_pe(pe, 2, T2, True)
        block1_ffn("pe", pe, "L0.ffn1", 2, T2)
        block1_ffn("pe", pe, "L1.ffn0", 3, T2)
        qkv_pe(pe, "L1", 4, S)
        qkv_done(pe, "L1")
        wa_rope_pe(pe)
        attention_pe(pe, "L1", wa_tiles())
        out_pe(pe, "L1.wo", S, uhi, ulo, lambda k: DVE_.at("L1", "out", k))
        means_pe(pe, 5, S, True)
        block1_ffn("pe", pe, "L1.ffn1", 5, S)
        for l in range(2):
            s = 7 + 3 * l
            means_pe(pe, s, S, False)
            ffn_in_pe(pe, f"M{l}.ffn0.in0", s, S, u2hi, u2lo)
            ffn_out_pe(pe, f"M{l}.ffn0.out0", S, NARROW)
            means_pe(pe, s + 1, S, False)
            z_pe(pe, l, s + 1)
            sb_pe(pe, l)
            ml_pe(pe, l)
            mla_pe(pe, l)
            merge_pe(pe, l)
            out_pe(pe, f"M{l}.wo", S, mhi, mlo, lambda k: (merged_lo, 8 * l + k + 1))
            means_pe(pe, s + 2, S, False)
            ffn_in_pe(pe, f"M{l}.ffn1.in0", s + 2, S, u2hi, u2lo)
            ffn_out_pe(pe, f"M{l}.ffn1.out0", S, NARROW)

    @block.scalar
    def _(act):
        mod_act(act)
        act.wait_ge(*DVE_.at("vectors"))
        layer_input_act(act, 0, T2, None, scale1(0), shift1(0), uhi)
        block1_ffn("act", act, "L0.ffn0", 0, T2)
        norm1_act(act, 1, T2)
        qkv_act(act, "L0", T2)
        attention_act(act, "L0", na_tiles(), uhi)
        out_act(act, "L0.wo", 2, T2)
        norm1_act(act, 2, T2)
        block1_ffn("act", act, "L0.ffn1", 2, T2)
        norm1_act(act, 3, T2)
        block1_ffn("act", act, "L1.ffn0", 3, T2)
        norm1_act(act, 4, T2)
        qkv_act(act, "L1", S)
        attention_act(act, "L1", wa_tiles(), uhi)
        out_act(act, "L1.wo", 5, S)
        norm1_act(act, 5, S)
        block1_ffn("act", act, "L1.ffn1", 5, S)
        norm1_act(act, 6, S)
        act.wait_ge(*ACT_.at("h", 6, KC - 1))
        for dst, src in ((k2, "const2"), (v2, "vec2"), (rows2, "rows2"), (positions, "positions")):
            act.dma_start(dst[:], A[src]).then_inc(block2_loaded, 16)
        squares_act(act, 7, S, lambda cc: ACT_.at("h", 6, cc), range(KC))
        for l in range(2):
            s = 7 + 3 * l
            if l == 0:
                act.wait_ge(block2_loaded, 16 * N_BLOCK2)
            norm2_act(act, s, l, "ffn1_norm", u2hi)
            ffn_in_act(act, f"M{l}.ffn0.in0", S, NARROW)
            out_act(act, f"M{l}.ffn0.out0", s + 1, S)
            norm2_act(act, s + 1, l, "mix_norm", u2hi)
            if l == 0:
                rope_tables_act(act)
            z_act(act, l)
            sb_act(act, l)
            ml_act(act, l)
            mla_act(act, l)
            merge_act(act, l)
            out_act(act, f"M{l}.wo", s + 2, S)
            norm2_act(act, s + 2, l, "ffn2_norm", u2hi)
            ffn_in_act(act, f"M{l}.ffn1.in0", S, NARROW)
            out_act(act, f"M{l}.ffn1.out0", *((s + 3, S) if l == 0 else ()))

    @block.vector
    def _(dve):
        mod_dve(dve)
        for cc in range(KC):
            low_dve(dve, 0, T2, cc, uhi, ulo)
        block1_ffn("dve", dve, "L0.ffn0", 0, T2)
        norm1_dve(dve, 1, T2)
        qkv_dve(dve, "L0")
        attention_dve(dve, "L0", na_tiles(), uhi, ulo)
        out_dve(dve, "L0.wo", T2, gate1(1), lambda cc: POOL_.at("h", 1, cc))
        norm1_dve(dve, 2, T2)
        block1_ffn("dve", dve, "L0.ffn1", 2, T2)
        norm1_dve(dve, 3, T2)
        block1_ffn("dve", dve, "L1.ffn0", 3, T2)
        norm1_dve(dve, 4, T2)
        qkv_dve(dve, "L1")
        wa_rope_dve(dve)
        attention_dve(dve, "L1", wa_tiles(), uhi, ulo)
        out_dve(dve, "L1.wo", S, gate1(4), lambda cc: POOL_.at("h", 4, cc))
        norm1_dve(dve, 5, S)
        block1_ffn("dve", dve, "L1.ffn1", 5, S)
        norm1_dve(dve, 6, S)
        for l in range(2):
            s = 7 + 3 * l
            norm2_dve(dve, s, u2hi, u2lo)
            half_gate = lambda cc, kind: 0.5
            ffn_in_dve(dve, f"M{l}.ffn0.in0", S, NARROW)
            out_dve(dve, f"M{l}.ffn0.out0", S, half_gate, None)
            norm2_dve(dve, s + 1, u2hi, u2lo)
            if l == 0:
                rope_tables_dve(dve)
            z_dve(dve, l)
            sb_dve(dve, l)
            ml_dve(dve, l)
            mla_dve(dve, l)
            merge_dve(dve, l)
            out_dve(dve, f"M{l}.wo", S, lambda cc, kind: 1.0, None)
            norm2_dve(dve, s + 2, u2hi, u2lo)
            ffn_in_dve(dve, f"M{l}.ffn1.in0", S, NARROW)
            out_dve(dve, f"M{l}.ffn1.out0", S, half_gate, None)

    @block.gpsimd
    def _(pool):
        residual_pool(pool, 0, T2)
        block1_ffn("pool", pool, "L0.ffn0", 0, T2)
        residual_pool(pool, 1, T2)
        bias_pool(pool)
        sums_pool(pool, 2, T2, last_evicted(phases["L0.wo"]), True)
        residual_pool(pool, 2, T2)
        block1_ffn("pool", pool, "L0.ffn1", 2, T2)
        residual_pool(pool, 3, T2)
        block1_ffn("pool", pool, "L1.ffn0", 3, T2)
        residual_pool(pool, 4, S)
        sums_pool(pool, 5, S, last_evicted(phases["L1.wo"]), True)
        residual_pool(pool, 5, S)
        block1_ffn("pool", pool, "L1.ffn1", 5, S)
        for l in range(2):
            s = 7 + 3 * l
            if l == 0:
                sums_pool(pool, s, S, None, False)
            sums_pool(pool, s + 1, S, None, False)
            mix_pool(pool, l)
            merge_pool(pool, l)
            sums_pool(pool, s + 2, S, None, False)
            if l == 0:
                sums_pool(pool, s + 3, S, None, False)

    ctx.close()


def units(w, chunks=None):
    w = np.asarray(w)
    K, N = w.shape[-2:]
    w = w.reshape(-1, K // P, P, N // 256, 256)
    return np.ascontiguousarray(w.transpose(0, 3, 2, 1, 4)).reshape(-1, P, K // P * 256)


def by_partition(v):
    v = np.asarray(v)
    return v.reshape(-1, P).T


def lay_out(a):
    n = {k: np.asarray(v) for k, v in a.items()}
    c1, c2 = const_arrays()
    out = {"const1": c1, "const2": c2}
    tokens = np.concatenate([n["x"][0], n["ctx"][0]], 0)
    out["x"] = tokens.reshape(T2, KC, P).transpose(2, 1, 0)
    out["cvec"] = np.stack([n["c"][0], n["c_ctx"]], -1).reshape(KC, P, 2).transpose(1, 0, 2)
    out["vec1"] = np.concatenate([by_partition(n[k]) for k in ("b_mod", "ln_g", "ln_b")], 1)
    out["wa_sinks"] = np.broadcast_to(n["wa_sinks"], (P, NH))
    out["w_mod"] = units(n["w_mod"])

    def ffn_in(w, hidden):
        w = w.reshape(-1, D, 2, hidden // P, P).transpose(0, 1, 3, 2, 4).reshape(-1, D, 2 * hidden)
        return units(w)

    def ffn_out(w):
        return units(w.reshape(-1, HALF, D))

    out["ffn_in"], out["ffn_out"] = ffn_in(n["ffn_w_in"], FF), ffn_out(n["ffn_w_out"])
    for j in (1, 2):
        out[f"ffn{j}_in"] = ffn_in(n[f"ffn{j}_wi_2"], FF2)
        out[f"ffn{j}_out"] = ffn_out(n[f"ffn{j}_wo_2"])
    out["na_qkv"], out["na_o"] = units(n["na_w_qkv"]), units(n["na_w_o"])
    heads = [8 * (c // 4) + c % 4 + 4 * side for c in range(KC) for side in range(2)]
    wq = n["wa_w_qkv"][0]
    q = np.concatenate([wq[:, hd * HD:(hd + 1) * HD] for hd in heads], 1)
    out["wa_qkv"] = units(np.concatenate([q, wq[:, D:]], 1))
    out["wa_o"] = units(np.concatenate([n["wa_w_o"][0][hd * HD:(hd + 1) * HD] for hd in heads], 0))
    rpb = np.pad(n["na_rpb"][0], ((0, 0), (0, 0), (GRID_W - NA_KW, GRID_W - NA_KW)))
    rows = []
    for tile in range(2):
        for q_row in (2 * tile, 2 * tile + 1):
            keys = rpb[:, NA_KH - 1 - q_row:NA_KH - 1 - q_row + ROWS]
            rows.append(np.stack([keys[:, :, GRID_W - 1 - qc:2 * GRID_W - 1 - qc] for qc in range(GRID_W)], 1))
    tiles = [np.concatenate(rows[2 * t:2 * t + 2], 1).reshape(NH, P, 1, S) for t in range(2)]
    out["na_rpb"] = np.concatenate(tiles, 2).reshape(NH, P, 2 * S)

    w, b = n["w_in_2"], n["b_in_2"]
    GATES = 3240

    def pack(x):
        i_f, ckv, k_rot = x[..., 2816:2824], x[..., 3080:3208], x[..., 3208:3240]
        last = [ckv, i_f, ckv[..., 0:56], k_rot, ckv[..., 0:32]]
        return np.concatenate([x[..., 0:2816], x[..., 2824:3080], *last], -1)

    out["w_in"] = units(pack(w))
    merge = []
    gates = w[..., GATES:].reshape(2, D, 3, 4, 256)
    ups = np.concatenate([n["w_up_sb_2"], n["w_up_ml_2"], n["w_up_mla_2"]], 1).reshape(2, D, 4, 256)
    for l in range(2):
        for j in range(4):
            merge += [gates[l, :, br, j] for br in range(3)] + [ups[l, :, j]]
    out["w_merge"] = units(np.stack(merge))
    out["w_out"] = units(n["w_out_2"])
    packed = pack(b)
    conv_w = n["ml_conv_w_2"]
    vec = []
    for l in range(2):
        pad = np.zeros(P, np.float32)
        q_gain, k_gain = (np.concatenate([n[k][l], pad[QK:]]) for k in ("mla_q_gain_2", "mla_k_gain_2"))
        parts = [n["ffn1_norm_2"][l], n["mix_norm_2"][l], n["ffn2_norm_2"][l], packed[l, 0:256], packed[l, 256:512],
                 packed[l, 768:1792], packed[l, 2304:2816], packed[l, 2816:3072], packed[l, 3072:3200],
                 packed[l, 3200:3328], b[l, GATES:], conv_w[l].reshape(-1), n["ml_conv_b_2"][l],
                 n["ml_out_norm_2"][l], n["mla_q_norm_2"][l], n["mla_kv_norm_2"][l], q_gain, k_gain]
        vec.append(np.concatenate([by_partition(x) for x in parts], 1))
    out["vec2"] = np.stack(vec, 1)
    row = np.concatenate([b[:, 512:768], b[:, 1792:2304], b[:, 2816:2824]], 1)
    out["rows2"] = np.broadcast_to(row, (P, 2, N_ROW2))
    out["positions"] = np.broadcast_to(n["positions_2"], (QK, S))
    out["mla_wq_up"] = n["mla_wq_up_2"].reshape(2, 2, P, 384).transpose(0, 2, 1, 3)
    out["mla_wkv_up"] = n["mla_wkv_up_2"]
    return {k: np.ascontiguousarray(v) for k, v in out.items()}


def kernel(**inputs):
    import concourse.bacc as bacc
    from concourse.bass_utils import run_bass_kernel_spmd

    laid = lay_out(inputs)
    book = {}
    for _ in range(2):
        nc = bacc.Bacc("TRN2", target_bir_lowering=False, num_devices=1)
        A, arrays = {}, {}
        for name, a in laid.items():
            arrays[f"in_{name}"] = a
            A[name] = nc.dram_tensor(f"in_{name}", a.shape, mybir.dt.from_np(a.dtype), kind="ExternalInput").ap()
        A["out"] = nc.dram_tensor("out", (P, KC, S), F32, kind="ExternalOutput").ap()
        book.pop("missing", None)
        build(nc, A, book)
    assert not book.get("missing"), book["missing"]
    result = run_bass_kernel_spmd(nc, [arrays], core_ids=[0]).results[0]["out"]
    return np.asarray(result).transpose(2, 1, 0).reshape(1, S, D)
```

```python
from contextlib import ExitStack

import numpy as np
import concourse.bass as bass
from concourse import mybir

P = 128
D = 1024
KC = D // P
S = 256
T2 = 2 * S
FF = 2816
HALF = FF // 2
FC = HALF // P
FF2 = 1408
NH = 16
HD = 64
GRID_W = 64
ROWS = S // GRID_W
NA_KH, NA_KW = 8, 16
WA_KV = 4
WINDOW = 128
N_MOD = 9
MOD_CHUNKS = 2 * N_MOD * KC
START_CHUNKS = 2 * KC
ALPHA = 4 ** 0.25
ML_H, SB_H, MLA_H = 4, 4, 4
QK = 96
NEG = -1e30
LN_EPS, RMS_EPS = 1e-5, 1e-6

F32 = mybir.dt.float32
F32R = mybir.dt.float32r
I32 = mybir.dt.int32
ALU = mybir.AluOpType
ACT = mybir.ActivationFunctionType
AX = mybir.AxisListType


class Tally:

    def __init__(self, sem, name, book):
        self.sem, self.name, self.book, self.n = sem, name, book, 0

    def up(self, label=None):
        self.n += 1
        if label is not None:
            self.book[(self.name, label)] = self.n
        return self.sem, 1

    def here(self):
        return self.sem, self.n

    def at(self, *label):
        label = label[0] if len(label) == 1 else label
        if (self.name, label) not in self.book:
            self.book.setdefault("missing", set()).add((self.name, label))
        return self.sem, self.book.get((self.name, label), 1)


def columns(*widths):
    at, out = 0, {}
    for name, n in widths:
        out[name] = (at, n)
        at += n
    return out, at


CONST1, N_CONST1 = columns(("ident", P), ("mean1024", P), ("na_mask", GRID_W), ("rope_perm", P),
                           ("one", 1), ("ln_eps", 1), ("rms_eps", 1))
CONSTW, N_CONSTW = columns(("wa_mask", 2 * S), ("rope_cos", S), ("rope_sin", S))
CONST2, N_CONST2 = columns(("ones", P), ("mean256", P), ("mean128", P), ("mean96", P), ("tri_strict", P),
                           ("tri_incl", P), ("causal", 2 * S), ("causal_t", P), ("sb_mask", 384),
                           ("mla_perm", P), ("inv_freq", 1), ("half_pi", 1))
VEC1, N_VEC1 = columns(("b_mod", 2 * N_MOD * KC), ("ln_g", 6 * KC), ("ln_b", 6 * KC))
VEC2, N_VEC2 = columns(("ffn1_norm", KC), ("mix_norm", KC), ("ffn2_norm", KC), ("b_sbq", 2), ("b_sbk", 2),
                       ("b_mlqk", 8), ("b_mlo", 4), ("b_cq", 2), ("b_ckv", 1), ("b_kr", 1), ("b_gates", 24),
                       ("conv_w", 32), ("conv_b", 8), ("ml_gain", 4), ("q_norm", 2), ("kv_norm", 1),
                       ("q_gain", 1), ("k_gain", 1))
ROW2, N_ROW2 = columns(("b_sbv", 256), ("b_mlv", 512), ("b_if", 8))


def const_arrays():
    c1 = np.zeros((P, N_CONST1), np.float32)
    cw = np.zeros((P, N_CONSTW), np.float32)
    c2 = np.zeros((P, N_CONST2), np.float32)

    def put(c, cols, name, value):
        at, n = cols[name]
        value = np.asarray(value, np.float32)
        c[:value.shape[0], at:at + value.shape[1]] = value

    i = np.arange(P)
    put(c1, CONST1, "ident", np.eye(P))
    put(c1, CONST1, "mean1024", np.full((P, P), 1 / 1024))
    qc, kc = np.arange(P) % GRID_W, np.arange(GRID_W)
    start = np.clip(qc - NA_KW // 2, 0, GRID_W - NA_KW)[:, None]
    put(c1, CONST1, "na_mask", np.where((kc >= start) & (kc < start + NA_KW), 0, NEG))
    q, k = np.arange(S).reshape(2, P), np.arange(S)
    near = np.abs(q[:, :, None] - k) <= WINDOW
    put(cw, CONSTW, "wa_mask", np.where(near, 0, NEG).transpose(1, 0, 2).reshape(P, 2 * S))
    perm = np.zeros((P, P))
    for f in range(P):
        j = f % 32
        perm[f + 16 if j < 16 else f - 16, f] = -1 if j < 16 else 1
    put(c1, CONST1, "rope_perm", perm)
    inv = (np.float32(10000.0) ** (-np.arange(16, dtype=np.float32) / np.float32(16))).astype(np.float32)
    t = np.arange(S)
    pos = np.where((i % HD < 32)[:, None], t // GRID_W, t % GRID_W).astype(np.float32)
    ang = pos * inv[i % 16][:, None]
    put(cw, CONSTW, "rope_cos", np.cos(ang))
    put(cw, CONSTW, "rope_sin", np.sin(ang))
    put(c1, CONST1, "one", np.ones((P, 1)))
    put(c1, CONST1, "ln_eps", np.full((P, 1), LN_EPS))
    put(c1, CONST1, "rms_eps", np.full((P, 1), RMS_EPS))
    put(c2, CONST2, "ones", np.ones((P, P)))
    put(c2, CONST2, "mean256", np.full((P, P), 1 / 256))
    put(c2, CONST2, "mean128", np.full((P, P), 1 / 128))
    put(c2, CONST2, "mean96", np.full((QK, QK), 1 / QK))
    put(c2, CONST2, "tri_strict", i[:, None] > i[None])
    put(c2, CONST2, "tri_incl", i[:, None] <= i[None])
    put(c2, CONST2, "causal", np.where(k <= q[:, :, None], 0, NEG).transpose(1, 0, 2).reshape(P, 2 * S))
    put(c2, CONST2, "causal_t", np.where(i[:, None] <= i[None], 0, NEG))
    strict = i[:, None] < i[None]
    put(c2, CONST2, "sb_mask", np.concatenate([strict, np.ones((P, P)), strict], 1))
    perm = np.zeros((QK, QK))
    for f in range(HD, QK):
        j = f - HD
        perm[f + 16 if j < 16 else f - 16, f] = -1 if j < 16 else 1
    put(c2, CONST2, "mla_perm", perm)
    freq = np.zeros((QK, 1), np.float32)
    freq[HD:, 0] = inv[np.arange(32) % 16]
    put(c2, CONST2, "inv_freq", freq)
    put(c2, CONST2, "half_pi", np.full((P, 1), np.pi / 2))
    return c1, cw, c2


class Phase:

    def __init__(self, array, index, n, kc):
        self.array, self.index, self.n, self.kc = array, index, n, kc
        self.size = kc * 256


def plan():
    phases = {}

    def ffn(name, arrays, at, halves):
        for half in range(halves):
            n = at * halves + half
            phases[f"{name}.in{half}"] = Phase(arrays[0], n * FC, FC, KC)
            phases[f"{name}.out{half}"] = Phase(arrays[1], n * 4, 4, FC)

    ffn("L0.ffn0", ("ffn_in", "ffn_out"), 0, 2)
    for j, what in enumerate("qkv"):
        phases[f"L0.{what}"] = Phase("na_qkv", 4 * j, 4, KC)
    phases["L0.wo"] = Phase("na_o", 0, 4, KC)
    ffn("L0.ffn1", ("ffn_in", "ffn_out"), 1, 2)
    ffn("L1.ffn0", ("ffn_in", "ffn_out"), 2, 2)
    phases["L1.q"] = Phase("wa_qkv", 0, 4, KC)
    phases["L1.k"] = Phase("wa_qkv", 4, 1, KC)
    phases["L1.v"] = Phase("wa_qkv", 5, 1, KC)
    phases["L1.wo"] = Phase("wa_o", 0, 4, KC)
    ffn("L1.ffn1", ("ffn_in", "ffn_out"), 3, 2)
    for l in range(2):
        ffn(f"M{l}.ffn0", ("ffn1_in", "ffn1_out"), l, 1)
        phases[f"M{l}.z"] = Phase("w_in", 13 * l, 13, KC)
        phases[f"M{l}.merge"] = Phase("w_merge", 16 * l, 16, KC)
        phases[f"M{l}.wo"] = Phase("w_out", 4 * l, 4, KC)
        ffn(f"M{l}.ffn1", ("ffn2_in", "ffn2_out"), l, 1)
    u = 0
    for ph in phases.values():
        ph.u0 = u
        u += ph.n
    return phases


def build(nc, A, book):
    phases = plan()
    unit_size = [ph.size for ph in phases.values() for _ in range(ph.n)]
    n_units = len(unit_size)
    ctx, block1, start_mem, ffn1_mem, att_mem, block2, ffn2_mem, mix_mem, merge_mem = (ExitStack() for _ in range(9))

    def sb(name, shape, dt=F32, scope=ctx):
        return scope.enter_context(nc.sbuf_tensor(name, shape, dt))

    def sem(name):
        return ctx.enter_context(nc.semaphore(name))

    def tally(name):
        return Tally(sem(name), name, book)

    banks = ctx.enter_context(nc.psum_tensor("banks", [P, 8, 512], F32))
    raw = [sb(f"raw{i}", [P, FC * 256]) for i in range(2)]
    whi = [sb(f"whi{i}", [P, FC * 256], F32R) for i in range(2)]
    wlo = [sb(f"wlo{i}", [P, FC * 256], F32R) for i in range(2)]
    h = sb("h", [P, KC, T2])
    squares = sb("squares", [P, 2, T2])
    sums = sb("sums", [P, 2, T2])
    scaled = sb("scaled", [P, 2, T2])
    full_u = sb("full_u", [P, 2, T2])
    rstd = sb("rstd", [P, T2])
    var = sums[:, 0]
    k1 = sb("k1", [P, N_CONST1])
    small = sb("small", [P, 160])
    v1 = sb("v1", [P, N_VEC1], scope=block1)
    mods = sb("mods", [P, 2, N_MOD * KC, 2], scope=block1)
    crow = sb("crow", [P, 2, D], scope=block1)
    mod_slot = sb("mod_slot", [P, 2, D], scope=block1)
    sinks = sb("sinks", [P, NH], scope=block1)
    vS1 = sb("vS1", [P, 7, KC, 2], scope=block1)
    vS0 = sb("vS0", [P, 7, KC, 2], scope=block1)
    vG = sb("vG", [P, 6, KC, 2], scope=block1)
    gA = sb("gA", [P, 6, KC], scope=block1)
    bA = sb("bA", [P, 6, KC], scope=block1)
    uhi = sb("uhi", [P, KC, T2], F32R, scope=block1)
    ulo = sb("ulo", [P, KC, T2], F32R, scope=block1)
    mod_start = sb("mod_start", [P, START_CHUNKS // 2, D], scope=start_mem)
    start_mem.close()
    fhi = sb("fhi", [P, FC, T2], F32R, scope=ffn1_mem)
    flo = sb("flo", [P, FC, T2], F32R, scope=ffn1_mem)
    ffn1_mem.close()
    qT = sb("qT", [P, KC, T2], scope=att_mem)
    kT = sb("kT", [P, KC, T2], scope=att_mem)
    vv = sb("vv", [P, 4, D], scope=att_mem)
    att_mem.close()
    block1.close()
    u2hi = sb("u2hi", [P, KC, S], F32R, scope=block2)
    u2lo = sb("u2lo", [P, KC, S], F32R, scope=block2)
    yhi = sb("yhi", [P, KC, S], F32R, scope=block2)
    ylo = sb("ylo", [P, KC, S], F32R, scope=block2)
    k2 = sb("k2", [P, N_CONST2], scope=block2)
    v2 = sb("v2", [P, 2, N_VEC2], scope=block2)
    rows2 = sb("rows2", [P, 2, N_ROW2], scope=block2)
    positions = sb("positions", [QK, S], I32, scope=block2)
    rope_c = sb("rope_c", [QK, S], scope=block2)
    rope_s = sb("rope_s", [QK, S], scope=block2)
    f2hi = sb("f2hi", [P, FC, S], F32R, scope=ffn2_mem)
    f2lo = sb("f2lo", [P, FC, S], F32R, scope=ffn2_mem)
    silu_a2 = sb("silu_a2", [P, 2, S], scope=ffn2_mem)
    hidden2 = sb("hidden2", [P, 2, S], scope=ffn2_mem)
    ffn2_mem.close()
    w_q = sb("w_q", [P, 2, 384], scope=mix_mem)
    w_kv = sb("w_kv", [P, 512], scope=mix_mem)
    sbq = sb("sbq", [P, 2, S], scope=mix_mem)
    sbk = sb("sbk", [P, 2, S], scope=mix_mem)
    sbv = sb("sbv", [P, 2, 256], scope=mix_mem)
    conv_in = sb("conv_in", [P, KC, S + 3], scope=mix_mem)
    mlv = sb("mlv", [P, 2, 512], scope=mix_mem)
    osig = sb("osig", [P, 4, S], scope=mix_mem)
    cq = sb("cq", [P, 3, S], scope=mix_mem)
    kr = sb("kr", [P, S], scope=mix_mem)
    iff = sb("iff", [P, 2, 8], scope=mix_mem)
    qk = sb("qk", [P, 8, S], scope=mix_mem)
    mla_v = sb("mla_v", [P, 2, 256], scope=mix_mem)
    mix_mem.close()
    gate = sb("gate", [P, 6, S], scope=merge_mem)
    gated = sb("gated", [P, 2, 3, S], scope=merge_mem)
    mhi = sb("mhi", [P, KC, S], F32R, scope=merge_mem)
    mlo = sb("mlo", [P, KC, S], F32R, scope=merge_mem)
    merge_mem.close()
    block2.close()
    mlqk = h[:, :, S:T2]
    def probs(n):
        return (scaled, sums)[n // 2 % 2][:, n % 2]

    probs_t = full_u
    silu_a, hidden = scaled, full_u
    na_bias = squares
    window_tables = mod_slot[:, 0]
    assert N_CONSTW == D

    def c(name):
        table, cols = next((t, n) for t, n in ((k1, CONST1), (window_tables, CONSTW), (k2, CONST2)) if name in n)
        at, n = cols[name]
        return table[:, at:at + n]

    def vec2(l, name, k=0, n=1):
        at = VEC2[name][0] + k
        return v2[:, l, at:at + n]

    ident = c("ident")

    landed = [sem("weights_landed_0"), sem("weights_landed_1")]
    hi_done = sem("weights_hi_done")
    lo_done = sem("weights_lo_done")
    product = sem("product_done")
    evicted = sem("product_evicted")
    mod_landed = [sem("modulation_weights_landed_0"), sem("modulation_weights_landed_1")]
    start_landed = [sem(f"start_modulation_weights_landed_{i}") for i in range(START_CHUNKS // 2)]
    mod_done = sem("modulation_products_done")
    window_loaded = sem("window_tables_loaded")
    crow_loaded = sem("modulation_inputs_loaded")
    inputs_loaded = sem("inputs_loaded")
    block2_loaded = sem("block2_inputs_loaded")
    mla_loaded = sem("mla_weights_loaded")
    bias_loaded = [sem("na_bias_loaded_0"), sem("na_bias_loaded_1")]
    stored = sem("output_stored")
    f_silu, f_hi, f_split = sem("ffn_silu_done"), sem("ffn_hidden_hi_done"), sem("ffn_hidden_split_done")
    PE_, ACT_, DVE_, POOL_ = tally("pe_step"), tally("act_step"), tally("dve_step"), tally("pool_step")
    N_INPUTS, N_BLOCK2 = 4, 4

    def plus(x, k, it):
        return x if it is None else x + k * it

    def load(sp, ph, i, u, it):
        if u >= 2:
            sp.wait_ge(lo_done, plus(u - 1, 2, it))
        sp.dma_start(raw[u % 2][:, 0:ph.size], A[ph.array][ph.index + i]).then_inc(landed[u % 2], 16)

    def sweep_loads(sp, ph):
        sweep(sp, ph, lambda u, i, it: load(sp, ph, i, u, it))

    after_norm = [ph for name, ph in phases.items() if name.endswith((".in0", ".q", ".z"))]
    split_early = {ph.u0 + 1 for ph in after_norm}

    def split_hi(act, u, it=None, early=False):
        if u >= n_units or (it is None and u in split_early and not early):
            return
        act.wait_ge(landed[u % 2], plus(16 * (u // 2 + 1), 16, it))
        if u >= 2:
            act.wait_ge(product, plus(2 * (u - 1), 4, it))
        act.copy(whi[u % 2][:, 0:unit_size[u]], raw[u % 2][:, 0:unit_size[u]]).then_inc(hi_done, 1)

    def split_lo(dve, u, it=None, early=False):
        if u >= n_units or (it is None and u in split_early and not early):
            return
        n = unit_size[u]
        dve.wait_ge(hi_done, plus(u + 1, 2, it))
        dve.tensor_tensor(wlo[u % 2][:, 0:n], raw[u % 2][:, 0:n], whi[u % 2][:, 0:n].bitcast(F32),
                          ALU.subtract).then_inc(lo_done, 1)

    def sweep(e, ph, one):
        first = min(2, ph.n)
        for i in range(first):
            one(ph.u0 + i, i, None)
        pairs = (ph.n - first - 1) // 2 if ph.n >= 8 else 0
        if pairs:
            with e.Fori(0, pairs) as it:
                for j in range(2):
                    one(ph.u0 + first + j, 2 * it + (first + j), it)
        for i in range(first + 2 * pairs, ph.n):
            one(ph.u0 + i, i, None)

    def start_unit(pe, u, it=None, per=2):
        pe.wait_ge(lo_done, plus(u + 1, per, it))
        if u >= 2:
            pe.wait_ge(evicted, plus(u - 1, per, it))

    def bank(u, half):
        return 2 * (u % 2) + half

    def cols(t, u, k, a, b):
        return t[u % 2][:, k * 256 + a:k * 256 + b]

    def feature_major(pe, u, half, chunks, x_hi, x_lo, T, out=None, arrived=None):
        out = banks[:, bank(u, half), 0:T] if out is None else out
        for n, k in enumerate(chunks):
            if arrived is not None:
                pe.wait_ge(*arrived(k))
            w_hi, w_lo = cols(whi, u, k, half * P, half * P + P), cols(wlo, u, k, half * P, half * P + P)
            pe.matmul(out, w_hi, x_hi[:, k, 0:T], start=(n == 0), stop=False)
            pe.matmul(out, w_hi, x_lo[:, k, 0:T], start=False, stop=False)
            mm = pe.matmul(out, w_lo, x_hi[:, k, 0:T], start=False, stop=(n == len(chunks) - 1))
        return mm

    def first_unit(pe, ph, s, x_hi, x_lo, T):
        u = ph.u0
        start_unit(pe, u)
        for k in range(KC):
            pe.wait_ge(*DVE_.at("u", s, k))
            for v in (u,):
                for half in range(2):
                    out = banks[:, bank(v, half), 0:T]
                    w_hi, w_lo = (cols(t, v, k, half * P, half * P + P) for t in (whi, wlo))
                    pe.matmul(out, w_hi, x_hi[:, k, 0:T], start=(k == 0), stop=False)
                    pe.matmul(out, w_hi, x_lo[:, k, 0:T], start=False, stop=False)
                    mm = pe.matmul(out, w_lo, x_hi[:, k, 0:T], start=False, stop=(k == KC - 1))
                    if k == KC - 1:
                        mm.then_inc(product, 1)

    def token_major(pe, u, out, tile, a, b, x_hi, x_lo):
        ts = slice(tile * P, tile * P + P)
        for k in range(KC):
            pe.matmul(out, x_hi[:, k, ts], cols(whi, u, k, a, b), start=(k == 0), stop=False)
            pe.matmul(out, x_hi[:, k, ts], cols(wlo, u, k, a, b), start=False, stop=False)
            mm = pe.matmul(out, x_lo[:, k, ts], cols(whi, u, k, a, b), start=False, stop=(k == KC - 1))
        return mm

    MOD_FIRST = {"L0.ffn0.in0": 16, "L0.ffn0.in1": 32, "L0.q": 48, "L0.k": 56, "L0.v": 64, "L0.ffn1.in0": 72,
                 "L0.ffn1.in1": 88, "L1.ffn0.in0": 104, "L1.ffn0.out0": 120, "L1.ffn0.in1": 128}

    def mod_load(pool, n, it=None):
        if n >= START_CHUNKS + 2:
            pool.wait_ge(mod_done, plus(2 * (n - 1), 4, it))
        pool.dma_start(mod_slot[:, n % 2], A["w_mod"][plus(n, 2, it)]).then_inc(mod_landed[n % 2], 16)

    def mod_loads(pool, name):
        first = MOD_FIRST[name]
        count = 2 * KC if ".in" in name else KC
        if first == START_CHUNKS:
            for n in range(first, first + 2):
                mod_load(pool, n)
            first, count = first + 2, count - 2
        with pool.Fori(0, count // 2) as it:
            for j in range(2):
                mod_load(pool, first + j, it)

    def mod_products(dve, n, it=None, source=None, ready=None):
        source = mod_slot[:, n % 2] if source is None else source
        ready = (mod_landed[n % 2], plus(16 * ((n - START_CHUNKS) // 2 + 1), 32, it)) if ready is None else ready
        dve.wait_ge(*ready)
        flat_mods = mods[:].rearrange("p l m v -> p (l m v)")
        junk = squares[:].rearrange("p a b -> p (a b)")
        for v in range(2):
            if n or v:
                dve.wait_ge(mod_done, plus(2 * n + v, 8, it))
            dve.scalar_tensor_tensor(junk, source, 1.0, crow[:, v], ALU.mult, ALU.mult,
                                     accum_out=flat_mods[:, bass.ds(2 * n + v + 8 * it, 1)] if it is not None
                                     else flat_mods[:, 2 * n + v:2 * n + v + 1]).then_inc(mod_done, 1)

    def start_load(pool, n):
        half = START_CHUNKS // 2
        if n >= half:
            pool.wait_ge(mod_done, 2 * (n - half + 1))
        pool.dma_start(mod_start[:, n % half], A["w_mod"][n]).then_inc(start_landed[n % half], 16)

    def mod_start_dve(dve):
        dve.wait_ge(*ACT_.at("c silu"))
        half = START_CHUNKS // 2
        for n in range(START_CHUNKS):
            mod_products(dve, n, None, mod_start[:, n % half], (start_landed[n % half], 16 * (n // half + 1)))
        dve.wait_ge(inputs_loaded, 16 * N_INPUTS)
        ag, ab = VEC1["ln_g"][0], VEC1["ln_b"][0]
        dve.tensor_scalar(gA[:].rearrange("p s k -> p (s k)"), v1[:, ag:ag + 6 * KC], ALPHA, None, ALU.mult)\
            .then_inc(*DVE_.up())
        dve.tensor_scalar(bA[:].rearrange("p s k -> p (s k)"), v1[:, ab:ab + 6 * KC], ALPHA, None, ALU.mult)\
            .then_inc(*DVE_.up())
        vectors_dve(dve, (0, 1), "in", 0)

    def vectors_dve(dve, chunks, *parts):
        ag, ab = VEC1["ln_g"][0], VEC1["ln_b"][0]
        first, last = chunks[0] * KC, (chunks[-1] + 1) * KC
        mv = mods[:].rearrange("p l m v -> p (l m) v")[:, first:last]
        at = VEC1["b_mod"][0]
        bias = v1[:, at + first:at + last].rearrange("p (m o) -> p m o", o=1)
        dve.wait_ge(mod_done, 2 * last)
        for v in range(2):
            dve.tensor_tensor(mv[:, :, v:v + 1], mv[:, :, v:v + 1], bias, ALU.add).then_inc(*DVE_.up())
        dve.wait_ge(*DVE_.here())
        for what, s in zip(parts[0::2], parts[1::2]):
            l, j = s // 3, s % 3
            for v in range(2):
                s1, s0 = vS1[:, s, :, v], vS0[:, s, :, v]
                g, b = (v1[:, a + KC * (s - 1):a + KC * s] for a in (ag, ab)) if s else (None, None)
                if s == 6:
                    dve.tensor_copy(s1, g).then_inc(*DVE_.up())
                    dve.tensor_copy(s0, b).then_inc(*DVE_.up())
                    continue
                shift, scale, gated_by = (mods[:, l, (3 * j + m) * KC:(3 * j + m + 1) * KC, v] for m in range(3))
                if what == "gate":
                    dve.tensor_scalar(vG[:, s, :, v], gated_by, 1.0 if j == 1 else 0.5, None, ALU.mult)\
                        .then_inc(*DVE_.up())
                    continue
                dve.tensor_scalar(s1, scale, 1.0, None, ALU.add).then_inc(*DVE_.up())
                dve.wait_ge(*DVE_.here())
                if s == 0:
                    dve.tensor_copy(s0, shift).then_inc(*DVE_.up(("shift", v)))
                    continue
                dve.tensor_tensor(s0, b, s1, ALU.mult).then_inc(*DVE_.up())
                dve.wait_ge(*DVE_.here())
                dve.tensor_tensor(s0, s0, shift, ALU.add).then_inc(*DVE_.up())
                dve.tensor_tensor(s1, s1, g, ALU.mult).then_inc(*DVE_.up())
        dve.wait_ge(*DVE_.here())

    VECTORS_AFTER = {
        "L0.ffn0.in0": ((2, 3), ("gate", 0)), "L0.ffn0.in1": ((4, 5), ("in", 1, "gate", 1)),
        "L0.v": ((6, 7, 8), ("in", 2, "gate", 2)), "L0.ffn1.in0": ((9, 10), ("in", 3)),
        "L0.ffn1.in1": ((11, 12), ("gate", 3)), "L1.ffn0.in0": ((13, 14), ("in", 4, "gate", 4)),
        "L1.ffn0.in1": ((15, 16, 17), ("in", 5, "gate", 5, "in", 6))}

    def vectors_after(dve, name):
        if name in VECTORS_AFTER:
            chunks, parts = VECTORS_AFTER[name]
            vectors_dve(dve, chunks, *parts)

    def start_act(act):
        act.wait_ge(crow_loaded, 16)
        act.activation(crow[:], crow[:], ACT.Silu).then_inc(*ACT_.up("c silu"))
        split_hi(act, 0)
        split_hi(act, 1, early=True)

    def kinds(T):
        return ((0, 0, S), (1, S, T2)) if T == T2 else ((0, 0, S),)

    def squares_act(act, s, T, source, ccs):
        for cc in ccs:
            act.wait_ge(*source(cc))
            if cc >= 2:
                act.wait_ge(*POOL_.at("sq sum", s, cc - 2))
            act.activation(squares[:, cc % 2, 0:T], h[:, cc, 0:T], ACT.Square).then_inc(*ACT_.up(("sq", s, cc)))

    def sums_pool(pool, s, T, source, mean):
        for cc in range(KC - 2):
            if mean:
                pool.wait_ge(*source(cc))
                if cc == 0:
                    pool.tensor_copy(sums[:, 0, 0:T], h[:, 0, 0:T]).then_inc(*POOL_.up(("sum", s, cc)))
                else:
                    pool.wait_ge(*POOL_.at("sum", s, cc - 1))
                    pool.tensor_tensor(sums[:, 0, 0:T], sums[:, 0, 0:T], h[:, cc, 0:T], ALU.add)\
                        .then_inc(*POOL_.up(("sum", s, cc)))
            pool.wait_ge(*ACT_.at("sq", s, cc))
            if cc == 0:
                pool.tensor_copy(sums[:, 1, 0:T], squares[:, 0, 0:T]).then_inc(*POOL_.up(("sq sum", s, cc)))
            else:
                pool.wait_ge(*POOL_.at("sq sum", s, cc - 1))
                pool.tensor_tensor(sums[:, 1, 0:T], sums[:, 1, 0:T], squares[:, cc % 2, 0:T], ALU.add)\
                    .then_inc(*POOL_.up(("sq sum", s, cc)))

    def means_pe(pe, s, T, source):
        def means(bank_, parts):
            for n, (ready, x) in enumerate(parts):
                pe.wait_ge(*ready)
                mm = pe.matmul(banks[:, bank_, 0:T], c("mean1024"), x, start=(n == 0), stop=(n == len(parts) - 1))
            return mm
        last = (KC - 2, KC - 1)
        if source is not None:
            means(4, [(POOL_.at("sum", s, KC - 3), sums[:, 0, 0:T])] + [(source(cc), h[:, cc, 0:T]) for cc in last])
        means(5, [(POOL_.at("sq sum", s, KC - 3), sums[:, 1, 0:T])]
              + [(ACT_.at("sq", s, cc), squares[:, cc % 2, 0:T]) for cc in last]).then_inc(*PE_.up(("means", s)))

    TAKES = {s: ph for s, ph in zip([x for x in range(6)] + list(range(7, 13)), after_norm)}

    def rstd_act(act, s, T, mean):
        if s in TAKES:
            split_hi(act, TAKES[s].u0 + 1, early=True)
        act.wait_ge(*PE_.at("means", s))
        if mean:
            act.activation(var[:, 0:T], banks[:, 4, 0:T], ACT.Square).then_inc(*ACT_.up(("mean2", s)))
            act.wait_ge(*DVE_.at("var", s))
            act.activation(var[:, 0:T], var[:, 0:T], ACT.Ln, bias=c("ln_eps")).then_inc(*ACT_.up())
        else:
            act.activation(var[:, 0:T], banks[:, 5, 0:T], ACT.Ln, bias=c("rms_eps")).then_inc(*ACT_.up())
        act.wait_ge(*ACT_.here())
        act.activation(rstd[:, 0:T], var[:, 0:T], ACT.Exp, scale=-0.5).then_inc(*ACT_.up(("rstd", s)))

    def centre_dve(dve, s, T):
        dve.wait_ge(*ACT_.at("mean2", s))
        dve.tensor_tensor(var[:, 0:T], banks[:, 5, 0:T], var[:, 0:T], ALU.subtract).then_inc(*DVE_.up())
        dve.wait_ge(*DVE_.here())
        dve.tensor_scalar(var[:, 0:T], var[:, 0:T], 0.0, None, ALU.max).then_inc(*DVE_.up(("var", s)))
        for cc in range(KC // 2):
            centre_chunk(dve, s, T, cc)

    def centre_chunk(dve, s, T, cc):
        dve.tensor_tensor(h[:, cc, 0:T], h[:, cc, 0:T], banks[:, 4, 0:T], ALU.subtract)\
            .then_inc(*DVE_.up(("centred", s, cc)))

    def layer_input_act(act, s, T, ready, scale, shift, x_hi, src=None):
        for cc in range(KC):
            if ready is not None:
                act.wait_ge(*ready(cc))
            x = h[:, cc] if src is None else src[:, cc % 2]
            for kind, a, b in kinds(T):
                args = dict(scale=scale(cc, kind)) | ({} if shift is None else dict(bias=shift(cc, kind)))
                act.activation(x_hi[:, cc, a:b], x[:, a:b], ACT.Identity, **args)\
                    .then_inc(*ACT_.up(("u hi", s, cc)))

    def full_pool(pool, s, T, ready, scale, shift, src=None):
        for cc in range(KC):
            pool.wait_ge(*ready(cc))
            if cc >= 2:
                pool.wait_ge(*DVE_.at("u", s, cc - 2))
            x = h[:, cc] if src is None else src[:, cc % 2]
            for kind, a, b in kinds(T):
                if shift is None:
                    ins = pool.tensor_scalar(full_u[:, cc % 2, a:b], x[:, a:b], scale(cc, kind), None, ALU.mult)
                else:
                    ins = pool.tensor_scalar(full_u[:, cc % 2, a:b], x[:, a:b], scale(cc, kind), shift(cc, kind),
                                             ALU.mult, ALU.add)
            ins.then_inc(*POOL_.up(("full", s, cc)))

    def full1_pool(pool, s, T, T_residual=None):
        ready = (lambda cc: DVE_.at("shift", 1)) if s == 0 else (lambda cc: DVE_.at("n", s, cc))
        full_pool(pool, s, T, ready, scale1(s), shift1(s))
        residual_pool(pool, s, T_residual or T)

    def full2_pool(pool, s, l, name):
        if l == 0:
            pool.wait_ge(block2_loaded, 16 * N_BLOCK2)
        full_pool(pool, s, S, lambda cc: DVE_.at("n", s, cc), lambda cc, kind: vec2(l, name, cc), None, src=scaled)

    def low_dve(dve, s, T, cc, x_hi, x_lo):
        dve.wait_ge(*ACT_.at("u hi", s, cc))
        dve.wait_ge(*POOL_.at("full", s, cc))
        dve.tensor_tensor(x_lo[:, cc, 0:T], full_u[:, cc % 2, 0:T], x_hi[:, cc, 0:T].bitcast(F32),
                          ALU.subtract).then_inc(*DVE_.up(("u", s, cc)))

    def residual_pool(pool, s, T):
        pool.wait_ge(*POOL_.at("full", s, KC - 1))
        for cc in range(KC):
            pool.wait_ge(*ACT_.at("u hi", s, cc))
            if s == 0:
                pool.tensor_scalar(h[:, cc, 0:T], h[:, cc, 0:T], ALPHA, None, ALU.mult)\
                    .then_inc(*POOL_.up(("h", s, cc)))
            else:
                pool.tensor_scalar(h[:, cc, 0:T], h[:, cc, 0:T], gA[:, s - 1, cc:cc + 1],
                                   bA[:, s - 1, cc:cc + 1], ALU.mult, ALU.add).then_inc(*POOL_.up(("h", s, cc)))

    def last_evicted(ph):
        return lambda cc: (evicted, ph.u0 + cc // 2 + 1)

    def scale1(s):
        return lambda cc, kind: vS1[:, s, cc, kind:kind + 1]

    def shift1(s):
        return lambda cc, kind: vS0[:, s, cc, kind:kind + 1]

    def norm1_dve(dve, s, T):
        if s in TAKES:
            split_lo(dve, TAKES[s].u0 + 1, early=True)
        centre_dve(dve, s, T)
        dve.wait_ge(*ACT_.at("rstd", s))
        for cc in range(KC + 1):
            if cc < KC:
                dve.wait_ge(*DVE_.at("centred", s, cc))
                dve.tensor_tensor(h[:, cc, 0:T], h[:, cc, 0:T], rstd[:, 0:T], ALU.mult)\
                    .then_inc(*DVE_.up(("n", s, cc)))
            if cc < KC // 2:
                centre_chunk(dve, s, T, cc + KC // 2)
            if cc and s < 6:
                low_dve(dve, s, T, cc - 1, uhi, ulo)

    def norm1_act(act, s, T):
        rstd_act(act, s, T, True)
        if s < 6:
            layer_input_act(act, s, T, lambda cc: DVE_.at("n", s, cc), scale1(s), shift1(s), uhi)
            return
        for cc in range(KC):
            act.wait_ge(*DVE_.at("n", s, cc))
            act.activation(h[:, cc, 0:T], h[:, cc, 0:T], ACT.Identity, scale=vS1[:, s, cc, 0:1],
                           bias=vS0[:, s, cc, 0:1]).then_inc(*ACT_.up(("h", s, cc)))

    def norm2_dve(dve, s, x_hi, x_lo):
        split_lo(dve, TAKES[s].u0 + 1, early=True)
        dve.wait_ge(*ACT_.at("rstd", s))
        for cc in range(KC + 1):
            if cc < KC:
                if cc >= 2:
                    dve.wait_ge(*ACT_.at("u hi", s, cc - 2))
                    dve.wait_ge(*POOL_.at("full", s, cc - 2))
                dve.tensor_tensor(scaled[:, cc % 2, 0:S], h[:, cc, 0:S], rstd[:, 0:S], ALU.mult)\
                    .then_inc(*DVE_.up(("n", s, cc)))
            if cc:
                low_dve(dve, s, S, cc - 1, x_hi, x_lo)

    def norm2_act(act, s, l, name, x_hi):
        rstd_act(act, s, S, False)
        layer_input_act(act, s, S, lambda cc: DVE_.at("n", s, cc), lambda cc, kind: vec2(l, name, cc), None,
                        x_hi, src=scaled)

    seen, at = {}, 0
    for name, ph in phases.items():
        if ".in" in name:
            seen[name] = at
            at += ph.n
    WIDE = dict(hi=fhi, lo=flo, a=silu_a, full=hidden)
    NARROW = dict(hi=f2hi, lo=f2lo, a=silu_a2, full=hidden2)

    def ffn_in_pe(pe, name, s, T, x_hi, x_lo):
        ph = phases[name]

        def one(u, i, it):
            if ph in after_norm and u == ph.u0:
                first_unit(pe, ph, s, x_hi, x_lo, T)
                return
            start_unit(pe, u, it)
            for half in range(2):
                feature_major(pe, u, half, range(KC), x_hi, x_lo, T).then_inc(product, 1)
        sweep(pe, ph, one)

    def ffn_in_act(act, name, T, buf):
        ph = phases[name]

        def one(u, i, it):
            f = seen[name] + u - ph.u0
            split_hi(act, u + 1, it)
            act.wait_ge(product, plus(2 * u + 1, 4, it))
            if u >= 2:
                act.wait_ge(evicted, plus(u - 1, 2, it))
            act.activation(buf["a"][:, u % 2, 0:T], banks[:, bank(u, 0), 0:T], ACT.Silu).then_inc(f_silu, 1)
            act.wait_ge(evicted, plus(u + 1, 2, it))
            act.copy(buf["hi"][:, i, 0:T], buf["full"][:, u % 2, 0:T]).then_inc(f_hi, 1)
        sweep(act, ph, one)

    def ffn_in_dve(dve, name, T, buf):
        ph = phases[name]

        def one(u, i, it):
            f = seen[name] + u - ph.u0
            split_lo(dve, u + 1, it)
            dve.wait_ge(product, plus(2 * u + 2, 4, it))
            dve.wait_ge(f_silu, plus(f + 1, 2, it))
            if f >= 2:
                dve.wait_ge(f_split, plus(f - 1, 2, it))
            dve.tensor_tensor(buf["full"][:, u % 2, 0:T], buf["a"][:, u % 2, 0:T], banks[:, bank(u, 1), 0:T],
                              ALU.mult).then_inc(evicted, 1)
            dve.wait_ge(f_hi, plus(f + 1, 2, it))
            dve.tensor_tensor(buf["lo"][:, i, 0:T], buf["full"][:, u % 2, 0:T],
                              buf["hi"][:, i, 0:T].bitcast(F32), ALU.subtract).then_inc(f_split, 1)
            if it is not None and name in MOD_FIRST:
                for n in range(2):
                    mod_products(dve, MOD_FIRST[name] + 2 * ((u - ph.u0) % 2) + n, it)
        sweep(dve, ph, one)
        vectors_after(dve, name)

    def ffn_out_pe(pe, name, T, buf):
        ph, before = phases[name], seen[name.replace("out", "in")]
        for i in range(ph.n):
            start_unit(pe, ph.u0 + i)
            for half in range(2):
                feature_major(pe, ph.u0 + i, half, range(FC), buf["hi"], buf["lo"], T,
                              arrived=(lambda k: (f_split, before + k + 1)) if i + half == 0 else None)\
                    .then_inc(product, 1)

    def out_pe(pe, name, T, x_hi, x_lo, arrived):
        ph = phases[name]
        for i in range(ph.n):
            start_unit(pe, ph.u0 + i)
            for half in range(2):
                feature_major(pe, ph.u0 + i, half, range(KC), x_hi, x_lo, T,
                              arrived=arrived if i + half == 0 else None).then_inc(product, 1)

    def out_act(act, name, s=None, T=None):
        ph = phases[name]
        for i in range(ph.n):
            split_hi(act, ph.u0 + i + 1)
            if s is not None:
                squares_act(act, s, T, last_evicted(ph), (2 * i, 2 * i + 1))

    def out_dve(dve, name, T, gated_by, ready):
        ph = phases[name]
        for i in range(ph.n):
            u = ph.u0 + i
            split_lo(dve, u + 1)
            for half in range(2):
                cc = 2 * i + half
                dve.wait_ge(product, 2 * u + half + 1)
                if ready is not None:
                    dve.wait_ge(*ready(cc))
                for kind, a, b in kinds(T):
                    ins = dve.scalar_tensor_tensor(h[:, cc, a:b], banks[:, bank(u, half), a:b], gated_by(cc, kind),
                                                   h[:, cc, a:b], ALU.mult, ALU.add)
            ins.then_inc(evicted, 1)
            if name in MOD_FIRST:
                for n in range(2):
                    mod_products(dve, MOD_FIRST[name] + 2 * i + n)

    def gate1(s):
        return lambda cc, kind: vG[:, s, cc, kind:kind + 1]

    def block1_ffn(engine, e, tag, s, T):
        after = dict(s=s + 1, T=T)
        if engine == "pe":
            for half in range(2):
                ffn_in_pe(e, f"{tag}.in{half}", s, T, uhi, ulo)
                ffn_out_pe(e, f"{tag}.out{half}", T, WIDE)
            means_pe(e, s + 1, T, last_evicted(phases[f"{tag}.out1"]))
        if engine == "act":
            for half in range(2):
                ffn_in_act(e, f"{tag}.in{half}", T, WIDE)
                out_act(e, f"{tag}.out{half}", **(after if half else {}))
        if engine == "dve":
            for half in range(2):
                ffn_in_dve(e, f"{tag}.in{half}", T, WIDE)
                out_dve(e, f"{tag}.out{half}", T, gate1(s),
                        last_evicted(phases[f"{tag}.out0"]) if half else lambda cc: POOL_.at("h", s, cc))
        if engine == "pool":
            for part in ("in0", "out0", "in1"):
                if f"{tag}.{part}" in MOD_FIRST:
                    mod_loads(e, f"{tag}.{part}")
            sums_pool(e, s + 1, T, last_evicted(phases[f"{tag}.out1"]), True)

    SCORE_BANKS = (0, 1, 4, 5)

    def score_bank(n):
        return SCORE_BANKS[n % 4]

    def attention_pe(pe, tag, tiles):
        def scores(n):
            t = tiles[n]
            if n >= 4:
                pe.wait_ge(*ACT_.at(tag, "exp", n - 4))
            pe.matmul(banks[:, score_bank(n), 0:t["n"]], t["q"], t["k"], start=True, stop=True)\
                .then_inc(*PE_.up((tag, "scores", n)))

        def transposes(n):
            t = tiles[n]
            pe.wait_ge(*DVE_.at(tag, "probs", n))
            if n >= 2:
                pe.wait_ge(*ACT_.at(tag, "probs_t", n - 2))
            for j in range(t["n"] // P):
                mm = pe.transpose(banks[:, 2 + n % 2, j * P:(j + 1) * P], probs(n)[:, j * P:(j + 1) * P], ident)
            mm.then_inc(*PE_.up((tag, "transposed", n)))

        def values(n):
            t = tiles[n]
            pe.wait_ge(*ACT_.at(tag, "probs_t", n))
            if t["first"] and t["group"] >= 2:
                pe.wait_ge(*DVE_.at(tag, "out", t["group"] - 2))
            p0, a = t["at"]
            for j, v in enumerate(t["v"]):
                mm = pe.matmul(banks[p0:p0 + HD, 6 + t["group"] % 2, a:a + P], v, probs_t[:, n % 2, j * P:(j + 1) * P],
                               start=(j == 0), stop=(j == len(t["v"]) - 1))
            mm.then_inc(*PE_.up((tag, "values", n)))

        N = len(tiles)
        scores(0)
        scores(1)
        for n in range(N + 2):
            if n + 2 < N:
                scores(n + 2)
            if 1 <= n <= N:
                transposes(n - 1)
            if n >= 2:
                values(n - 2)

    def attention_act(act, tag, tiles, y_hi):
        N = len(tiles)
        for n in range(N + 3):
            if n < N:
                t = tiles[n]
                act.wait_ge(*DVE_.at(tag, "max", n))
                if n >= 4:
                    act.wait_ge(*PE_.at(tag, "transposed", n - 4))
                act.activation(probs(n)[:, 0:t["n"]], banks[:, score_bank(n), 0:t["n"]], ACT.Exp,
                               bias=small[:, n % 4:n % 4 + 1], accum_out=small[:, 4 + n % 4:5 + n % 4])\
                    .then_inc(*ACT_.up((tag, "exp", n)))
                if t["sink"] is not None:
                    act.activation(small[:, 8 + n % 4:9 + n % 4], t["sink"], ACT.Exp, bias=small[:, n % 4:n % 4 + 1])\
                        .then_inc(*ACT_.up((tag, "sink", n)))
            if 1 <= n <= N:
                m = n - 1
                act.wait_ge(*PE_.at(tag, "transposed", m))
                if m >= 2:
                    act.wait_ge(*PE_.at(tag, "values", m - 2))
                w = tiles[m]["n"]
                act.copy(probs_t[:, m % 2, 0:w], banks[:, 2 + m % 2, 0:w]).then_inc(*ACT_.up((tag, "probs_t", m)))
            if n >= 3 and tiles[n - 3]["last"]:
                t = tiles[n - 3]
                act.wait_ge(*PE_.at(tag, "values", n - 3))
                w = t["width"]
                act.copy(y_hi[:, t["chunk"], 0:w], banks[:, 6 + t["group"] % 2, 0:w])\
                    .then_inc(*ACT_.up((tag, "out", t["group"])))

    def attention_dve(dve, tag, tiles, y_hi, y_lo):
        N = len(tiles)
        for n in range(N + 4):
            if n < N:
                t = tiles[n]
                sc = banks[:, score_bank(n), 0:t["n"]]
                dve.wait_ge(*PE_.at(tag, "scores", n))
                nmax, other = small[:, n % 4:n % 4 + 1], small[:, 120 + n % 4:121 + n % 4]
                if t["added"] is None:
                    dve.tensor_reduce(nmax, sc, AX.X, ALU.max, negate=True).then_inc(*DVE_.up((tag, "max", n)))
                else:
                    if t["added ready"] is not None:
                        dve.wait_ge(*t["added ready"])
                    w = t["added"].shape[-1]
                    part = sc[:, 0:w]
                    floor = NEG if t["sink"] is None else t["sink"]
                    if t["scale"] == 1.0:
                        dve.tensor_tensor_reduce(part, part, t["added"], 1.0, floor, ALU.add, ALU.max, nmax)\
                            .then_inc(*DVE_.up((tag, "added", n)))
                    else:
                        dve.scalar_tensor_tensor(part, part, t["scale"], t["added"], ALU.mult, ALU.add)\
                            .then_inc(*DVE_.up((tag, "added", n)))
                        dve.wait_ge(*DVE_.here())
                        dve.tensor_reduce(nmax, sc, AX.X, ALU.max, negate=True)\
                            .then_inc(*DVE_.up((tag, "max", n)))
                    if t["n"] > w:
                        dve.tensor_reduce(other, sc[:, w:], AX.X, ALU.max).then_inc(*DVE_.up())
                        dve.wait_ge(*DVE_.here())
                        dve.tensor_scalar(nmax, nmax, other, -1.0, ALU.max, ALU.mult)\
                            .then_inc(*DVE_.up((tag, "max", n)))
            if 1 <= n <= N:
                m = n - 1
                t = tiles[m]
                total, inv = small[:, 4 + m % 4:5 + m % 4], small[:, 12 + m % 4:13 + m % 4]
                dve.wait_ge(*ACT_.at(tag, "exp", m))
                if t["sink"] is not None:
                    dve.wait_ge(*ACT_.at(tag, "sink", m))
                    dve.tensor_tensor(total, total, small[:, 8 + m % 4:9 + m % 4], ALU.add).then_inc(*DVE_.up())
                    dve.wait_ge(*DVE_.here())
                dve.reciprocal(inv, total).then_inc(*DVE_.up())
                dve.wait_ge(*DVE_.here())
                pr = probs(m)[:, 0:t["n"]]
                dve.tensor_scalar(pr, pr, inv, None, ALU.mult).then_inc(*DVE_.up((tag, "probs", m)))
            if n >= 4 and tiles[n - 4]["last"]:
                t = tiles[n - 4]
                dve.wait_ge(*ACT_.at(tag, "out", t["group"]))
                w = t["width"]
                dve.tensor_tensor(y_lo[:, t["chunk"], 0:w], banks[:, 6 + t["group"] % 2, 0:w],
                                  y_hi[:, t["chunk"], 0:w].bitcast(F32), ALU.subtract)\
                    .then_inc(*DVE_.up((tag, "out", t["group"])))

    def na_tiles():
        tiles = []
        for hd in range(NH):
            ck, p0 = hd // 2, HD * (hd % 2)
            for t in range(4):
                k0 = 0 if t < 2 else S
                tiles.append(dict(
                    q=qT[p0:p0 + HD, ck, t * P:(t + 1) * P], k=kT[p0:p0 + HD, ck, k0:T2], n=T2 - k0,
                    added=na_bias[:, hd % 2, t * S:(t + 1) * S] if t < 2 else None, scale=1.0,
                    sink=None, v=[vv[:, kt, hd * HD:(hd + 1) * HD] for kt in range(k0 // P, 4)],
                    group=ck, chunk=ck, at=(p0, t * P), first=(hd % 2 == 0 and t == 0),
                    last=(hd % 2 == 1 and t == 3), width=T2))
                tiles[-1]["added ready"] = POOL_.at("bias", hd) if t == 0 else None
        return tiles

    def wa_tiles():
        tiles = []
        for ck in range(KC):
            for side in range(2):
                hd = 8 * (ck // 4) + ck % 4 + 4 * side
                kv, p0 = 2 * (ck // 4) + side, HD * side
                for t in range(2):
                    tiles.append(dict(
                        q=qT[p0:p0 + HD, ck, t * P:(t + 1) * P], k=kT[p0:p0 + HD, ck // 4, 0:T2], n=T2,
                        added=c("wa_mask")[:, t * S:(t + 1) * S], scale=1.0, sink=sinks[:, hd:hd + 1],
                        v=[vv[:, kt, kv * HD:(kv + 1) * HD] for kt in range(4)], group=ck, chunk=ck,
                        at=(p0, t * P), first=(side == 0 and t == 0), last=(side == 1 and t == 1), width=S))
                    tiles[-1]["added ready"] = None
        return tiles

    def mla_tiles():
        tiles = []
        for hd in range(MLA_H):
            for t in range(2):
                n = (t + 1) * P
                tiles.append(dict(
                    q=qk[0:QK, hd, t * P:(t + 1) * P], k=qk[0:QK, 4 + hd, 0:n], n=n,
                    added=c("causal")[:, t * S:t * S + n], scale=QK ** -0.5, sink=None,
                    v=[mla_v[:, kt, hd * HD:(hd + 1) * HD] for kt in range(t + 1)], group=hd // 2,
                    chunk=6 + hd // 2, at=(HD * (hd % 2), t * P), first=(hd % 2 == 0 and t == 0),
                    last=(hd % 2 == 1 and t == 1), width=S))
                tiles[-1]["added ready"] = None
        return tiles

    def qkv_pe(pe, tag, s, Tq):
        for what, T in (("q", Tq), ("k", T2)):
            ph = phases[f"{tag}.{what}"]
            first = 0
            if what == "q":
                first_unit(pe, ph, s, uhi, ulo, T)
                first = 1
            for i in range(first, ph.n):
                start_unit(pe, ph.u0 + i)
                for half in range(2):
                    feature_major(pe, ph.u0 + i, half, range(KC), uhi, ulo, T).then_inc(product, 1)
        ph = phases[f"{tag}.v"]
        for i in range(ph.n):
            u = ph.u0 + i
            start_unit(pe, u)
            for tile in range(4):
                out = banks[:, bank(u, tile // 2), (tile % 2) * 256:(tile % 2) * 256 + 256]
                mm = token_major(pe, u, out, tile, 0, 256, uhi, ulo)
                if tile % 2:
                    mm.then_inc(product, 1)

    def qkv_act(act, tag, Tq):
        for what, T, dst, scale in (("q", Tq, qT, HD ** -0.5), ("k", T2, kT, 1.0)):
            ph = phases[f"{tag}.{what}"]
            for i in range(ph.n):
                u = ph.u0 + i
                split_hi(act, u + 1)
                for half in range(2):
                    act.wait_ge(product, 2 * u + half + 1)
                    ins = act.activation(dst[:, 2 * i + half, 0:T], banks[:, bank(u, half), 0:T], ACT.Copy, scale=scale)
                ins.then_inc(evicted, 1)
        ph = phases[f"{tag}.v"]
        for i in range(ph.n):
            u = ph.u0 + i
            split_hi(act, u + 1)
            for half in range(2):
                act.wait_ge(product, 2 * u + half + 1)
                ins = act.copy(vv[:, 2 * half:2 * half + 2, i * 256:(i + 1) * 256],
                               banks[:, bank(u, half), :].rearrange("p (t n) -> p t n", t=2))
            ins.then_inc(evicted, 1)

    def qkv_dve(dve, tag):
        for what in "qkv":
            name = f"{tag}.{what}"
            ph = phases[name]
            for i in range(ph.n):
                split_lo(dve, ph.u0 + i + 1)
                if name in MOD_FIRST:
                    for n in range(2):
                        mod_products(dve, MOD_FIRST[name] + 2 * i + n)
            vectors_after(dve, name)

    def qkv_done(e, tag):
        ph = phases[f"{tag}.v"]
        e.wait_ge(evicted, ph.u0 + ph.n)

    def wa_rope_pe(pe):
        for j in range(10):
            src = qT[:, j, 0:S] if j < KC else kT[:, j - KC, 0:S]
            if j >= 4:
                pe.wait_ge(*DVE_.at("rotated", j - 4))
            pe.matmul(banks[:, 4 + j % 4, 0:S], c("rope_perm"), src, start=True, stop=True)\
                .then_inc(*PE_.up(("swapped", j)))
        pe.wait_ge(*DVE_.at("rotated", 9))

    def wa_rope_dve(dve):
        qkv_done(dve, "L1")
        dve.wait_ge(window_loaded, 16)
        for j in range(10):
            x = qT[:, j, 0:S] if j < KC else kT[:, j - KC, 0:S]
            t = squares[:, j % 2, 0:S]
            dve.wait_ge(*PE_.at("swapped", j))
            dve.tensor_tensor(t, banks[:, 4 + j % 4, 0:S], c("rope_sin"), ALU.mult).then_inc(*DVE_.up())
            dve.tensor_tensor(x, x, c("rope_cos"), ALU.mult).then_inc(*DVE_.up())
            dve.wait_ge(*DVE_.here())
            dve.tensor_tensor(x, x, t, ALU.add).then_inc(*DVE_.up(("rotated", j)))

    def bias_pool(pool):
        pool.wait_ge(mod_done, 2 * (MOD_FIRST["L0.v"] + KC))
        for hd in range(NH + 1):
            if hd < NH:
                if hd >= 2:
                    pool.wait_ge(*DVE_.at("L0", "added", 4 * (hd - 2) + 1))
                pool.dma_start(na_bias[:, hd % 2, :], A["na_rpb"][hd]).then_inc(bias_loaded[hd % 2], 16)
            if hd >= 1:
                m = hd - 1
                pool.wait_ge(bias_loaded[m % 2], 16 * (m // 2 + 1))
                bias = na_bias[:, m % 2, :].rearrange("p (r c) -> p r c", c=GRID_W)
                mask = c("na_mask").rearrange("p (o c) -> p o c", o=1).to_broadcast([P, T2 // GRID_W, GRID_W])
                pool.tensor_tensor(bias, bias, mask, ALU.add)\
                    .then_inc(*POOL_.up(("bias", m)))

    def z_pe(pe, l, s):
        ph = phases[f"M{l}.z"]
        first_unit(pe, ph, s, u2hi, u2lo, S)
        for i in range(1, ph.n):
            u = ph.u0 + i
            start_unit(pe, u)
            if i in (2, 7, 8):
                for tile in range(2):
                    token_major(pe, u, banks[:, bank(u, tile), 0:256], tile, 0, 256, u2hi, u2lo)\
                        .then_inc(product, 1)
                continue
            for half in range(2):
                mm = feature_major(pe, u, half, range(KC), u2hi, u2lo, S)
                if i == 12 and half == 1:
                    for tile in range(2):
                        mm = token_major(pe, u, banks[:, bank(u, 1), 256 + 8 * tile:264 + 8 * tile], tile,
                                         P, P + 8, u2hi, u2lo)
                mm.then_inc(product, 1)

    def z_act(act, l):
        ph = phases[f"M{l}.z"]
        for i in range(ph.n):
            u = ph.u0 + i
            split_hi(act, u + 1)
            if i in (2, 7, 8):
                continue
            if i:
                act.wait_ge(evicted, u)
            for half in range(2):
                ps = banks[:, bank(u, half), 0:S]
                act.wait_ge(product, 2 * u + half + 1)
                if i == 0:
                    act.wait_ge(*DVE_.at("sbq bias"))
                    ins = act.activation(sbq[:, half], ps, ACT.Identity, scale=HD ** -0.5, bias=vec2(l, "b_sbq", half))
                elif i == 1:
                    ins = act.activation(sbk[:, half], ps, ACT.Identity, bias=vec2(l, "b_sbk", half))
                elif i < 7:
                    cc = 2 * (i - 3) + half
                    ins = act.activation(conv_in[:, cc, 3:], ps, ACT.Identity, bias=vec2(l, "b_mlqk", cc))
                elif i < 11:
                    cc = 2 * (i - 9) + half
                    ins = act.activation(osig[:, cc], ps, ACT.Sigmoid, bias=vec2(l, "b_mlo", cc))
                elif i == 11:
                    ins = act.activation(cq[:, half], ps, ACT.Identity, bias=vec2(l, "b_cq", half))
                elif half == 0:
                    ins = act.activation(cq[:, 2], ps, ACT.Identity, bias=vec2(l, "b_ckv"))
                else:
                    ins = act.activation(kr[HD:QK, :], banks[HD:QK, bank(u, 1), 0:S], ACT.Identity,
                                         bias=vec2(l, "b_kr")[HD:QK])
            if i < 12:
                ins.then_inc(evicted, 1)
            else:
                ins.then_inc(*ACT_.up(("kr", l)))

    def conv_dve(dve, l, tap):
        for cc in range(KC):
            x, w = conv_in[:, cc, tap:tap + S], vec2(l, "conv_w", 8 * tap + cc)
            if tap == 0:
                dve.wait_ge(*POOL_.at("conv pad", l))
                dve.wait_ge(evicted, phases[f"M{l}.z"].u0 + CONV_READY)
                dve.tensor_scalar(mlqk[:, cc], x, w, vec2(l, "conv_b", cc), ALU.mult, ALU.add)\
                    .then_inc(*DVE_.up(("ml tap", l, tap, cc)))
            else:
                dve.wait_ge(*DVE_.at("ml tap", l, tap - 1, cc))
                dve.scalar_tensor_tensor(mlqk[:, cc], x, w, mlqk[:, cc], ALU.mult, ALU.add)\
                    .then_inc(*DVE_.up(("ml tap", l, tap, cc)))

    CONV_READY = 7

    def z_dve(dve, l):
        ph = phases[f"M{l}.z"]
        for i in range(ph.n):
            u = ph.u0 + i
            split_lo(dve, u + 1)
            if i in (2, 7, 8, 12):
                dve.wait_ge(evicted, u)
            if i in (2, 7, 8):
                for tile in range(2):
                    dst = sbv[:, tile, :] if i == 2 else mlv[:, tile, (i - 7) * 256:(i - 6) * 256]
                    at = ROW2["b_sbv"][0] if i == 2 else ROW2["b_mlv"][0] + (i - 7) * 256
                    dve.wait_ge(product, 2 * u + tile + 1)
                    ins = dve.tensor_tensor(dst, banks[:, bank(u, tile), 0:256], rows2[:, l, at:at + 256], ALU.add)
                ins.then_inc(evicted, 1)
            if 8 <= i < 12:
                conv_dve(dve, l, i - 8)
            if i == 12:
                dve.wait_ge(*ACT_.at("kr", l))
                at = ROW2["b_if"][0]
                for tile in range(2):
                    ins = dve.tensor_tensor(iff[:, tile], banks[:, bank(u, 1), 256 + 8 * tile:264 + 8 * tile],
                                            rows2[:, l, at:at + 8], ALU.add)
                ins.then_inc(evicted, 1)

    def z_done(e, l):
        ph = phases[f"M{l}.z"]
        e.wait_ge(evicted, ph.u0 + ph.n)

    def sb_bufs(r):
        def pair(t):
            t = t if len(t.shape) == 2 else t.rearrange("p a b -> p (a b)")
            return t.rearrange("p (a b) -> p a b", a=2)
        conv = conv_in[:].rearrange("p a b -> p (a b)")
        e, keep, zl, w = ((squares[:, :, 0:384], sums[:, :, 0:384], scaled[:, :, 0:384], full_u[:, :, 0:384]),
                          (pair(conv[:, 0:768]), pair(conv[:, 768:1536]), pair(qk[:, 0:3]), pair(qk[:, 0:3])))[r]
        return banks[:, 2 * r:2 * r + 2, 0:384], banks[:, 4 + 2 * r:6 + 2 * r, 0:384], e, keep, zl, w

    def sb_pe(pe, l):
        z_done(pe, l)
        for r in range(2):
            for hh in range(2):
                rows = slice(HD * hh, HD * hh + HD)
                pe.matmul(banks[:, 2 * r + hh, 0:256], sbk[rows, r, 0:P], sbq[rows, r, :], start=True, stop=True)
                mm = pe.matmul(banks[:, 2 * r + hh, 256:384], sbk[rows, r, P:S], sbq[rows, r, P:S],
                               start=True, stop=True)
            mm.then_inc(*PE_.up(("sb z", l, r)))
        for r in range(2):
            log_keep = sb_bufs(r)[3]
            pe.wait_ge(*DVE_.at("sb keep", l, r))
            for hh in range(2):
                pe.matmul(banks[:, 4 + 2 * r + hh, 0:384], c("tri_strict"), log_keep[:, hh, 0:384],
                          start=True, stop=True)
                mm = pe.matmul(banks[:, 4 + 2 * r + hh, P:S], c("ones"), log_keep[:, hh, 256:384],
                               start=False, stop=True, skip_group_check=True)
            mm.then_inc(*PE_.up(("sb later", l, r)))
        for r in range(2):
            w = sb_bufs(r)[5]
            pe.wait_ge(*DVE_.at("sb w", l, r))
            for hh in range(2):
                hd = 2 * r + hh
                out = banks[HD * hh:HD * hh + HD, 2 * r, :]
                pe.matmul(out[:, 0:S], sbv[:, 0, hd * HD:(hd + 1) * HD], w[:, hh, 0:256], start=True, stop=True)
                mm = pe.matmul(out[:, P:S], sbv[:, 1, hd * HD:(hd + 1) * HD], w[:, hh, 256:384],
                               start=False, stop=True, skip_group_check=True)
            mm.then_inc(*PE_.up(("sb out", l, r)))

    def sb_act(act, l):
        for r in range(2):
            z, later, e, keep, zl, w = sb_bufs(r)
            act.wait_ge(*PE_.at("sb z", l, r))
            if r:
                act.wait_ge(*DVE_.at("ml tap", l, 3, KC - 1))
            act.activation(e, z, ACT.Abs).then_inc(*ACT_.up(("sb abs", l, r)))
        for r in range(2):
            e = sb_bufs(r)[2]
            act.wait_ge(*ACT_.at("sb abs", l, r))
            act.activation(e, e, ACT.Exp, scale=-1.0).then_inc(*ACT_.up(("sb e", l, r)))
        for r in range(2):
            e = sb_bufs(r)[2]
            act.wait_ge(*ACT_.at("sb e", l, r))
            act.activation(e, e, ACT.Ln, bias=c("one")).then_inc(*ACT_.up(("sb ln", l, r)))
        for r in range(2):
            zl, w = sb_bufs(r)[4:]
            act.wait_ge(*DVE_.at("sb logw", l, r))
            act.activation(w, zl, ACT.Exp).then_inc(*ACT_.up(("sb exp", l, r)))
        for r in range(2):
            act.wait_ge(*PE_.at("sb out", l, r))
            act.copy(yhi[:, r, :], banks[:, 2 * r, 0:S]).then_inc(*ACT_.up(("sb y", l, r)))

    def sb_dve(dve, l):
        mask = c("sb_mask")
        for r in range(2):
            z, later, e, keep, zl, w = sb_bufs(r)
            dve.wait_ge(*ACT_.at("sb ln", l, r))
            dve.scalar_tensor_tensor(keep, z, 0.0, e, ALU.max, ALU.add).then_inc(*DVE_.up())
            dve.wait_ge(*DVE_.here())
            dve.tensor_tensor(zl, z, keep, ALU.subtract).then_inc(*DVE_.up())
            dve.wait_ge(*DVE_.here())
            for hh in range(2):
                dve.scalar_tensor_tensor(keep[:, hh], keep[:, hh], -1.0, mask, ALU.mult, ALU.mult)\
                    .then_inc(*DVE_.up(("sb keep", l, r)))
        for r in range(2):
            z, later, e, keep, zl, w = sb_bufs(r)
            dve.wait_ge(*PE_.at("sb later", l, r))
            dve.tensor_tensor(zl, later, zl, ALU.add).then_inc(*DVE_.up(("sb logw", l, r)))
        for r in range(2):
            w = sb_bufs(r)[5]
            dve.wait_ge(*ACT_.at("sb exp", l, r))
            for hh in range(2):
                dve.tensor_tensor(w[:, hh], w[:, hh], mask, ALU.mult).then_inc(*DVE_.up(("sb w", l, r)))
        for r in range(2):
            dve.wait_ge(*ACT_.at("sb y", l, r))
            dve.tensor_tensor(ylo[:, r, :], banks[:, 2 * r, 0:S], yhi[:, r, :].bitcast(F32), ALU.subtract)\
                .then_inc(*DVE_.up(("y", l, r)))

    def slot(n, w=8):
        return small[:, 16 + 8 * n:16 + 8 * n + w]

    LF, CUM, FTOT, R_, M_, RMAX, NEGM, EXPARG, EXPS, DEN, RDEN, SS, MNEW, ABS = 0, 1, 2, 3, 4, 5, 6, 7, 9, 11, 13, 14, 15, 16

    def tc(ap):
        return ap.rearrange("p (t c) -> p t c", t=2)

    sT, w_buf, n_buf = squares, scaled, sums

    def flat(t):
        return t[:].rearrange("p a b -> p (a b)")

    def ml_pe(pe, l):
        tri, ones, q, k = c("tri_incl"), c("ones"), mlqk[:, 0:4], mlqk[:, 4:8]
        pe.wait_ge(*DVE_.at("ml lf", l))
        pe.matmul(banks[:, 4, 0:8], tri, slot(LF), start=True, stop=True)
        pe.matmul(banks[:, 4, 8:16], ones, slot(LF), start=True, stop=True).then_inc(*PE_.up(("ml cum", l)))
        pe.wait_ge(*DVE_.at("ml diag r", l))
        for t in range(2):
            mm = pe.matmul(banks[:, 4 + t, :], ones, sT[:, t, :], start=True, stop=True)
        mm.then_inc(*PE_.up(("ml r rows", l)))
        pe.wait_ge(*ACT_.at("ml k", l))
        for t in range(2):
            for hd in range(4):
                ts = slice(t * P, t * P + P)
                mm = pe.matmul(banks[:, 6 + t, hd * P:(hd + 1) * P], k[:, hd, ts], q[:, hd, ts],
                               start=True, stop=True)
        mm.then_inc(*PE_.up(("ml kq", l)))
        pe.wait_ge(*DVE_.at("y", l, 1))
        for hd in range(4):
            mm = pe.transpose(banks[:, 0, hd * P:(hd + 1) * P], k[:, hd, 0:P], ident)
        mm.then_inc(*PE_.up(("ml k tokens", l)))
        pe.wait_ge(*DVE_.at("ml diag m", l))
        for t in range(2):
            mm = pe.matmul(banks[:, 4 + t, :], ones, sT[:, t, :], start=True, stop=True)
        mm.then_inc(*PE_.up(("ml m rows", l)))
        pe.wait_ge(*ACT_.at("ml k end", l))
        for hd in range(4):
            kd = full_u[:, 0, hd * P:(hd + 1) * P]
            pe.matmul(banks[:, 1, hd * P:(hd + 1) * P], kd, mlv[:, 0, hd * P:(hd + 1) * P], start=True, stop=True)
            mm = pe.matmul(banks[:, 2, hd:hd + 1], kd, ones[:, 0:1], start=True, stop=True)
        mm.then_inc(*PE_.up(("ml state", l)))
        pe.wait_ge(*ACT_.at("ml state", l))
        for hd in range(4):
            pe.matmul(banks[:, 3, hd * P:(hd + 1) * P], q[:, hd, P:S], full_u[:, 1, hd * P:(hd + 1) * P],
                      start=True, stop=True)
            mm = pe.matmul(banks[:, 0, 8 + hd:9 + hd], q[:, hd, P:S], slot(ABS)[:, hd:hd + 1], start=True, stop=True)
        pe.wait_ge(*DVE_.at("ml scores", l))
        for j in range(8):
            t, hd = j // 4, j % 4
            s_ = flat(sT)[:, j * P:(j + 1) * P]
            pe.matmul(banks[:, 4 + t, hd * P:(hd + 1) * P], s_, mlv[:, t, hd * P:(hd + 1) * P], start=True, stop=True)
            mm = pe.matmul(banks[:, 0, j:j + 1], s_, ones[:, 0:1], start=True, stop=True)
        mm.then_inc(*PE_.up(("ml num", l)))
        pe.wait_ge(*DVE_.at("ml h", l))
        for j in range(8):
            t, hd = j // 4, j % 4
            at = (hd % 2) * S + t * P
            mm = pe.transpose(banks[:, 6 + hd // 2, at:at + P], flat(n_buf)[:, j * P:(j + 1) * P], ident)
        mm.then_inc(*PE_.up(("ml h features", l)))

    def ml_act(act, l):
        f = iff[:, :, 4:8]
        z_done(act, l)
        ab = tc(slot(ABS))
        act.activation(ab, f, ACT.Abs).then_inc(*ACT_.up())
        act.wait_ge(*ACT_.here())
        act.activation(ab, ab, ACT.Exp, scale=-1.0).then_inc(*ACT_.up())
        act.wait_ge(*ACT_.here())
        act.activation(ab, ab, ACT.Ln, bias=c("one")).then_inc(*ACT_.up(("ml ln", l)))
        act.wait_ge(*DVE_.at("ml tap", l, 3, KC - 1))
        for g in range(2):
            x = mlqk[:, 4 * g:4 * g + 4]
            act.activation(x, x, ACT.Silu).then_inc(*ACT_.up())
        act.wait_ge(*ACT_.here())
        act.mul(mlqk[:, 4:8], mlqk[:, 4:8], 128 ** -0.5).then_inc(*ACT_.up(("ml k", l)))
        act.wait_ge(*DVE_.at("ml args", l))
        act.activation(slot(EXPS, 16), slot(EXPARG, 16), ACT.Exp).then_inc(*ACT_.up(("ml exps", l)))
        act.wait_ge(*ACT_.here())
        act.wait_ge(*PE_.at("ml k tokens", l))
        act.wait_ge(*PE_.at("sb out", l, 1))
        for hd in range(4):
            act.activation(full_u[:, 0, hd * P:(hd + 1) * P], banks[:, 0, hd * P:(hd + 1) * P], ACT.Copy,
                           scale=slot(EXPS)[:, hd:hd + 1]).then_inc(*ACT_.up(("ml k end", l)))
        act.wait_ge(*DVE_.at("ml m masked", l))
        for j in range(8):
            w = flat(w_buf)[:, j * P:(j + 1) * P]
            act.activation(w, w, ACT.Exp, bias=slot(R_)[:, j:j + 1]).then_inc(*ACT_.up(("ml w", l)))
        act.wait_ge(*PE_.at("ml state", l))
        act.copy(full_u[:, 1, :], banks[:, 1, :]).then_inc(*ACT_.up())
        act.copy(slot(ABS)[:, 0:4], banks[:, 2, 0:4]).then_inc(*ACT_.up(("ml state", l)))
        act.wait_ge(*DVE_.at("ml ss", l))
        act.activation(slot(SS), slot(SS), ACT.Ln, scale=1 / 128, bias=c("rms_eps")).then_inc(*ACT_.up())
        act.wait_ge(*ACT_.here())
        act.activation(slot(SS), slot(SS), ACT.Exp, scale=-0.5).then_inc(*ACT_.up(("ml rms", l)))
        for hd in range(4):
            act.wait_ge(*DVE_.at("ml y", l, hd))
            act.copy(yhi[:, 2 + hd, :], flat(w_buf)[:, hd * S:(hd + 1) * S]).then_inc(*ACT_.up(("ml y hi", l, hd)))

    def ml_dve(dve, l):
        tt, up = dve.tensor_tensor, DVE_.up
        dve.wait_ge(*ACT_.at("ml ln", l))
        dve.scalar_tensor_tensor(tc(slot(LF)), iff[:, :, 4:8], 0.0, tc(slot(ABS)), ALU.min, ALU.subtract)\
            .then_inc(*up(("ml lf", l)))
        dve.wait_ge(*PE_.at("ml cum", l))
        dve.tensor_copy(slot(CUM, 16), banks[:, 4, 0:16]).then_inc(*up())
        dve.wait_ge(*DVE_.here())
        tt(tc(slot(R_)), iff[:, :, 0:4], tc(slot(CUM)), ALU.subtract).then_inc(*up())
        dve.wait_ge(*DVE_.here())
        for j in range(8):
            dve.tensor_scalar(flat(sT)[:, j * P:(j + 1) * P], ident, slot(R_)[:, j:j + 1], None, ALU.mult)\
                .then_inc(*up(("ml diag r", l)))
        dve.wait_ge(*PE_.at("ml r rows", l))
        rows = banks[:, 4:6, :].rearrange("p t (c s) -> p (t c) s", c=4)
        dve.tensor_reduce(slot(RMAX), rows, AX.X, ALU.max).then_inc(*up())
        causal = c("causal")[:, 0:P]
        wb = flat(w_buf).rearrange("p (j s) -> p j s", j=8)
        for j in range(8):
            tt(wb[:, j], rows[:, j], causal, ALU.add).then_inc(*up())
        dve.wait_ge(*DVE_.here())
        dve.tensor_reduce(slot(M_), wb, AX.X, ALU.max).then_inc(*up())
        dve.wait_ge(*DVE_.here())
        dve.tensor_scalar(slot(M_)[:, 0:4], slot(M_)[:, 0:4], 0.0, None, ALU.max).then_inc(*up())
        dve.scalar_tensor_tensor(slot(MNEW)[:, 0:4], slot(RMAX)[:, 0:4], 0.0, slot(FTOT)[:, 0:4], ALU.max, ALU.add)\
            .then_inc(*up())
        dve.wait_ge(*DVE_.here())
        tt(slot(M_)[:, 4:8], slot(M_)[:, 4:8], slot(MNEW)[:, 0:4], ALU.max).then_inc(*up())
        args = slot(EXPARG, 16)
        tt(args[:, 0:4], slot(FTOT)[:, 0:4], slot(MNEW)[:, 0:4], ALU.subtract).then_inc(*up())
        dve.wait_ge(*DVE_.here())
        tt(args[:, 0:4], args[:, 0:4], slot(R_)[:, 0:4], ALU.add).then_inc(*up())
        tt(args[:, 4:8], slot(MNEW)[:, 0:4], slot(M_)[:, 4:8], ALU.subtract).then_inc(*up())
        dve.scalar_tensor_tensor(args[:, 8:16], slot(CUM), -1.0, slot(M_), ALU.mult, ALU.subtract)\
            .then_inc(*up(("ml args", l)))
        dve.tensor_scalar(slot(NEGM), slot(M_), -1.0, None, ALU.mult).then_inc(*up())
        dve.wait_ge(*DVE_.here())
        for j in range(8):
            dve.tensor_scalar(flat(sT)[:, j * P:(j + 1) * P], ident, slot(NEGM)[:, j:j + 1], None, ALU.mult)\
                .then_inc(*up(("ml diag m", l)))
        dve.wait_ge(*PE_.at("ml m rows", l))
        for j in range(8):
            tt(wb[:, j], rows[:, j], c("causal_t"), ALU.add).then_inc(*up(("ml m masked", l)))
        dve.wait_ge(*ACT_.at("ml w", l))
        dve.wait_ge(*PE_.at("ml kq", l))
        kq = banks[:, 6:8, :]
        tt(sT[:], kq, w_buf[:], ALU.mult).then_inc(*up(("ml scores", l)))
        dve.wait_ge(*PE_.at("ml num", l))
        dve.wait_ge(*ACT_.at("ml exps", l))
        nb = flat(n_buf).rearrange("p (j s) -> p j s", j=8)
        w_inter = slot(EXPS)[:, 4:8]
        dve.tensor_copy(slot(DEN, 12), banks[:, 0, 0:12]).then_inc(*up())
        dve.tensor_copy(nb[:, 0:4], banks[:, 4, :].rearrange("p (c s) -> p c s", c=4)).then_inc(*up())
        dve.tensor_copy(nb[:, 4:8], banks[:, 5, :].rearrange("p (c s) -> p c s", c=4)).then_inc(*up())
        dve.wait_ge(*DVE_.here())
        for hd in range(4):
            dve.scalar_tensor_tensor(nb[:, 4 + hd], banks[:, 3, hd * P:(hd + 1) * P], w_inter[:, hd:hd + 1],
                                     nb[:, 4 + hd], ALU.mult, ALU.add).then_inc(*up())
        den = slot(DEN, 12)
        tt(den[:, 8:12], den[:, 8:12], w_inter, ALU.mult).then_inc(*up())
        dve.wait_ge(*DVE_.here())
        tt(den[:, 4:8], den[:, 4:8], den[:, 8:12], ALU.add).then_inc(*up())
        dve.wait_ge(*DVE_.here())
        dve.tensor_scalar(slot(RDEN), den[:, 0:8], -1.0, None, ALU.mult).then_inc(*up())
        dve.wait_ge(*DVE_.here())
        tt(den[:, 0:8], den[:, 0:8], slot(RDEN), ALU.max).then_inc(*up())
        dve.wait_ge(*DVE_.here())
        tt(den[:, 0:8], den[:, 0:8], slot(EXPS, 16)[:, 8:16], ALU.max).then_inc(*up())
        dve.wait_ge(*DVE_.here())
        dve.reciprocal(slot(RDEN), den[:, 0:8]).then_inc(*up())
        dve.wait_ge(*DVE_.here())
        for j in range(8):
            dve.tensor_scalar(nb[:, j], nb[:, j], slot(RDEN)[:, j:j + 1], None, ALU.mult).then_inc(*up())
        dve.wait_ge(*DVE_.here())
        tt(wb, nb, nb, ALU.mult).then_inc(*up())
        dve.wait_ge(*DVE_.here())
        dve.tensor_reduce(slot(SS), wb, AX.X, ALU.add).then_inc(*up(("ml ss", l)))
        dve.wait_ge(*ACT_.at("ml rms", l))
        for j in range(8):
            dve.tensor_scalar(nb[:, j], nb[:, j], slot(SS)[:, j:j + 1], None, ALU.mult).then_inc(*up(("ml h", l)))
        dve.wait_ge(*PE_.at("ml h features", l))
        for hd in range(5):
            if hd < 4:
                ps = banks[:, 6 + hd // 2, (hd % 2) * S:(hd % 2) * S + S]
                dve.scalar_tensor_tensor(flat(w_buf)[:, hd * S:(hd + 1) * S], ps, vec2(l, "ml_gain", hd), osig[:, hd],
                                         ALU.mult, ALU.mult).then_inc(*up(("ml y", l, hd)))
            if hd:
                g = hd - 1
                dve.wait_ge(*ACT_.at("ml y hi", l, g))
                tt(ylo[:, 2 + g, :], flat(w_buf)[:, g * S:(g + 1) * S], yhi[:, 2 + g, :].bitcast(F32), ALU.subtract)\
                    .then_inc(*up(("y", l, 2 + g)))

    rot = conv_in[0:QK, :, 0:S]

    def mla_pe(pe, l):
        pe.wait_ge(*ACT_.at("mla sq", l))
        sq = flat(squares)
        pe.matmul(banks[:, 0, 0:S], c("mean256"), sq[:, 0:S], start=True, stop=False)
        pe.matmul(banks[:, 0, 0:S], c("mean256"), sq[:, S:2 * S], start=False, stop=True)
        pe.matmul(banks[:, 0, S:2 * S], c("mean128"), sq[:, 2 * S:3 * S], start=True, stop=True)\
            .then_inc(*PE_.up(("mla ms", l)))
        pe.wait_ge(*DVE_.at("mla latents", l))
        pe.wait_ge(mla_loaded, 32 * (l + 1))
        for hd in range(4):
            out = (hd % 2) * S
            for k in range(2):
                pe.matmul(banks[0:QK, 1 + hd // 2, out:out + S], w_q[:, k, hd * QK:(hd + 1) * QK], cq[:, k],
                          start=(k == 0), stop=(k == 1))
            pe.matmul(banks[0:HD, 3 + hd // 2, out:out + S], w_kv[:, hd * P:hd * P + HD], cq[:, 2],
                      start=True, stop=True)
        wv = w_kv[:].rearrange("p (h two d) -> p h two d", h=4, two=2)[:, :, 1, :]
        for t in range(2):
            mm = pe.matmul(banks[:, 5, t * S:(t + 1) * S], cq[:, 2, t * P:(t + 1) * P], wv, start=True, stop=True)
        mm.then_inc(*PE_.up(("mla qkv", l)))
        pe.wait_ge(*ACT_.at("mla head sq", l))
        for j in range(4):
            mm = pe.matmul(banks[0:QK, j, :], c("mean96")[0:QK, 0:QK], rot[:, 2 * j:2 * j + 2, :], start=True, stop=True)
        mm.then_inc(*PE_.up(("mla head ms", l)))
        pe.wait_ge(*DVE_.at("mla heads", l))
        for j in range(4):
            mm = pe.matmul(banks[0:QK, 4 + j, :], c("mla_perm")[0:QK, 0:QK], qk[0:QK, 2 * j:2 * j + 2, :],
                           start=True, stop=True)
        mm.then_inc(*PE_.up(("mla swapped", l)))
        pe.wait_ge(*DVE_.at("mla rotated", l))
        attention_pe(pe, f"M{l}", mla_tiles())

    def mla_act(act, l):
        act.activation(flat(squares)[:, 0:3 * S], cq[:].rearrange("p a b -> p (a b)"), ACT.Square)\
            .then_inc(*ACT_.up(("mla sq", l)))
        act.wait_ge(*PE_.at("mla ms", l))
        act.activation(var[:], banks[:, 0, :], ACT.Ln, bias=c("rms_eps")).then_inc(*ACT_.up())
        act.wait_ge(*ACT_.here())
        act.activation(rstd[:], var[:], ACT.Exp, scale=-0.5).then_inc(*ACT_.up(("mla rms", l)))
        act.wait_ge(*PE_.at("mla qkv", l))
        for j in range(2):
            act.copy(qk[0:QK, 2 * j:2 * j + 2, :], banks[0:QK, 1 + j, :].rearrange("p (h t) -> p h t", h=2))\
                .then_inc(*ACT_.up())
            act.copy(qk[0:HD, 4 + 2 * j:6 + 2 * j, :], banks[0:HD, 3 + j, :].rearrange("p (h t) -> p h t", h=2))\
                .then_inc(*ACT_.up(("mla copied", l)))
        act.wait_ge(*POOL_.at("mla kr", l))
        act.wait_ge(*ACT_.here())
        act.activation(rot, qk[0:QK], ACT.Square).then_inc(*ACT_.up(("mla head sq", l)))
        act.wait_ge(*PE_.at("mla head ms", l))
        ms = banks[0:QK, 0:4, :].rearrange("p b (h t) -> p (b h) t", h=2)
        act.activation(rot, ms, ACT.Ln, bias=c("rms_eps")[0:QK]).then_inc(*ACT_.up())
        act.wait_ge(*ACT_.here())
        act.activation(rot, rot, ACT.Exp, scale=-0.5).then_inc(*ACT_.up(("mla head rms", l)))
        attention_act(act, f"M{l}", mla_tiles(), yhi)

    def mla_dve(dve, l):
        up = DVE_.up
        dve.wait_ge(*ACT_.at("mla rms", l))
        for k in range(3):
            gain = vec2(l, "q_norm", k) if k < 2 else vec2(l, "kv_norm")
            rs = rstd[:, 0:S] if k < 2 else rstd[:, S:2 * S]
            dve.scalar_tensor_tensor(cq[:, k], cq[:, k], gain, rs, ALU.mult, ALU.mult)\
                .then_inc(*up(("mla latents", l)))
        dve.wait_ge(*PE_.at("mla qkv", l))
        dve.tensor_copy(mla_v[:].rearrange("p t n -> p (t n)"), banks[:, 5, :]).then_inc(*up(("mla v", l)))
        dve.wait_ge(*ACT_.at("mla head rms", l))
        for g, name in ((0, "q_gain"), (1, "k_gain")):
            x = qk[0:QK, 4 * g:4 * g + 4, :]
            dve.scalar_tensor_tensor(x, x, vec2(l, name)[0:QK], rot[:, 4 * g:4 * g + 4, :], ALU.mult, ALU.mult)\
                .then_inc(*up(("mla heads", l)))
        dve.wait_ge(*PE_.at("mla swapped", l))
        swapped = banks[0:QK, 4:8, :].rearrange("p b (h t) -> p (b h) t", h=2)
        for j in range(8):
            dve.tensor_tensor(rot[:, j], swapped[:, j], rope_s[:], ALU.mult).then_inc(*up())
            dve.tensor_tensor(qk[0:QK, j], qk[0:QK, j], rope_c[:], ALU.mult).then_inc(*up())
        dve.wait_ge(*DVE_.here())
        dve.tensor_tensor(qk[0:QK], qk[0:QK], rot, ALU.add).then_inc(*up(("mla rotated", l)))
        attention_dve(dve, f"M{l}", mla_tiles(), yhi, ylo)

    def mix_pool(pool, l):
        ph = phases[f"M{l}.ffn0.out0"]
        pool.wait_ge(evicted, ph.u0 + ph.n)
        pool.memset(conv_in[:, :, 0:3], 0.0).then_inc(*POOL_.up(("conv pad", l)))
        z_done(pool, l)
        pool.wait_ge(*ACT_.at("kr", l))
        for hd in range(4):
            pool.wait_ge(*POOL_.here())
            pool.tensor_copy(qk[HD:QK, 4 + hd, :], kr[HD:QK, :]).then_inc(*POOL_.up(("mla kr", l)))

    def rope_tables_dve(dve):
        ang, turns, red = sums[0:QK, 0, 0:S], sums[0:QK, 1, 0:S], (squares[0:QK, 0, 0:S], squares[0:QK, 1, 0:S])
        up, TURN, MAGIC = DVE_.up, 2 * np.pi, float(1.5 * 2 ** 23)
        first = float(np.float32(6.28125))
        second = float(np.float32(np.round((TURN - first) * 2 ** 21) / 2 ** 21))
        third = float(np.float32(TURN - first - second))
        dve.wait_ge(block2_loaded, 16 * N_BLOCK2)
        dve.tensor_copy(ang, positions[:]).then_inc(*up())
        dve.wait_ge(*DVE_.here())
        dve.tensor_scalar(ang, ang, c("inv_freq")[0:QK], None, ALU.mult).then_inc(*up())
        dve.wait_ge(*DVE_.here())
        for j, quarter in enumerate((0.0, 0.25)):
            r = red[j]
            dve.tensor_scalar(turns, ang, float(1 / TURN), quarter, ALU.mult, ALU.add).then_inc(*up())
            dve.wait_ge(*DVE_.here())
            dve.tensor_scalar(turns, turns, MAGIC, None, ALU.add).then_inc(*up())
            dve.wait_ge(*DVE_.here())
            dve.tensor_scalar(turns, turns, MAGIC, None, ALU.subtract).then_inc(*up())
            dve.wait_ge(*DVE_.here())
            dve.scalar_tensor_tensor(r, turns, -first, ang, ALU.mult, ALU.add).then_inc(*up())
            for x in (second, third):
                dve.wait_ge(*DVE_.here())
                dve.scalar_tensor_tensor(r, turns, -x, r, ALU.mult, ALU.add).then_inc(*up())
            dve.wait_ge(*DVE_.here())
            dve.tensor_scalar(r, r, float(quarter * TURN), 3.1415925, ALU.add, ALU.min).then_inc(*up())
            dve.wait_ge(*DVE_.here())
            dve.tensor_scalar(r, r, -3.1415925, None, ALU.max).then_inc(*up("reduced"))
        for l in range(2):
            b = vec2(l, "b_sbq", 0, 2)
            dve.tensor_scalar(b, b, HD ** -0.5, None, ALU.mult).then_inc(*up("sbq bias"))

    def rope_tables_act(act):
        act.wait_ge(*DVE_.at("reduced"))
        act.activation(rope_s[:], squares[0:QK, 0, 0:S], ACT.Sin).then_inc(*ACT_.up())
        act.activation(rope_c[:], squares[0:QK, 1, 0:S], ACT.Sin).then_inc(*ACT_.up("rope tables"))

    def merge_loop(e, l, one):
        ph = phases[f"M{l}.merge"]
        with e.Fori(0, 4) as it:
            for j in range(4):
                one(ph.u0 + j, j, it)

    def merge_pe(pe, l):
        for r in range(KC):
            if r < 6:
                pe.wait_ge(*DVE_.at("y", l, r))
        for g in range(2):
            pe.wait_ge(*DVE_.at(f"M{l}", "out", g))

        def one(u, j, it):
            start_unit(pe, u, it, per=4)
            for half in range(2):
                if j < 3:
                    feature_major(pe, u, half, range(KC), u2hi, u2lo, S).then_inc(product, 1)
                    continue
                b = bank(u, half)
                feature_major(pe, u, half, range(0, 2), yhi, ylo, S, out=banks[:, b, 0:S])
                feature_major(pe, u, half, range(2, 6), yhi, ylo, S, out=banks[:, b, S:2 * S])
                feature_major(pe, u, half, range(6, 8), yhi, ylo, S, out=banks[:, 4 + half, 0:S])\
                    .then_inc(product, 1)
        merge_loop(pe, l, one)

    def split_hi_merge(act, u, it):
        act.wait_ge(landed[u % 2], 16 * (u // 2 + 1) + 32 * it)
        act.wait_ge(product, 2 * (u - 1) + 8 * it)
        act.copy(whi[u % 2][:, 0:KC * 256], raw[u % 2][:, 0:KC * 256]).then_inc(hi_done, 1)

    def merge_act(act, l):
        def one(u, j, it):
            split_hi_merge(act, u + 1, it)
            if j == 3:
                for half in range(2):
                    act.wait_ge(merged_full, 16 * l + 2 * half + 2 + 4 * it)
                    ins = act.copy(mhi[:, 2 * it + half, :], gated[:, half, 0, :])
                    ins.then_inc(merged_hi, 1)
                return
            if j == 0:
                act.wait_ge(evicted, u + 4 * it)
            for half in range(2):
                act.wait_ge(product, 2 * u + half + 1 + 8 * it)
                at = VEC2["b_gates"][0] + 8 * j + half
                ins = act.activation(gate[:, 2 * j + half, :], banks[:, bank(u, half), 0:S], ACT.Sigmoid,
                                     bias=v2[:, l, bass.ds(at + 2 * it, 1)])
            ins.then_inc(evicted, 1)
        merge_loop(act, l, one)

    merged_hi = sem("merged_hi_done")
    merged_lo = sem("merged_lo_done")
    merged_full = sem("merged_full_done")
    gated_done = sem("branches_gated")

    def merge_dve(dve, l):
        def one(u, j, it):
            dve.wait_ge(hi_done, u + 2 + 4 * it)
            v = (u + 1) % 2
            dve.tensor_tensor(wlo[v][:, 0:KC * 256], raw[v][:, 0:KC * 256], whi[v][:, 0:KC * 256].bitcast(F32),
                              ALU.subtract).then_inc(lo_done, 1)
            if j < 3:
                return
            dve.wait_ge(evicted, u + 4 * it)
            for half in range(2):
                dve.wait_ge(product, 2 * u + half + 1 + 8 * it)
                for b in range(3):
                    src = banks[:, bank(u, half), b * S:(b + 1) * S] if b < 2 else banks[:, 4 + half, 0:S]
                    ins = dve.tensor_tensor(gated[:, half, b, :], gate[:, 2 * b + half, :], src, ALU.mult)
                    if b < 2 or half == 0:
                        ins.then_inc(gated_done, 1)
                    else:
                        ins.then_inc(evicted, 1)
            for half in range(2):
                dve.wait_ge(merged_hi, 8 * l + half + 1 + 2 * it)
                dve.tensor_tensor(mlo[:, 2 * it + half, :], gated[:, half, 0, :],
                                  mhi[:, 2 * it + half, :].bitcast(F32), ALU.subtract).then_inc(merged_lo, 1)
        merge_loop(dve, l, one)

    def merge_pool(pool, l):
        pool.wait_ge(*POOL_.here())
        u = phases[f"M{l}.merge"].u0 + 3
        with pool.Fori(0, 4) as it:
            for half in range(2):
                if half == 0:
                    pool.wait_ge(gated_done, 20 * l + 3 + 5 * it)
                else:
                    pool.wait_ge(evicted, u + 1 + 4 * it)
                pool.tensor_tensor(gated[:, half, 0, :], gated[:, half, 0, :], gated[:, half, 1, :], ALU.add)\
                    .then_inc(merged_full, 1)
                pool.wait_ge(merged_full, 16 * l + 2 * half + 1 + 4 * it)
                pool.tensor_tensor(gated[:, half, 0, :], gated[:, half, 0, :], gated[:, half, 2, :], ALU.add)\
                    .then_inc(merged_full, 1)

    block = ctx.enter_context(nc.Block())

    @block.sync
    def _(sp):
        sp.dma_start(crow[:], A["crow"]).then_inc(crow_loaded, 16)
        sp.dma_start(v1[:], A["vec1"]).then_inc(inputs_loaded, 16)
        sp.dma_start(k1[:], A["const1"]).then_inc(inputs_loaded, 16)
        sp.dma_start(sinks[:], A["wa_sinks"]).then_inc(inputs_loaded, 16)
        sp.dma_start(h[:], A["x"]).then_inc(inputs_loaded, 16)
        for name, ph in phases.items():
            if name in ("M0.z", "M1.z"):
                out, l = phases[name.replace("z", "ffn0.out0")], int(name[1])
                sweep_loads(sp, ph)
                sp.wait_ge(evicted, out.u0 + out.n)
                sp.dma_start(w_q[:], A["mla_wq_up"][l]).then_inc(mla_loaded, 16)
                sp.dma_start(w_kv[:], A["mla_wkv_up"][l]).then_inc(mla_loaded, 16)
                continue
            sweep_loads(sp, ph)
        sp.wait_ge(evicted, n_units)
        sp.dma_start(A["out"], h[:, :, 0:S]).then_inc(stored, 16)
        sp.wait_ge(stored, 16)

    @block.tensor
    def _(pe):
        block1_ffn("pe", pe, "L0.ffn0", 0, T2)
        qkv_pe(pe, "L0", 1, T2)
        qkv_done(pe, "L0")
        attention_pe(pe, "L0", na_tiles())
        out_pe(pe, "L0.wo", T2, uhi, ulo, lambda k: DVE_.at("L0", "out", k))
        means_pe(pe, 2, T2, last_evicted(phases["L0.wo"]))
        block1_ffn("pe", pe, "L0.ffn1", 2, T2)
        block1_ffn("pe", pe, "L1.ffn0", 3, T2)
        qkv_pe(pe, "L1", 4, S)
        qkv_done(pe, "L1")
        wa_rope_pe(pe)
        attention_pe(pe, "L1", wa_tiles())
        out_pe(pe, "L1.wo", S, uhi, ulo, lambda k: DVE_.at("L1", "out", k))
        means_pe(pe, 5, S, last_evicted(phases["L1.wo"]))
        block1_ffn("pe", pe, "L1.ffn1", 5, S)
        for l in range(2):
            s = 7 + 3 * l
            means_pe(pe, s, S, None)
            ffn_in_pe(pe, f"M{l}.ffn0.in0", s, S, u2hi, u2lo)
            ffn_out_pe(pe, f"M{l}.ffn0.out0", S, NARROW)
            means_pe(pe, s + 1, S, None)
            z_pe(pe, l, s + 1)
            sb_pe(pe, l)
            ml_pe(pe, l)
            mla_pe(pe, l)
            merge_pe(pe, l)
            out_pe(pe, f"M{l}.wo", S, mhi, mlo, lambda k: (merged_lo, 8 * l + k + 1))
            means_pe(pe, s + 2, S, None)
            ffn_in_pe(pe, f"M{l}.ffn1.in0", s + 2, S, u2hi, u2lo)
            ffn_out_pe(pe, f"M{l}.ffn1.out0", S, NARROW)

    @block.scalar
    def _(act):
        start_act(act)
        act.wait_ge(*DVE_.at("shift", 1))
        layer_input_act(act, 0, T2, None, scale1(0), shift1(0), uhi)
        block1_ffn("act", act, "L0.ffn0", 0, T2)
        norm1_act(act, 1, T2)
        qkv_act(act, "L0", T2)
        attention_act(act, "L0", na_tiles(), uhi)
        out_act(act, "L0.wo", 2, T2)
        norm1_act(act, 2, T2)
        block1_ffn("act", act, "L0.ffn1", 2, T2)
        norm1_act(act, 3, T2)
        block1_ffn("act", act, "L1.ffn0", 3, T2)
        norm1_act(act, 4, T2)
        qkv_act(act, "L1", S)
        attention_act(act, "L1", wa_tiles(), uhi)
        out_act(act, "L1.wo", 5, S)
        norm1_act(act, 5, S)
        block1_ffn("act", act, "L1.ffn1", 5, S)
        norm1_act(act, 6, S)
        act.wait_ge(*ACT_.at("h", 6, KC - 1))
        for dst, src in ((k2, "const2"), (v2, "vec2"), (rows2, "rows2"), (positions, "positions")):
            act.dma_start(dst[:], A[src]).then_inc(block2_loaded, 16)
        squares_act(act, 7, S, lambda cc: ACT_.at("h", 6, cc), range(KC))
        for l in range(2):
            s = 7 + 3 * l
            if l == 0:
                act.wait_ge(block2_loaded, 16 * N_BLOCK2)
            norm2_act(act, s, l, "ffn1_norm", u2hi)
            ffn_in_act(act, f"M{l}.ffn0.in0", S, NARROW)
            out_act(act, f"M{l}.ffn0.out0", s + 1, S)
            norm2_act(act, s + 1, l, "mix_norm", u2hi)
            if l == 0:
                rope_tables_act(act)
            z_act(act, l)
            sb_act(act, l)
            ml_act(act, l)
            mla_act(act, l)
            merge_act(act, l)
            out_act(act, f"M{l}.wo", s + 2, S)
            norm2_act(act, s + 2, l, "ffn2_norm", u2hi)
            ffn_in_act(act, f"M{l}.ffn1.in0", S, NARROW)
            out_act(act, f"M{l}.ffn1.out0", *((s + 3, S) if l == 0 else ()))

    @block.vector
    def _(dve):
        mod_start_dve(dve)
        split_lo(dve, 0)
        split_lo(dve, 1, early=True)
        for cc in range(KC):
            low_dve(dve, 0, T2, cc, uhi, ulo)
        block1_ffn("dve", dve, "L0.ffn0", 0, T2)
        norm1_dve(dve, 1, T2)
        qkv_dve(dve, "L0")
        attention_dve(dve, "L0", na_tiles(), uhi, ulo)
        out_dve(dve, "L0.wo", T2, gate1(1), lambda cc: POOL_.at("h", 1, cc))
        norm1_dve(dve, 2, T2)
        block1_ffn("dve", dve, "L0.ffn1", 2, T2)
        norm1_dve(dve, 3, T2)
        block1_ffn("dve", dve, "L1.ffn0", 3, T2)
        norm1_dve(dve, 4, T2)
        qkv_dve(dve, "L1")
        wa_rope_dve(dve)
        attention_dve(dve, "L1", wa_tiles(), uhi, ulo)
        out_dve(dve, "L1.wo", S, gate1(4), lambda cc: POOL_.at("h", 4, cc))
        norm1_dve(dve, 5, S)
        block1_ffn("dve", dve, "L1.ffn1", 5, S)
        norm1_dve(dve, 6, S)
        for l in range(2):
            s = 7 + 3 * l
            norm2_dve(dve, s, u2hi, u2lo)
            half_gate = lambda cc, kind: 0.5
            ffn_in_dve(dve, f"M{l}.ffn0.in0", S, NARROW)
            out_dve(dve, f"M{l}.ffn0.out0", S, half_gate, None)
            norm2_dve(dve, s + 1, u2hi, u2lo)
            if l == 0:
                rope_tables_dve(dve)
            z_dve(dve, l)
            sb_dve(dve, l)
            ml_dve(dve, l)
            mla_dve(dve, l)
            merge_dve(dve, l)
            out_dve(dve, f"M{l}.wo", S, lambda cc, kind: 1.0, None)
            norm2_dve(dve, s + 2, u2hi, u2lo)
            ffn_in_dve(dve, f"M{l}.ffn1.in0", S, NARROW)
            out_dve(dve, f"M{l}.ffn1.out0", S, half_gate, None)

    @block.gpsimd
    def _(pool):
        for n in range(START_CHUNKS):
            start_load(pool, n)
        full1_pool(pool, 0, T2)
        block1_ffn("pool", pool, "L0.ffn0", 0, T2)
        full1_pool(pool, 1, T2)
        for what in "qkv":
            mod_loads(pool, f"L0.{what}")
        bias_pool(pool)
        sums_pool(pool, 2, T2, last_evicted(phases["L0.wo"]), True)
        full1_pool(pool, 2, T2)
        block1_ffn("pool", pool, "L0.ffn1", 2, T2)
        full1_pool(pool, 3, T2)
        block1_ffn("pool", pool, "L1.ffn0", 3, T2)
        pool.wait_ge(mod_done, 2 * MOD_CHUNKS)
        pool.dma_start(window_tables, A["const_wa"]).then_inc(window_loaded, 16)
        full1_pool(pool, 4, T2, S)
        sums_pool(pool, 5, S, last_evicted(phases["L1.wo"]), True)
        full1_pool(pool, 5, S)
        block1_ffn("pool", pool, "L1.ffn1", 5, S)
        for l in range(2):
            s = 7 + 3 * l
            if l == 0:
                sums_pool(pool, s, S, None, False)
            full2_pool(pool, s, l, "ffn1_norm")
            sums_pool(pool, s + 1, S, None, False)
            full2_pool(pool, s + 1, l, "mix_norm")
            mix_pool(pool, l)
            merge_pool(pool, l)
            sums_pool(pool, s + 2, S, None, False)
            full2_pool(pool, s + 2, l, "ffn2_norm")
            if l == 0:
                sums_pool(pool, s + 3, S, None, False)

    ctx.close()


def units(w, chunks=None):
    w = np.asarray(w)
    K, N = w.shape[-2:]
    w = w.reshape(-1, K // P, P, N // 256, 256)
    return np.ascontiguousarray(w.transpose(0, 3, 2, 1, 4)).reshape(-1, P, K // P * 256)


def by_partition(v):
    v = np.asarray(v)
    return v.reshape(-1, P).T


def lay_out(a):
    n = {k: np.asarray(v) for k, v in a.items()}
    c1, cw, c2 = const_arrays()
    out = {"const1": c1, "const_wa": cw, "const2": c2}
    tokens = np.concatenate([n["x"][0], n["ctx"][0]], 0)
    out["x"] = tokens.reshape(T2, KC, P).transpose(2, 1, 0)
    out["crow"] = np.broadcast_to(np.stack([n["c"][0], n["c_ctx"]]), (P, 2, D))
    out["vec1"] = np.concatenate([by_partition(n[k]) for k in ("b_mod", "ln_g", "ln_b")], 1)
    out["wa_sinks"] = np.broadcast_to(n["wa_sinks"], (P, NH))
    out["w_mod"] = n["w_mod"].transpose(0, 2, 1).reshape(MOD_CHUNKS, P, D)

    def ffn_in(w, hidden):
        w = w.reshape(-1, D, 2, hidden // P, P).transpose(0, 1, 3, 2, 4).reshape(-1, D, 2 * hidden)
        return units(w)

    def ffn_out(w):
        return units(w.reshape(-1, HALF, D))

    out["ffn_in"], out["ffn_out"] = ffn_in(n["ffn_w_in"], FF), ffn_out(n["ffn_w_out"])
    for j in (1, 2):
        out[f"ffn{j}_in"] = ffn_in(n[f"ffn{j}_wi_2"], FF2)
        out[f"ffn{j}_out"] = ffn_out(n[f"ffn{j}_wo_2"])
    out["na_qkv"], out["na_o"] = units(n["na_w_qkv"]), units(n["na_w_o"])
    heads = [8 * (c // 4) + c % 4 + 4 * side for c in range(KC) for side in range(2)]
    wq = n["wa_w_qkv"][0]
    q = np.concatenate([wq[:, hd * HD:(hd + 1) * HD] for hd in heads], 1)
    out["wa_qkv"] = units(np.concatenate([q, wq[:, D:]], 1))
    out["wa_o"] = units(np.concatenate([n["wa_w_o"][0][hd * HD:(hd + 1) * HD] for hd in heads], 0))
    rpb = np.pad(n["na_rpb"][0], ((0, 0), (0, 0), (GRID_W - NA_KW, GRID_W - NA_KW)))
    rows = []
    for tile in range(2):
        for q_row in (2 * tile, 2 * tile + 1):
            keys = rpb[:, NA_KH - 1 - q_row:NA_KH - 1 - q_row + ROWS]
            rows.append(np.stack([keys[:, :, GRID_W - 1 - qc:2 * GRID_W - 1 - qc] for qc in range(GRID_W)], 1))
    tiles = [np.concatenate(rows[2 * t:2 * t + 2], 1).reshape(NH, P, 1, S) for t in range(2)]
    out["na_rpb"] = np.concatenate(tiles, 2).reshape(NH, P, 2 * S)

    w, b = n["w_in_2"], n["b_in_2"]
    GATES = 3240

    def pack(x):
        i_f, ckv, k_rot = x[..., 2816:2824], x[..., 3080:3208], x[..., 3208:3240]
        last = [ckv, i_f, ckv[..., 0:56], k_rot, ckv[..., 0:32]]
        return np.concatenate([x[..., 0:2816], x[..., 2824:3080], *last], -1)

    out["w_in"] = units(pack(w))
    merge = []
    gates = w[..., GATES:].reshape(2, D, 3, 4, 256)
    ups = np.concatenate([n["w_up_sb_2"], n["w_up_ml_2"], n["w_up_mla_2"]], 1).reshape(2, D, 4, 256)
    for l in range(2):
        for j in range(4):
            merge += [gates[l, :, br, j] for br in range(3)] + [ups[l, :, j]]
    out["w_merge"] = units(np.stack(merge))
    out["w_out"] = units(n["w_out_2"])
    packed = pack(b)
    conv_w = n["ml_conv_w_2"]
    vec = []
    for l in range(2):
        pad = np.zeros(P, np.float32)
        q_gain, k_gain = (np.concatenate([n[k][l], pad[QK:]]) for k in ("mla_q_gain_2", "mla_k_gain_2"))
        parts = [n["ffn1_norm_2"][l], n["mix_norm_2"][l], n["ffn2_norm_2"][l], packed[l, 0:256], packed[l, 256:512],
                 packed[l, 768:1792], packed[l, 2304:2816], packed[l, 2816:3072], packed[l, 3072:3200],
                 packed[l, 3200:3328], b[l, GATES:], conv_w[l].reshape(-1), n["ml_conv_b_2"][l],
                 n["ml_out_norm_2"][l], n["mla_q_norm_2"][l], n["mla_kv_norm_2"][l], q_gain, k_gain]
        vec.append(np.concatenate([by_partition(x) for x in parts], 1))
    out["vec2"] = np.stack(vec, 1)
    row = np.concatenate([b[:, 512:768], b[:, 1792:2304], b[:, 2816:2824]], 1)
    out["rows2"] = np.broadcast_to(row, (P, 2, N_ROW2))
    out["positions"] = np.broadcast_to(n["positions_2"], (QK, S))
    out["mla_wq_up"] = n["mla_wq_up_2"].reshape(2, 2, P, 384).transpose(0, 2, 1, 3)
    out["mla_wkv_up"] = n["mla_wkv_up_2"]
    return {k: np.ascontiguousarray(v) for k, v in out.items()}


def kernel(**inputs):
    import concourse.bacc as bacc
    from concourse.bass_utils import run_bass_kernel_spmd

    laid = lay_out(inputs)
    book = {}
    for _ in range(2):
        nc = bacc.Bacc("TRN2", target_bir_lowering=False, num_devices=1)
        A, arrays = {}, {}
        for name, a in laid.items():
            arrays[f"in_{name}"] = a
            A[name] = nc.dram_tensor(f"in_{name}", a.shape, mybir.dt.from_np(a.dtype), kind="ExternalInput").ap()
        A["out"] = nc.dram_tensor("out", (P, KC, S), F32, kind="ExternalOutput").ap()
        book.pop("missing", None)
        build(nc, A, book)
    assert not book.get("missing"), book["missing"]
    result = run_bass_kernel_spmd(nc, [arrays], core_ids=[0]).results[0]["out"]
    return np.asarray(result).transpose(2, 1, 0).reshape(1, S, D)
```
